# Optimizing a Trainium2 kernel written in Bass

```python
import math
import jax
import jax.numpy as jnp
from jax import lax
import numpy as np

D_MODEL = 1024
BATCH = 1
SEQ = 1024
DEPTH = 1

CHUNK = 64
BLOCK_Q = 128
N_BRANCH = 4
HEAD_DIM = 64
BRANCH_HEADS = 4
BRANCH_WIDTH = BRANCH_HEADS * HEAD_DIM

LRU_WIDTH = BRANCH_WIDTH
LRU_BLOCKS = BRANCH_HEADS
LRU_BLOCK = LRU_WIDTH // LRU_BLOCKS
LRU_C = 8.0
CONV_W = 4
SB_HEADS = BRANCH_HEADS
SB_WIDTH = BRANCH_WIDTH
GDN_HEADS = BRANCH_HEADS
GDN_WIDTH = BRANCH_WIDTH
RW_HEADS = BRANCH_HEADS
RW_WIDTH = BRANCH_WIDTH
W_LORA = 32
A_LORA = 32
G_LORA = 64
RW_LN_EPS = 64e-5
FFN_DIM = 2816
FFN_CONV_W = 3
EPS = 1e-6

LRU_IN = (LRU_WIDTH, LRU_WIDTH)
SB_IN = (SB_WIDTH, SB_WIDTH, SB_WIDTH)
GDN_IN = (GDN_WIDTH, GDN_WIDTH, GDN_WIDTH, GDN_WIDTH, GDN_HEADS, GDN_HEADS)
RW_IN = (RW_WIDTH, RW_WIDTH, RW_WIDTH, W_LORA, A_LORA, G_LORA)
MIXER_IN = (sum(LRU_IN), sum(SB_IN), sum(GDN_IN), sum(RW_IN))
IN_DIM = sum(MIXER_IN)

kernel_name = "hybrid_gated_parallel_mixer_trunk"

def _split(t, widths):
    cuts = [int(v) for v in np.cumsum(widths)[:-1]]
    return jnp.split(t, cuts, axis=-1)

def rms_norm(x, g):
    xf = x.astype(jnp.float32)
    y = xf * lax.rsqrt(jnp.mean(xf * xf, axis=-1, keepdims=True) + EPS)
    return (y * g.astype(jnp.float32)).astype(x.dtype)

def l2_normalize(t):
    return t * lax.rsqrt(jnp.sum(t * t, axis=-1, keepdims=True) + EPS)

def causal_depthwise_conv(x, w):
    width, seq = w.shape[0], x.shape[1]
    xp = jnp.pad(x, ((0, 0), (width - 1, 0), (0, 0)))
    return sum(xp[:, j:j + seq] * w[j] for j in range(width))

def token_shift(x):
    return jnp.pad(x, ((0, 0), (1, 0), (0, 0)))[:, :-1]

def rg_lru_branch(p, conv_w, conv_b, w_r, b_r, w_i, b_i, lam):
    bsz, seq, _ = p.shape
    x_in, y_in = _split(p, LRU_IN)
    u = (causal_depthwise_conv(x_in, conv_w) + conv_b).astype(jnp.float32)
    ub = u.reshape(bsz, seq, LRU_BLOCKS, LRU_BLOCK)
    r = jax.nn.sigmoid(jnp.einsum('bsne,nef->bsnf', ub, w_r.astype(jnp.float32)).reshape(bsz, seq, LRU_WIDTH) + b_r)
    i = jax.nn.sigmoid(jnp.einsum('bsne,nef->bsnf', ub, w_i.astype(jnp.float32)).reshape(bsz, seq, LRU_WIDTH) + b_i)
    log_a = -LRU_C * r * jax.nn.softplus(-lam.astype(jnp.float32))
    a = jnp.exp(log_a)
    b = jnp.sqrt(-jnp.expm1(2.0 * log_a)) * (i * u)

    def combine(e1, e2):
        return (e1[0] * e2[0], e2[0] * e1[1] + e2[1])

    _, h = lax.associative_scan(combine, (a, b), axis=1)
    return (h * jax.nn.gelu(y_in.astype(jnp.float32))).astype(p.dtype)

def stick_breaking_branch(p):
    bsz, seq, _ = p.shape
    q, k, v = [t.reshape(bsz, seq, SB_HEADS, HEAD_DIM).astype(jnp.float32) for t in _split(p, SB_IN)]
    scale = HEAD_DIM ** -0.5
    blocks = []
    for blk in range(seq // BLOCK_Q):
        start, end = blk * BLOCK_Q, (blk + 1) * BLOCK_Q
        z = jnp.einsum('bqhd,bshd->bhqs', q[:, start:end], k[:, :end]) * scale
        t_pos = start + jnp.arange(BLOCK_Q)
        s_pos = jnp.arange(end)
        past = s_pos[None, :] < t_pos[:, None]
        neg_log_keep = jnp.where(past, jax.nn.softplus(z), 0.0)
        between = lax.cumsum(neg_log_keep, axis=3, reverse=True) - neg_log_keep
        weight = jnp.where(past, jnp.exp(jax.nn.log_sigmoid(z) - between), 0.0)
        blocks.append(jnp.einsum('bhqs,bshd->bqhd', weight, v[:, :end]))
    return jnp.concatenate(blocks, axis=1).reshape(bsz, seq, SB_WIDTH).astype(p.dtype)

def chunked_gated_delta_rule(q, k, v, g, beta):
    bsz, seq, nh, dk = q.shape
    dv = v.shape[-1]
    nc = seq // CHUNK

    def chunks(t):
        return t.reshape(bsz, nc, CHUNK, nh, t.shape[-1]).transpose(0, 3, 1, 2, 4)

    q, k, v = chunks(q), chunks(k), chunks(v)
    g = g.reshape(bsz, nc, CHUNK, nh).transpose(0, 3, 1, 2)
    beta = beta.reshape(bsz, nc, CHUNK, nh).transpose(0, 3, 1, 2)
    G = jnp.cumsum(g, axis=-1)
    pos = jnp.arange(CHUNK)
    incl = pos[:, None] >= pos[None, :]
    strict = pos[:, None] > pos[None, :]
    decay = jnp.exp(jnp.where(incl, G[..., :, None] - G[..., None, :], -jnp.inf))
    k_beta = k * beta[..., None]
    lower = jnp.where(strict, jnp.einsum('bhnid,bhnjd->bhnij', k_beta, k) * decay, 0.0)
    rhs = jnp.concatenate([v * beta[..., None], k_beta * jnp.exp(G)[..., None]], axis=-1)
    sol = lax.linalg.triangular_solve(lower + jnp.eye(CHUNK, dtype=lower.dtype), rhs,
                                      left_side=True, lower=True, unit_diagonal=True)
    u_intra, w_state = sol[..., :dv], sol[..., dv:]
    qk = jnp.einsum('bhnid,bhnjd->bhnij', q, k) * decay
    q_dec = q * jnp.exp(G)[..., None]
    G_last = G[..., -1:]
    k_dec = k * jnp.exp(G_last - G)[..., None]
    chunk_decay = jnp.exp(G_last[..., 0])

    def step(state, inp):
        u_i, w_i, qk_i, qd_i, kd_i, cd_i = inp
        u = u_i - jnp.einsum('bhik,bhkv->bhiv', w_i, state)
        o = jnp.einsum('bhik,bhkv->bhiv', qd_i, state) + jnp.einsum('bhij,bhjv->bhiv', qk_i, u)
        state = state * cd_i[..., None, None] + jnp.einsum('bhjk,bhjv->bhkv', kd_i, u)
        return state, o

    xs = tuple(jnp.moveaxis(t, 2, 0) for t in (u_intra, w_state, qk, q_dec, k_dec, chunk_decay))
    _, o = lax.scan(step, jnp.zeros((bsz, nh, dk, dv), q.dtype), xs)
    return o.transpose(1, 0, 3, 2, 4).reshape(bsz, seq, nh, dv)

def gated_deltanet_branch(p, conv_w, a_log, dt_bias, norm_g):
    bsz, seq, _ = p.shape
    q, k, v, z, a_in, b_in = _split(p, GDN_IN)
    qkv = jax.nn.silu(causal_depthwise_conv(jnp.concatenate([q, k, v], axis=-1), conv_w)).astype(jnp.float32)

    def heads(t):
        return t.reshape(bsz, seq, GDN_HEADS, HEAD_DIM)

    q, k, v = [heads(t) for t in jnp.split(qkv, 3, axis=-1)]
    q = l2_normalize(q) * (HEAD_DIM ** -0.5)
    k = l2_normalize(k)
    beta = jax.nn.sigmoid(b_in.astype(jnp.float32))
    g = -jnp.exp(a_log.astype(jnp.float32)) * jax.nn.softplus(a_in.astype(jnp.float32) + dt_bias.astype(jnp.float32))
    o = chunked_gated_delta_rule(q, k, v, g, beta)
    o = o * lax.rsqrt(jnp.mean(o * o, axis=-1, keepdims=True) + EPS) * norm_g.astype(jnp.float32)
    o = o * jax.nn.silu(heads(z.astype(jnp.float32)))
    return o.reshape(bsz, seq, GDN_WIDTH).astype(p.dtype)

def rwkv7_scan(r, w, k, v, kk, a):
    bsz, _, nh, hd = r.shape

    def step(state, inp):
        r_t, w_t, k_t, v_t, kk_t, a_t = inp
        sa = jnp.einsum('bhvk,bhk->bhv', state, -kk_t)
        state = (state * w_t[:, :, None, :] + sa[..., None] * (kk_t * a_t)[:, :, None, :]
                 + v_t[..., None] * k_t[:, :, None, :])
        return state, jnp.einsum('bhvk,bhk->bhv', state, r_t)

    xs = tuple(jnp.moveaxis(t, 1, 0) for t in (r, w, k, v, kk, a))
    _, y = lax.scan(step, jnp.zeros((bsz, nh, hd, hd), r.dtype), xs)
    return jnp.moveaxis(y, 0, 1)

def rwkv7_branch(p, mu, w0, w_up, a0, a_up, g_up, k_k, k_a, r_k, ln_g, ln_b):
    bsz, seq, _ = p.shape
    pf = p.astype(jnp.float32)
    pf = pf + (token_shift(pf) - pf) * mu
    r, k, v, xw, xa, xg = _split(pf, RW_IN)
    w_log = -jax.nn.softplus(-(w0 + jnp.tanh(xw) @ w_up)) - 0.5
    decay = jnp.exp(-jnp.exp(w_log))
    a = jax.nn.sigmoid(a0 + xa @ a_up)
    gate = jax.nn.sigmoid(xg) @ g_up

    def heads(t):
        return t.reshape(bsz, seq, RW_HEADS, HEAD_DIM)

    kk = l2_normalize(heads(k * k_k))
    k = k * (1.0 + (a - 1.0) * k_a)
    r_h, k_h, v_h = heads(r), heads(k), heads(v)
    y = rwkv7_scan(r_h, heads(decay), k_h, v_h, kk, heads(a))
    mean = jnp.mean(y, axis=-1, keepdims=True)
    var = jnp.mean(jnp.square(y - mean), axis=-1, keepdims=True)
    y = ((y - mean) * lax.rsqrt(var + RW_LN_EPS)).reshape(bsz, seq, RW_WIDTH) * ln_g + ln_b
    bonus = jnp.sum(r_h * k_h * r_k, axis=-1, keepdims=True) * v_h
    return ((y + bonus.reshape(bsz, seq, RW_WIDTH)) * gate).astype(p.dtype)

def conv_ffn(h, w_gate, w_up, conv_w, w_down):
    a = causal_depthwise_conv(h @ w_gate, conv_w)
    return (jax.nn.gelu(a) * (h @ w_up)) @ w_down

def setup_inputs(seed: int = 0) -> dict:
    key = jax.random.key(seed)
    keys = iter(jax.random.split(key, 64))
    f32 = jnp.float32
    L, D = DEPTH, D_MODEL

    def nrm(shape, scale):
        return jax.random.normal(next(keys), shape, f32) * scale

    def uni(shape, lo, hi):
        return jax.random.uniform(next(keys), shape, f32, lo, hi)

    x = nrm((BATCH, SEQ, D), 1.0)
    c = nrm((BATCH, D), 1.0)
    s = uni((L, LRU_WIDTH), 0.9, 0.999) ** (1.0 / LRU_C)
    lru_lambda = jnp.log(s) - jnp.log1p(-s)
    dt = jnp.exp(uni((L, GDN_HEADS), math.log(1e-3), math.log(1e-1)))
    gdn_dt_bias = dt + jnp.log(-jnp.expm1(-dt))
    return {
        'x': x,
        'c': c,
        'norm1_g': 1.0 + nrm((L, D), 0.02),
        'norm2_g': 1.0 + nrm((L, D), 0.02),
        'final_g': 1.0 + nrm((D,), 0.02),
        'w_ada': nrm((L, D, 6 * D), D ** -0.5),
        'b_ada': nrm((L, 6 * D), 0.02),
        'w_in': nrm((L, D, IN_DIM), D ** -0.5),
        'lru_conv_w': nrm((L, CONV_W, LRU_WIDTH), CONV_W ** -0.5),
        'lru_conv_b': nrm((L, LRU_WIDTH), 0.02),
        'lru_w_r': nrm((L, LRU_BLOCKS, LRU_BLOCK, LRU_BLOCK), LRU_BLOCK ** -0.5),
        'lru_b_r': nrm((L, LRU_WIDTH), 0.02),
        'lru_w_i': nrm((L, LRU_BLOCKS, LRU_BLOCK, LRU_BLOCK), LRU_BLOCK ** -0.5),
        'lru_b_i': nrm((L, LRU_WIDTH), 0.02),
        'lru_lambda': lru_lambda,
        'gdn_conv_w': nrm((L, CONV_W, 3 * GDN_WIDTH), CONV_W ** -0.5),
        'gdn_a_log': jnp.log(uni((L, GDN_HEADS), 1.0, 16.0)),
        'gdn_dt_bias': gdn_dt_bias,
        'gdn_norm_g': 1.0 + nrm((L, HEAD_DIM), 0.02),
        'rw_mu': uni((L, sum(RW_IN)), 0.0, 1.0),
        'rw_w0': uni((L, RW_WIDTH), -6.0, -1.0),
        'rw_w_up': nrm((L, W_LORA, RW_WIDTH), W_LORA ** -0.5),
        'rw_a0': nrm((L, RW_WIDTH), 0.1),
        'rw_a_up': nrm((L, A_LORA, RW_WIDTH), A_LORA ** -0.5),
        'rw_g_up': nrm((L, G_LORA, RW_WIDTH), G_LORA ** -0.5),
        'rw_k_k': 0.85 + nrm((L, RW_WIDTH), 0.05),
        'rw_k_a': 1.0 + nrm((L, RW_WIDTH), 0.05),
        'rw_r_k': nrm((L, RW_HEADS, HEAD_DIM), 0.1),
        'rw_ln_g': 1.0 + nrm((L, RW_WIDTH), 0.02),
        'rw_ln_b': nrm((L, RW_WIDTH), 0.02),
        'w_branch': nrm((L, N_BRANCH, BRANCH_WIDTH, D), BRANCH_WIDTH ** -0.5),
        'w_gate': nrm((L, N_BRANCH, D, D), D ** -0.5),
        'b_gate': nrm((L, N_BRANCH, D), 0.02),
        'w_out': nrm((L, D, D), D ** -0.5),
        'ffn_w_gate': nrm((L, D, FFN_DIM), D ** -0.5),
        'ffn_w_up': nrm((L, D, FFN_DIM), D ** -0.5),
        'ffn_conv_w': nrm((L, FFN_CONV_W, FFN_DIM), FFN_CONV_W ** -0.5),
        'ffn_w_down': nrm((L, FFN_DIM, D), FFN_DIM ** -0.5),
    }

def reference(x, c, norm1_g, norm2_g, final_g, w_ada, b_ada, w_in,
              lru_conv_w, lru_conv_b, lru_w_r, lru_b_r, lru_w_i, lru_b_i, lru_lambda,
              gdn_conv_w, gdn_a_log, gdn_dt_bias, gdn_norm_g,
              rw_mu, rw_w0, rw_w_up, rw_a0, rw_a_up, rw_g_up, rw_k_k, rw_k_a, rw_r_k, rw_ln_g, rw_ln_b,
              w_branch, w_gate, b_gate, w_out,
              ffn_w_gate, ffn_w_up, ffn_conv_w, ffn_w_down):
    cond = jax.nn.silu(c)
    for l in range(DEPTH):
        mod = cond @ w_ada[l] + b_ada[l]
        shift1, scale1, gate1, shift2, scale2, gate2 = [m[:, None, :] for m in jnp.split(mod, 6, axis=-1)]
        h = rms_norm(x, norm1_g[l]) * (1.0 + scale1) + shift1
        p_lru, p_sb, p_gdn, p_rw = _split(h @ w_in[l], MIXER_IN)
        branches = (
            rg_lru_branch(p_lru, lru_conv_w[l], lru_conv_b[l], lru_w_r[l], lru_b_r[l],
                          lru_w_i[l], lru_b_i[l], lru_lambda[l]),
            stick_breaking_branch(p_sb),
            gated_deltanet_branch(p_gdn, gdn_conv_w[l], gdn_a_log[l], gdn_dt_bias[l], gdn_norm_g[l]),
            rwkv7_branch(p_rw, rw_mu[l], rw_w0[l], rw_w_up[l], rw_a0[l], rw_a_up[l], rw_g_up[l],
                         rw_k_k[l], rw_k_a[l], rw_r_k[l], rw_ln_g[l], rw_ln_b[l]),
        )
        mixed = sum(jax.nn.sigmoid(h @ w_gate[l, n] + b_gate[l, n]) * (o @ w_branch[l, n])
                    for n, o in enumerate(branches))
        x = x + gate1 * (mixed @ w_out[l])
        h = rms_norm(x, norm2_g[l]) * (1.0 + scale2) + shift2
        x = x + gate2 * conv_ffn(h, ffn_w_gate[l], ffn_w_up[l], ffn_conv_w[l], ffn_w_down[l])
    return rms_norm(x, final_g)


_drawn_inputs = setup_inputs


def setup_inputs(seed=0):
    import zlib

    import numpy as np

    out = dict(_drawn_inputs(seed))
    spreads = {}
    factors = {'norm1_g': 3.291,
     'norm2_g': 24.432,
     'final_g': 23.019,
     'lru_b_r': 143.02,
     'lru_b_i': 96.067,
     'gdn_norm_g': 79.759,
     'rw_a0': 8.0,
     'rw_ln_g': 200.0,
     'rw_ln_b': 200.0,
     'b_gate': 8.0,
     'lru_conv_b': 15.262,
     'rw_k_k': 4.903}
    for name, (base, spread) in spreads.items():
        noise = np.random.default_rng([zlib.crc32(name.encode()), seed]).standard_normal(out[name].shape)
        drawn = base * np.exp(spread * noise) if base else spread * noise
        out[name] = jnp.asarray(drawn.astype(out[name].dtype))
    for name, factor in factors.items():
        out[name] = (out[name] * factor).astype(out[name].dtype)
    return out
```

```python
from contextlib import ExitStack

import numpy as np

import concourse.bass as bass
from concourse import mybir

F32 = mybir.dt.float32
F32R = mybir.dt.float32r
ALU = mybir.AluOpType
ACT = mybir.ActivationFunctionType

P = 128
D = 1024
S = 1024
KT = D // P
HALF = 512
NB = S // P
EPS = 1e-6
RW_LN_EPS = 64e-5
HEAD = 64
CHUNK = 64
W_COLS = 10 * P
FFN = 2816
FT = FFN // P
GT = 4
NG = FT // GT
UG = 2 * GT + 4
U_MIX1, U_MIX2, U_OUT, U_FFN = 26, 42, 58, 66
UNITS = U_FFN + 2 * FT + 4 * NG + 2
RW_T, GDN_T = 7, 8
P_TILES = RW_T + GDN_T
HALO = 3
BLK = P + HALO
SB_STEPS = [(b, hd) for b in reversed(range(NB)) for hd in range(4)]
JOBS_AHEAD = 8
LRU_JOBS = [range(0, 2), range(2, 5), range(5, JOBS_AHEAD)]
ND = 30
E_HALF = float(np.exp(-0.5))

_INV_Z = ["rw_Z", "rw_Z", "gd_Z", "gd_Z"]
EVENTS = {
    "products": (["rw_p1", "rw_p2", "rw_p3", "rw_p4", "rw_p6", "rw_p5", "rw_p7", "rw_p8", "rw_r1"]
                 + ["gd_g1", "gd_g2", "gd_g3", "gd_g4", "gd_g5", "gd_g6"]
                 + (["rw_Y", "gd_Y"] + _INV_Z) * 4 + ["rw_Y", "gd_Y", "rw_Z", "gd_Z", "rw_r3", "gd_r3"]
                 + ["rw_ws", "gd_ws", "rw_s", "rw_Yd", "gd_s", "gd_Yd"] * 2 + ["rw_m1", "gd_m", "rw_m2"]),
    "functions": (["rw_lt"] * 3 + ["rw_sq", "rw_sw", "rw_sw", "rw_sa", "rw_sa", "rw_gate", "rw_ln", "rw_rn"]
                  + ["rw_ex"] * 3 + ["rw_tokVA", "rw_tokBK", "gd_silu", "pblk_read", "gd_sq", "gd_gbc", "gd_gbc"]
                  + ["rw_x", "gd_ln", "gd_rn", "gd_dt", "gd_eg", "rw_uw", "gd_uw", "rw_y", "gd_y2", "gd_lno", "gd_rno"]
                  + ["rw_y2", "rw_lno", "rw_rno"]),
    "values": (["rw_pm", "rw_kkr", "rw_gs", "rw_gs", "rw_gm", "rw_bonp", "rw_ar", "rw_ar", "rw_km", "rw_tl", "rw_tl"]
               + ["rw_bon", "rw_akt", "rw_akt", "rw_ltr", "rw_ltr", "gd_acc", "tkc", "rw_T", "gd_kn", "gd_kbq"]
               + ["gd_dtm", "gd_kbq", "gd_tok", "gd_tok", "gd_tok", "gd_ltr", "gd_qkt", "gd_T"]
               + ["rw_Ym", "gd_Ym", "rw_T", "rw_T", "gd_T", "gd_T"] * 4 + ["rw_Ym", "gd_Ym", "rw_T", "gd_T"]
               + (["rw_u", "gd_u"] + ["rw_S"] * 4 + ["gd_S"] * 4) * 2 + ["rw_yc", "gd_o", "rw_o"]),
}

PAR = {}
_n = 0
for _name, _w in (("n1", 8), ("n2", 8), ("nf", 8), ("b_ada", 48), ("lru_cw", 8), ("lru_cb", 2), ("lru_br", 2),
                  ("lru_bi", 2), ("lru_lam", 2), ("gdn_cw", 24), ("rw_mu", 7), ("rw_w0", 2), ("rw_a0", 2),
                  ("rw_kk", 2), ("rw_ka", 2), ("rw_rk", 2), ("rw_lng", 2), ("rw_lnb", 2), ("b_gate", 32),
                  ("ffn_cw", 66), ("gdn_ng", 1), ("alog", 4), ("dtb", 4)):
    PAR[_name] = slice(_n, _n + _w)
    _n += _w
NPAR = _n

MASKS = ["ident", "tri", "strict", "nstrict", "neg", "suffix", "bd", "lv1", "lv1T", "lv2", "lv4", "lv8", "lv16",
         "lv32", "reset", "ones", "past", "npast"]
M = {n: i for i, n in enumerate(MASKS)}


def mask_table():
    r = np.arange(P)[:, None]
    c = np.arange(P)[None, :]
    same = (r // CHUNK) == (c // CHUNK)
    t = {"ident": r == c, "tri": same & (c >= r), "strict": same & (c > r), "suffix": same & (r > c),
         "bd": (r // HEAD) == (c // HEAD), "ones": (r >= 0) & (c >= 0),
         "past": c < r, "npast": c >= r, "reset": (r >= 0) & (c % CHUNK != 0)}
    for s in (1, 2, 4, 8, 16, 32):
        t[f"lv{s}"] = (r // (2 * s) == c // (2 * s)) & (r % (2 * s) >= s) & (c % (2 * s) < s)
    t["lv1T"] = t["lv1"].T
    out = {k: v.astype(np.float32) for k, v in t.items()}
    out["nstrict"] = -out["strict"]
    out["neg"] = np.where(t["tri"], 0.0, -1e30).astype(np.float32)
    return np.stack([out[n] for n in MASKS], axis=1).reshape(P, len(MASKS) * P)


def program(nc, a, out):
    ctx = ExitStack()
    with ctx:
        def sb(name, shape, dt=F32):
            return ctx.enter_context(nc.sbuf_tensor(name, shape, dt))

        sems = {}
        group_of = {label: group for group, labels in EVENTS.items() for label in labels}
        emitted = {group: [] for group in EVENTS}

        def sem(name):
            name = group_of.get(name, name)
            if name not in sems:
                sems[name] = ctx.enter_context(nc.semaphore(name))
            return sems[name]

        def done(label):
            assert label == EVENTS[group_of[label]][len(emitted[group_of[label]])], label
            emitted[group_of[label]].append(label)
            return sem(label)

        def at(label, i, nth=None):
            events = EVENTS[group_of[label]]
            if isinstance(nth, int) and nth == 0:
                return i * len(events)
            places = [n for n, e in enumerate(events) if e == label]
            return i * len(events) + (places[-1 if nth is None else nth - 1] + 1)

        w_raw = sb("w_raw", [P, 2, W_COLS])
        w_hi = sb("w_hi", [P, 2, W_COLS], F32R)
        w_lo = sb("w_lo", [P, 2, W_COLS], F32R)
        h_hi = sb("h_hi", [P, KT, S], F32R)
        h_lo = sb("h_lo", [P, KT, S], F32R)
        ra = sb("ra", [P, 8, S], F32R)
        fa = sb("fa", [P, 20, S])
        msk = sb("msk", [P, len(MASKS), P])
        par = sb("par", [P, NPAR])
        mod = sb("mod", [P, 48])
        mod6 = sb("mod6", [P, 6])
        a1 = sb("a1", [P, 16])
        sl = sb("sl", [P, 4])
        lora = sb("lora", [P, 6, P])
        state = sb("state", [P, 2, 2, P])
        tk = sb("tk", [P, 6, 32])
        abt = sb("abt", [P, 64])
        ea = sb("ea", [P, 4])
        tkc = sb("tkc", [P, 20])
        bgc = sb("bgc", [P, 2])
        cwc = sb("cwc", [P, 3 * GT])
        zero = sb("zero", [P, 48])
        eps = sb("eps", [P, 2])
        lru_w = fa[:, 16, 0:4 * P].rearrange("p (n c) -> p n c", c=P)
        sp_t = fa[:, 17, 0:256].rearrange("p (k c) -> p k c", c=32)
        gbank = ctx.enter_context(nc.psum_tensor("gbank", [P, 4, HALF], F32))
        mbank = ctx.enter_context(nc.psum_tensor("mbank", [P, 4, HALF], F32))
        gb = [gbank[:, i, :] for i in range(4)]
        mb = [mbank[:, i, :] for i in range(4)]

        p_scr = nc.dram_tensor("p_scr", (P_TILES, P, HALO + S), F32, kind="Internal").ap()

        def m_(name):
            return msk[:, M[name], :]

        def pc(name, j=0):
            b = PAR[name].start + j
            return par[:, b:b + 1]

        mix_scr = nc.dram_tensor("mix_scr", (KT, P, S), F32, kind="Internal").ap()
        o_scr = nc.dram_tensor("o_scr", (4, P, S), F32, kind="Internal").ap()

        flat = fa[:].rearrange("p t s -> p (t s)")
        used = [0]
        names = {}

        def room(name, cols, like=None):
            if like is None:
                names[name] = flat[:, used[0]:used[0] + cols]
                used[0] += cols
                assert used[0] <= 20 * S, used
            else:
                names[name] = like[:, 0:cols]
            return names[name]

        pblk = room("pblk", P_TILES * BLK).rearrange("p (t c) -> p t c", c=BLK)
        sig, mix = room("sig", HALF), room("mix", S)
        X = room("X", 3456)
        xo = [0]

        def xroom(cols):
            xo[0] += cols
            assert xo[0] <= 3456, xo
            return X[:, xo[0] - cols:xo[0]]

        rw = {}
        for n_, c_ in (("pm", 7 * P), ("sw", 256), ("gs", 256), ("gm", 256), ("ex0", 256), ("exn", 256), ("sa", 256),
                       ("kkr", 256), ("t1", 256), ("rn", 256), ("lt", P)):
            rw[n_] = xroom(c_)
        for n_, c_ in (("ex1", 256), ("gate", 256), ("ar", 512), ("bm", 256), ("km", 256), ("tokVA", 512),
                       ("tokBK", 512), ("ltr", 512), ("akt", 512), ("rbt", 512), ("rkt", 512), ("T", 512), ("TT", 512),
                       ("Y", 512), ("uw", 512), ("u", 256), ("x", 256), ("o", 256), ("bon", 256)):
            rw[n_] = room("rw_" + n_, c_)
        rw["bt"], rw["kt"] = rw["T"][:, 0:256], rw["T"][:, 256:512]
        rw["y"], rw["yc"], rw["y2"] = rw["x"], rw["uw"][:, 0:256], rw["uw"][:, 256:512]
        xo[0] = 0
        gd = {}
        for n_, c_ in (("acc", 768), ("tmp", 768), ("sq", 512), ("rn", 512), ("kbc", 0)):
            gd[n_] = xroom(c_)
        for n_, c_ in (("z", 256), ("kn", 256), ("kbq", 512), ("qd", 256), ("eg", 256), ("vb", 256), ("kbe", 256),
                       ("kd", 256), ("ltr", 512), ("qkt", 512), ("T", 512), ("TT", 512), ("Y", 512), ("uw", 512),
                       ("u", 256)):
            gd[n_] = room("gd_" + n_, c_)
        gd["gbc"], gd["dt"], gd["bb"] = gd["Y"], gd["T"], gd["uw"]
        gd["o"], gd["y2"], gd["rno"] = gd["vb"], gd["kbe"], gd["kd"]

        def t2(ap):
            return ap.rearrange("p (t c) -> p t c", c=P)

        def t4(ap):
            return ap.rearrange("p (t c) -> p t c", c=P)

        def over4(name):
            return msk[:, M[name]:M[name] + 1, :].to_broadcast([P, 4, P])

        def over_t(col, n, w=P):
            return par[:, col:col + n].rearrange("p (t o) -> p t o", o=1).to_broadcast([P, n, w])

        vtok = fa[:, 10:12, :].rearrange("p t s -> p (t s)")

        SQ, ACC, RSTD = 16, 18, 19
        sig4 = [fa[:, 12 + j // 2, (j % 2) * HALF:(j % 2 + 1) * HALF] for j in range(4)]
        G = [flat[:, 8 * S + s_ * (S + 2):8 * S + (s_ + 1) * (S + 2)] for s_ in range(2)]
        C = [fa[:, 11, :], fa[:, 15, :]]

        block = ctx.enter_context(nc.Block())

        @block.sync
        def _(sp):
            sp.dma_start(par[:], a["par"]).then_inc(sem("par_in"), 16)
            sp.dma_start(msk[:].rearrange("p m c -> p (m c)"), a["masks"]).then_inc(sem("msk_in"), 16)
            sp.wait_ge(sem("zero_set"), 6)
            for g in range(2):
                for r in range(2):
                    sp.dma_start(lru_w[64 * r:64 * r + 64, 2 * g:2 * g + 2, 64 * r:64 * r + 64],
                                 a["lru_w"][g, r::2].rearrange("n e f -> e n f")).then_inc(sem("lru_w_in"), 16)
            for t in range(2):
                cols = slice(t * P, (t + 1) * P)
                sp.dma_start(lora[0:32, t, :], a["lora"][0:32, cols]).then_inc(sem("lora_in"), 16)
                sp.dma_start(lora[32:64, 2 + t, :], a["lora"][32:64, cols]).then_inc(sem("lora_in"), 16)
                sp.dma_start(lora[64:128, 4 + t, :], a["lora"][64:128, cols]).then_inc(sem("lora_in"), 16)
            sp.dma_start(p_scr[:, :, 0:HALO].rearrange("t p c -> p t c"),
                         zero[:, 0:P_TILES * HALO].rearrange("p (t c) -> p t c", c=HALO)).then_inc(sem("halo"), 16)
            sp.dma_start(fa[:, 11, :], a["c"].to_broadcast([P, D])).then_inc(sem("c_in"), 16)
            for k in range(KT):
                sp.dma_start(fa[:, k, :], a["xT"][k]).then_inc(sem(f"x_in{k}"), 16)

            for t in range(18):
                if t >= 3:
                    sp.wait_ge(sem("ada_used"), t - 2)
                sp.dma_start(fa[:, 12 + t % 3, :], a["w_ada"][t]).then_inc(sem(f"ada_in{t % 3}"), 16)

            def unit(name, row, slot, u, cols=KT * P):
                if not (isinstance(u, int) and u < 2):
                    sp.wait_ge(sem("w_split"), u - 1)
                sp.dma_start(w_raw[:, slot, 0:cols], a[name][row]).then_inc(sem(f"w_in{slot}"), 16)

            unit("w_in", 0, 0, 0)
            unit("w_in", 1, 1, 1)
            with sp.Fori(0, 4) as i:
                for s in range(2):
                    unit("w_in", i * 2 + (2 + s), s, i * 2 + (2 + s))
                for t in range(6):
                    sp.wait_ge(sem("ada_used"), i * 6 + (t + 16))
                    sp.dma_start(fa[:, 12 + t % 3, :], a["w_ada"][i * 6 + (18 + t)]).then_inc(sem(f"ada_in{t % 3}"), 16)
            for t in range(42, 48):
                sp.wait_ge(sem("ada_used"), t - 2)
                sp.dma_start(fa[:, 12 + t % 3, :], a["w_ada"][t]).then_inc(sem(f"ada_in{t % 3}"), 16)
            for u in range(10, 26):
                unit("w_in", u, u % 2, u)
            if True:
                for n in range(2):
                    unit("w_mix", n, n, 26 + n, W_COLS)
                sp.wait_ge(sem("p_out0"), 16 * 16)
                sp.wait_ge(sem("p_out1"), 14 * 16)
                sp.wait_ge(sem("halo"), 16)
                sp.wait_ge(sem("sb_lo"), 8)
                sp.wait_ge(sem("ab_read"), 1)

                def block_in(i):
                    sp.wait_ge(sem("halo"), 16)
                    sp.dma_start(pblk, p_scr[:, :, bass.ds(i * P, BLK)].rearrange("t p c -> p t c")).then_inc(sem("pblk_in"), 16)

                def block_out(i):
                    sp.wait_ge(sem("gated"), i * 4 + 4)
                    sp.wait_ge(sem("rw_o"), at("rw_o", i))
                    sp.dma_start(mix_scr[bass.ds(i, 1)].rearrange("t p c -> p (t c)"), mix).then_inc(sem("mix_stored"), 16)
                    for nm, o_, t in (("rw", rw["o"], 2), ("gd", gd["o"], 0)):
                        sp.dma_start(o_scr[t:t + 2, :, bass.ds(i * P, P)].rearrange("t p c -> p t c"), t2(o_)).then_inc(sem(f"{nm}_stored"), 16)

                block_in(0)
                with sp.Fori(0, NB - 1) as i:
                    for n in range(2):
                        unit("w_mix", i * 2 + (2 + n), n, i * 2 + (28 + n), W_COLS)
                    sp.wait_ge(sem("pblk_read"), at("pblk_read", i))
                    block_in(i + 1)
                    block_out(i)
                block_out(NB - 1)
            for n in range(2):
                unit("w_mix", 16 + n, n, U_MIX2 + n, W_COLS)
            sp.wait_ge(sem("gated"), 4 * NB)
            for nm in ("rw", "gd", "mix"):
                sp.wait_ge(sem(f"{nm}_stored"), 16 * NB)
            sp.dma_start(fa[:, 8:12, :], o_scr.rearrange("t p c -> p t c")).then_inc(sem("o_in"), 16)
            sp.dma_start(fa[:, 0:8, :], mix_scr.rearrange("t p c -> p t c")).then_inc(sem("mix_in"), 16)
            with sp.Fori(0, KT - 1) as i:
                for n in range(2):
                    unit("w_mix", i * 2 + (18 + n), n, i * 2 + (U_MIX2 + 2 + n), W_COLS)
            for n in range(2):
                unit("w_tail", n, n, U_OUT + n)
            for k in range(KT):
                sp.wait_ge(sem("mixed_lo"), k + 1)
                sp.dma_start(fa[:, k, :], a["xT"][k]).then_inc(sem(f"x_in{k}"), 16)
            with sp.Fori(0, (UNITS - U_OUT) // 2 - 1) as i:
                for n in range(2):
                    unit("w_tail", i * 2 + (2 + n), n, i * 2 + (U_OUT + 2 + n))
            for k in range(KT):
                sp.wait_ge(sem("out_done"), k + 1)
                sp.dma_start(out[k], fa[:, k, :]).then_inc(sem("stored"), 16)
            sp.wait_ge(sem("stored"), 16 * KT)

        @block.gpsimd
        def _(pool):
            pool.memset(zero[:], 0.0).then_inc(sem("zero_set"), 1)
            pool.memset(eps[:, 0:1], EPS).then_inc(sem("zero_set"), 1)
            pool.memset(eps[:, 1:2], RW_LN_EPS).then_inc(sem("zero_set"), 1)
            pool.memset(lru_w, 0.0).then_inc(sem("zero_set"), 1)
            pool.memset(lora[:], 0.0).then_inc(sem("zero_set"), 1)
            pool.memset(state[:], 0.0).then_inc(sem("zero_set"), 1)
            pool.wait_ge(sem("zero_set"), 6)

            def split(u, slot, landed, cols=KT * P, used=None):
                raw, hi, lo = w_raw[:, slot, 0:cols], w_hi[:, slot, 0:cols], w_lo[:, slot, 0:cols]
                pool.wait_ge(sem(f"w_in{slot}"), landed)
                if used:
                    pool.wait_ge(*used)
                elif not (isinstance(u, int) and u < 2):
                    pool.wait_ge(sem("gb2_full"), u - 1)
                pool.tensor_tensor(hi, raw, zero[:, 0:1].to_broadcast([P, cols]), ALU.add).then_inc(sem("w_hi_set"), 1)
                pool.wait_ge(sem("w_hi_set"), u + 1)
                pool.tensor_tensor(lo, raw, hi.bitcast(F32), ALU.subtract).then_inc(sem("w_split"), 1)

            split(0, 0, 16)
            split(1, 1, 16)
            with pool.Fori(0, 4) as i:
                split(i * 2 + 2, 0, i * 16 + 32)
                split(i * 2 + 3, 1, i * 16 + 32)
            for u in range(10, 26):
                split(u, u % 2, 16 * (u // 2 + 1))
            with pool.Fori(0, NB) as i:
                for n in range(2):
                    split(i * 2 + (U_MIX1 + n), n, i * 16 + 16 * (U_MIX1 // 2 + 1), W_COLS)
            with pool.Fori(0, KT) as i:
                for n in range(2):
                    pool.wait_ge(sem("gb3_full"), i * 2 + (U_MIX2 - 27 + n))
                    split(i * 2 + (U_MIX2 + n), n, i * 16 + 16 * (U_MIX2 // 2 + 1), W_COLS)
            for n in range(2):
                pool.wait_ge(sem("gb3_full"), U_OUT - 27 + n)
                split(U_OUT + n, n, 16 * (U_OUT // 2 + 1))
            with pool.Fori(0, (UNITS - U_OUT) // 2 - 1) as i:
                for n in range(2):
                    split(i * 2 + (U_OUT + 2 + n), n, i * 16 + 16 * (U_OUT // 2 + 2),
                          used=(sem("half_done"), i * 4 + (2 + 2 * n)))

        @block.tensor
        def _(pe):
            pe.wait_ge(sem("msk_in"), 16)
            for k in range(KT):
                pe.wait_ge(sem("sq"), k + 1)
                for hf in range(2):
                    last = pe.matmul(mb[hf], m_("ones"), fa[:, 8 + 2 * (k % 2), hf * HALF:(hf + 1) * HALF],
                                     start=(k == 0), stop=(k == KT - 1))
                last.then_inc(sem("sq_used"), 1)

            def gemm(bank, slot, hf, rhs_hi, rhs_lo, ks, first=0, last=None, off=0):
                last = 3 * ks if last is None else last
                for q in range(first, last):
                    k, which = divmod(q, 3)
                    w = (w_lo if which == 2 else w_hi)[:, slot, off + k * P:off + (k + 1) * P]
                    r = (rhs_lo if which == 1 else rhs_hi)[:, k, hf * HALF:(hf + 1) * HALF]
                    mm = pe.matmul(gb[bank], w, r, start=(q == 0), stop=(q == 3 * ks - 1))
                return mm

            pe.wait_ge(sem("h_done"), KT)
            with pe.Fori(0, 5) as i:
                for s in range(2):
                    pe.wait_ge(sem("w_split"), i * 2 + (s + 1))
                    for hf in range(2):
                        pe.wait_ge(sem(f"gb{2 * hf}_read"), i * 2 + s)
                        mm = gemm(2 * hf, s, hf, h_hi, h_lo, KT)
                        mm.then_inc(sem(f"gb{2 * hf}_full"), 1)

            pe.wait_ge(sem("gb2_read"), 10)
            pe.wait_ge(sem("rstd1"), 1)
            for blk in range(NB):
                for c in range(2):
                    o = (blk % 2) * 256 + c * P
                    last = pe.transpose(mb[blk // 2][:, o:o + P], fa[:, 8 + c, blk * P:(blk + 1) * P], m_("ident"))
                if blk % 2:
                    last.then_inc(sem("v_turned"), 1)

            def in_job(j, first=0, last=None):
                u, hf = 10 + j // 2, j % 2
                if first == 0:
                    pe.wait_ge(sem("w_split"), u + 1)
                    pe.wait_ge(sem(f"gb{2 * hf}_read"), u)
                mm = gemm(2 * hf, u % 2, hf, h_hi, h_lo, KT, first, last)
                if last is None or last == 3 * KT:
                    mm.then_inc(sem(f"gb{2 * hf}_full"), 1)

            pe.wait_ge(sem("lru_w_in"), 64)
            for c in range(2):
                for j in LRU_JOBS[c]:
                    in_job(j)
                pe.wait_ge(sem("lru_u"), c + 1)
                pe.wait_ge(sem("v_copied"), 4)
                if c == 1:
                    pe.wait_ge(sem("lru_gates"), 2)
                for g in range(2):
                    for hf in range(2):
                        last = pe.matmul(mb[2 * g + hf], lru_w[:, 2 * g + c, :], fa[:, 12, hf * HALF:(hf + 1) * HALF],
                                         start=True, stop=True)
                last.then_inc(sem("lru_ri"), 1)
            for j in LRU_JOBS[2]:
                in_job(j)

            def sb_scores(n):
                b, hd = SB_STEPS[n]
                r, c, keys = 64 * (hd % 2), hd // 2, (b + 1) * P
                pe.wait_ge(sem("sb_sig"), 2 * n)
                if n == 0:
                    pe.wait_ge(sem("lru_gates"), 4)
                for k0 in range(0, keys, HALF):
                    w = min(HALF, keys - k0)
                    last = pe.matmul(mb[k0 // HALF][:, 0:w], fa[r:r + 64, 4 + c, b * P:(b + 1) * P],
                                     fa[r:r + 64, 6 + c, k0:k0 + w], start=True, stop=True)
                last.then_inc(sem("sb_z"), 1)

            def sb_turn(n):
                b, hd = SB_STEPS[n]
                pe.wait_ge(sem("sb_wgt"), n + 1)
                pe.wait_ge(sem("sb_turned_read"), n)
                for k in range(b + 1):
                    last = pe.transpose(mb[2 + k // 4][:, (k % 4) * P:(k % 4 + 1) * P],
                                        fa[:, n % 2, k * P:(k + 1) * P], m_("ident"))
                last.then_inc(sem("sb_turned"), 1)

            def sb_values(n):
                b, hd = SB_STEPS[n]
                r, c, bank = 64 * (hd % 2), hd // 2, 1 + 2 * (n // 4 % 2)
                pe.wait_ge(sem("sb_turned_read"), n + 1)
                if n % 4 == 0 and n >= 8:
                    pe.wait_ge(sem("sb_lo"), n // 4 - 1)
                for k in range(b + 1):
                    last = pe.matmul(gb[bank][r:r + 64, c * P:(c + 1) * P],
                                     vtok[:, k * 256 + hd * 64:k * 256 + hd * 64 + 64],
                                     fa[:, 14 + n % 2, k * P:(k + 1) * P], start=(k == 0), stop=(k == b))
                last.then_inc(sem("sb_o"), 1)

            for n in range(len(SB_STEPS) + 1):
                j = n + JOBS_AHEAD
                if n < len(SB_STEPS):
                    sb_scores(n)
                if j < 32:
                    in_job(j, 0, 12)
                if n >= 1:
                    sb_turn(n - 1)
                if j < 32:
                    in_job(j, 12, 24)
                if n >= 1:
                    sb_values(n - 1)

            pe.wait_ge(sem("sb_turned_read"), 32)
            pe.wait_ge(sem("gb0_read"), 26)
            pe.wait_ge(sem("gb2_read"), 26)
            for blk in range(NB):
                last = pe.transpose(mb[0][:, blk * 8:blk * 8 + 8], fa[0:8, 9, blk * P:(blk + 1) * P],
                                    m_("ident")[0:8, 0:8])
            last.then_inc(sem("ab_turned"), 1)
            pe.wait_ge(sem("tk_g"), 1)
            pe.matmul(mb[1][:, 0:32], m_("tri"), tk[:, 0, :], start=True, stop=True)
            pe.matmul(mb[1][:, 32:64], m_("suffix"), tk[:, 0, :], start=True, stop=True).then_inc(sem("tk_sums"), 1)
            pe.wait_ge(sem("lora_in"), 96)
            for nm, n in (("lru_hi", 2), ("lru_lo", 2), ("sb_hi", 8), ("sb_lo", 8)):
                pe.wait_ge(sem(nm), n)

            with pe.Fori(0, NB) as i:
                v = i + 1
                at_mm = [0]

                def gates(upto):
                    upto = min(upto, 120)
                    while at_mm[0] < upto:
                        job, q = divmod(at_mm[0], 30)
                        n, hf = divmod(job, 2)
                        if q == 0:
                            pe.wait_ge(sem("w_split"), i * 2 + (27 + n))
                            pe.wait_ge(sem(f"gb{2 * hf}_read"), i * 2 + (26 + n))
                            pe.wait_ge(sem("gated"), i * 4 + (job - 1 if n else 0))
                        step = min(upto - at_mm[0], (6 - q) if q < 6 else (30 - q))
                        if q < 6:
                            mm = gemm(2 * hf + 1, n, hf, ra[:, 4 * n:4 * n + 2], ra[:, 4 * n + 2:4 * n + 4], 2, q,
                                      q + step, KT * P)
                            if q + step == 6:
                                mm.then_inc(sem(f"gb{2 * hf + 1}_full"), 1)
                        else:
                            mm = gemm(2 * hf, n, hf, h_hi, h_lo, KT, q - 6, q - 6 + step)
                            if q + step == 30:
                                mm.then_inc(sem(f"gb{2 * hf}_full"), 1)
                        at_mm[0] += step

                def heads(bank, lhs, rhs, signal, turn=False):
                    for h in range(4):
                        c = slice(h * P, (h + 1) * P)
                        if turn:
                            mm = pe.transpose(mb[bank][:, c], lhs[:, c], m_("ident"))
                        else:
                            mm = pe.matmul(mb[bank][:, c], lhs[:, c], rhs[:, c], start=True, stop=True)
                    mm.then_inc(done(signal), 1)

                gates(12)
                pe.wait_ge(sem("rw_lt"), at("rw_lt", i, 3))
                pe.wait_ge(sem("rw_o"), at("rw_o", i, 0))
                pe.wait_ge(sem("tk_ready"), 1)
                for t in range(6):
                    last = pe.matmul(mb[t // 4][:, (t % 4) * P:(t % 4 + 1) * P], lora[:, t, :], rw["lt"], start=True,
                                     stop=True)
                last.then_inc(done("rw_p1"), 1)
                pe.wait_ge(sem("rw_sq"), at("rw_sq", i))
                pe.matmul(mb[2][:, 0:256], m_("bd"), rw["t1"], start=True, stop=True).then_inc(done("rw_p2"), 1)
                gates(30)
                pe.wait_ge(sem("rw_bonp"), at("rw_bonp", i))
                pe.wait_ge(sem("rw_ln"), at("rw_ln", i))
                pe.matmul(mb[2][:, 256:512], m_("bd"), rw["bon"], start=True, stop=True).then_inc(done("rw_p3"), 1)
                pe.wait_ge(sem("rw_ar"), at("rw_ar", i, 2))
                for t in range(2):
                    pe.transpose(mb[3][:, t * P:(t + 1) * P], rw["pm"][:, (4 + t) * P:(5 + t) * P], m_("ident"))
                for t in range(2):
                    last = pe.transpose(mb[3][:, (2 + t) * P:(3 + t) * P], rw["ar"][:, t * 256:t * 256 + P], m_("ident"))
                last.then_inc(done("rw_p4"), 1)
                gates(38)
                pe.wait_ge(sem("rw_km"), at("rw_km", i))
                pe.wait_ge(sem("rw_gate"), at("rw_gate", i))

                def scores(b0, key, both, signal):
                    for h in range(4):
                        r, t = 64 * (h % 2), h // 2
                        last = pe.matmul(mb[b0 + h % 2][:, t * 256:t * 256 + 256],
                                         key[r:r + 64, t * P:(t + 1) * P], both[r:r + 64, t * 256:(t + 1) * 256],
                                         start=True, stop=True)
                    last.then_inc(done(signal), 1)

                scores(0, rw["km"], rw["ar"], "rw_p6")
                pe.wait_ge(sem("rw_bon"), at("rw_bon", i))
                for t in range(4):
                    last = pe.transpose(mb[2][:, t * P:(t + 1) * P], (rw["bt"] if t < 2 else rw["kt"])[:, (t % 2) * P:(t % 2 + 1) * P], m_("ident"))
                last.then_inc(done("rw_p5"), 1)
                pe.wait_ge(sem("rw_tokBK"), at("rw_tokBK", i))
                scores(2, rw["bm"], rw["ar"], "rw_p7")
                gates(50)
                pe.wait_ge(sem("rw_ltr"), at("rw_ltr", i, 2))
                heads(0, rw["ltr"], None, "rw_p8", turn=True)
                for h in range(4):
                    last = pe.matmul(mb[3][:, h * 64:h * 64 + 64], rw["akt"][:, h * P:(h + 1) * P],
                                     rw["tokVA"][:, h * 64:h * 64 + 64], start=True, stop=True)
                last.then_inc(done("rw_r1"), 1)

                pe.wait_ge(sem("gd_sq"), at("gd_sq", i))
                pe.matmul(mb[1][:], m_("bd"), gd["sq"], start=True, stop=True).then_inc(done("gd_g1"), 1)
                pe.wait_ge(sem("gd_gbc"), at("gd_gbc", i, 2))
                for h in range(4):
                    last = pe.matmul(mb[2][:, h * P:(h + 1) * P], gd["gbc"][:, h * P:(h + 1) * P], m_("tri"), start=True,
                                     stop=True)
                last.then_inc(done("gd_g2"), 1)
                gates(62)
                pe.wait_ge(sem("rw_x"), at("rw_x", i))
                for t in range(4):
                    last = pe.matmul(mb[3][:, t * P:(t + 1) * P], gd["bb"][:, t * P:(t + 1) * P],
                                     m_("tri" if t < 2 else "ident"), start=True, stop=True)
                last.then_inc(done("gd_g3"), 1)
                pe.wait_ge(sem("gd_rn"), at("gd_rn", i))
                pe.wait_ge(sem("gd_kn"), at("gd_kn", i))
                for t in range(2):
                    pe.transpose(mb[1][:, t * P:(t + 1) * P], gd["kn"][:, t * P:(t + 1) * P], m_("ident"))
                for t in range(2):
                    last = pe.transpose(mb[1][:, (2 + t) * P:(3 + t) * P], gd["acc"][:, (4 + t) * P:(5 + t) * P], m_("ident"))
                last.then_inc(done("gd_g4"), 1)
                pe.wait_ge(sem("gd_kbq"), at("gd_kbq", i, 2))
                pe.wait_ge(sem("gd_eg"), at("gd_eg", i))
                scores(2, gd["kn"], gd["kbq"], "gd_g5")
                gates(72)
                pe.wait_ge(sem("gd_ltr"), at("gd_ltr", i))
                heads(1, gd["ltr"], None, "gd_g6", turn=True)

                fill = 72
                for lv in range(5):
                    last_lv = lv == 4
                    for nm, b_, st in (("rw", rw, 0), ("gd", gd, 1)):
                        pe.wait_ge(sem(f"{nm}_T"), at(f"{nm}_T", i, 2 * lv + 1))
                        heads(0 if nm == "rw" else 3, b_["ltr"], b_["T"], f"{nm}_Y")
                    fill += 4
                    gates(fill)
                    for nm, b_ in (("rw", rw), ("gd", gd)):
                        if nm == "rw":
                            pe.wait_ge(sem("rw_Ym"), at("rw_Ym", i, lv + 1))
                        else:
                            pe.wait_ge(sem("rw_T"), at("rw_T", i, min(2 * lv + 3, 10)))
                        if not last_lv:
                            heads(1, b_["TT"], b_["Y"], f"{nm}_Z")
                        heads(2, b_["Y"], b_["TT"], f"{nm}_Z")
                        fill += 3
                        gates(fill)
                fill_inv = fill

                def intra(nm, bank, b_, rhs, key):
                    pe.wait_ge(sem(f"{nm}_T"), at(f"{nm}_T", i, 10))
                    for h in range(4):
                        pe.matmul(mb[bank][:, h * 64:h * 64 + 64], b_["TT"][:, h * P:(h + 1) * P],
                                  rhs[:, h * 64:h * 64 + 64], start=True, stop=True)
                    for h in range(4):
                        r, c = 64 * (h % 2), 256 + (h // 2) * P
                        last = pe.matmul(mb[bank][r:r + 64, c:c + P], key[:, h * 64:h * 64 + 64],
                                         b_["TT"][:, h * P:(h + 1) * P], start=True, stop=True)
                    last.then_inc(done(f"{nm}_r3"), 1)

                intra("rw", 1, rw, rw["x"], rw["tokVA"][:, 256:512])
                intra("gd", 3, gd, gd["vb"], gd["kbe"])
                gates(fill_inv + 4)
                for par_ in range(2):
                    R = slice(64 * par_, 64 * par_ + 64)
                    for nm, b_, st, ws in (("rw", rw, 0, 0), ("gd", gd, 1, 256)):
                        if par_ == 0:
                            pe.wait_ge(sem(f"{nm}_uw"), at(f"{nm}_uw", i))
                        if nm == "rw":
                            pe.wait_ge(sem("gd_S"), at("gd_S", i, 4 * par_))
                        for t in range(2):
                            last = pe.matmul(mb[0][R, ws + t * P:ws + (t + 1) * P],
                                             b_["uw"][:, 256 + t * P + 64 * par_:256 + t * P + 64 * par_ + 64],
                                             state[:, st, t, :], start=True, stop=True)
                        last.then_inc(done(f"{nm}_ws"), 1)
                    gates(fill_inv + 6 + 6 * par_)
                    for nm, b_, st, yb, sc in (("rw", rw, 0, 2, 1), ("gd", gd, 1, 3, 0)):
                        for t in range(2):
                            q_ = (rw["ar"][:, t * 256 + P + 64 * par_:t * 256 + P + 64 * par_ + 64] if nm == "rw"
                                  else gd["qd"][:, t * P + 64 * par_:t * P + 64 * par_ + 64])
                            if nm == "rw" and par_ == 0 and t == 0:
                                pe.wait_ge(sem("gd_T"), at("gd_T", i, 10))
                            pe.matmul(mb[yb][:, t * P + 64 * par_:t * P + 64 * par_ + 64], state[:, st, t, :], q_,
                                      start=(par_ == 0 and t == 0), stop=True, skip_group_check=True)
                        pe.wait_ge(sem(f"{nm}_u"), at(f"{nm}_u", i, par_ + 1))
                        for t in range(2):
                            c = slice(t * P, (t + 1) * P)
                            if nm == "rw":
                                pe.matmul(mb[sc][:, c], rw["tokBK"][R, c], rw["u"][R, c],
                                          start=True, stop=False)
                                last = pe.matmul(mb[sc][:, c], rw["tokBK"][R, 256 + t * P:256 + (t + 1) * P], rw["tokVA"][R, c],
                                                 start=False, stop=True)
                            else:
                                last = pe.matmul(mb[sc][:, c], gd["kd"][R, c], gd["u"][R, c], start=True, stop=True)
                        last.then_inc(done(f"{nm}_s"), 1)
                        terms = [(b_["u"], rw["rbt"] if nm == "rw" else gd["qkt"])]
                        if nm == "rw":
                            terms.append((rw["tokVA"], rw["rkt"]))
                        for h in range(4):
                            r, c = 64 * (h % 2), (h // 2) * P + 64 * par_
                            for lhs, rhs in terms:
                                last = pe.matmul(mb[yb][r:r + 64, c:c + 64], lhs[R, h * 64:h * 64 + 64],
                                                 rhs[R, h * P + 64 * par_:h * P + 64 * par_ + 64], start=False, stop=True,
                                                 skip_group_check=True)
                        last.then_inc(done(f"{nm}_Yd"), 1)
                gates(fill_inv + 14)
                pe.wait_ge(sem("rw_y"), at("rw_y", i))
                pe.wait_ge(sem("gd_S"), at("gd_S", i, 8))
                pe.matmul(mb[0][:, 0:256], m_("bd"), rw["y"], start=True, stop=True).then_inc(done("rw_m1"), 1)
                
                pe.wait_ge(sem("gd_y2"), at("gd_y2", i))
                pe.matmul(mb[1][:, 0:256], m_("bd"), gd["y2"], start=True, stop=True).then_inc(done("gd_m"), 1)
                gates(120)
                pe.wait_ge(sem("rw_y2"), at("rw_y2", i))
                pe.matmul(mb[0][:, 256:512], m_("bd"), rw["y2"], start=True, stop=True).then_inc(done("rw_m2"), 1)

            ra_in = [(ra[:, 4 * n:4 * n + 2], ra[:, 4 * n + 2:4 * n + 4]) for n in range(2)]
            with pe.Fori(0, KT) as i:
                for job in range(4):
                    n, hf = divmod(job, 2)
                    if hf == 0:
                        pe.wait_ge(sem("w_split"), i * 2 + (U_MIX2 + 1 + n))
                    pe.wait_ge(sem(f"gb{2 * hf}_read"), i * 2 + (U_MIX2 + n))
                    gemm(2 * hf, n, hf, h_hi, h_lo, KT).then_inc(sem(f"gb{2 * hf}_full"), 1)
                    pe.wait_ge(sem("gated"), i * 4 + (4 * NB - 1 + job))
                    pe.wait_ge(sem("o_lo"), 1 + n)
                    gemm(2 * hf + 1, n, hf, *ra_in[n], 2, off=KT * P).then_inc(sem(f"gb{2 * hf + 1}_full"), 1)

            def out_unit(m, slot, first):
                pe.wait_ge(sem("w_split"), m + (U_OUT + 1))
                for hf in range(2):
                    if first:
                        pe.wait_ge(sem("gated"), 8 * NB)
                    else:
                        pe.wait_ge(sem("x1"), m * 2 + (hf - 3))
                    if first and slot == 0:
                        for k in range(KT):
                            pe.wait_ge(sem("mixed_lo"), k + 1)
                            mm = gemm(2 * hf + slot, slot, hf, h_hi, h_lo, KT, 3 * k, 3 * k + 3)
                    else:
                        mm = gemm(2 * hf + slot, slot, hf, h_hi, h_lo, KT)
                    mm.then_inc(sem("half_done"), 1)

            for m in range(2):
                out_unit(m, m, True)
            with pe.Fori(0, KT // 2 - 1) as i:
                for n in range(2):
                    out_unit(i * 2 + (2 + n), n, False)

            def sum_over_channels(n, bank):
                pe.wait_ge(sem("sq_added"), n * (KT - 1))
                for hf in range(2):
                    mm = pe.matmul(bank[hf], m_("ones"), fa[:, ACC, hf * HALF:(hf + 1) * HALF], start=True, stop=True)
                mm.then_inc(sem("sq_summed"), 1)

            pe.wait_ge(sem("rw_rno"), at("rw_rno", NB - 1))
            pe.wait_ge(sem("rw_o"), at("rw_o", NB - 1))
            sum_over_channels(1, mb)

            def ffn_tile(t, u):
                first = isinstance(t, int) and t == 0
                for up in range(2):
                    pe.wait_ge(sem("w_split"), u + (1 + up))
                    for hf in range(2):
                        if first:
                            pe.wait_ge(sem("x1"), 2 * KT)
                        else:
                            pe.wait_ge(sem("up_read" if up else "gate_read"), t * 2 + (hf - 1))
                        if first and not up and hf == 0:
                            for k in range(KT):
                                pe.wait_ge(sem("h_done"), KT + k + 1)
                                mm = gemm(2 * hf + up, up, hf, h_hi, h_lo, KT, 3 * k, 3 * k + 3)
                        else:
                            mm = gemm(2 * hf + up, up, hf, h_hi, h_lo, KT)
                        mm.then_inc(sem("half_done"), 1)

            def ffn_down(g, u, d, ks):
                pe.wait_ge(sem("w_split"), u + (1 + d))
                n = KT // ks
                for ml in range(n):
                    m = d * n + ml
                    pe.wait_ge(sem("down_read"), g * KT + (m - 1 if m >= 2 else 0))
                    for hf in range(2):
                        for q in range(3 * ks):
                            k, which = divmod(q, 3)
                            w = (w_lo if which == 2 else w_hi)[:, d % 2, (ml * ks + k) * P:(ml * ks + k + 1) * P]
                            x_ = ra[:, (GT if which == 1 else 0) + k, hf * HALF:(hf + 1) * HALF]
                            mm = pe.matmul(mb[2 * (ml % 2) + hf], w, x_, start=(q == 0), stop=(q == 3 * ks - 1))
                    if ml % (n // 2) == n // 2 - 1:
                        mm.then_inc(sem("half_done"), 1)

            ffn_tile(0, U_FFN)
            pe.wait_ge(sem("rstd"), 1)
            with pe.Fori(0, NG) as g:
                for q in range(GT):
                    ffn_tile(g * GT + (1 + q), g * UG + (U_FFN + 2 + 2 * q))
                pe.wait_ge(sem("act_lo"), g * GT + GT)
                for d in range(4):
                    ffn_down(g, g * UG + (U_FFN + 2 + 2 * GT), d, GT)
            ffn_tile(FT - 1, UNITS - 4)
            pe.wait_ge(sem("act_lo"), FT)
            for d in range(2):
                ffn_down(NG, UNITS - 2, d, FT - NG * GT)

            pe.wait_ge(sem("up_read"), 2 * FT)
            pe.wait_ge(sem("gate_read"), 2 * FT)
            sum_over_channels(2, gb)

        @block.scalar
        def _(act):
            def softplus_act(nth, n):
                act.activation(sp_t[:, 2, 0:n], sp_t[:, 1, 0:n], ACT.Exp, scale=-1.0).then_inc(sem("softplus_exp"), 1)
                act.wait_ge(sem("softplus_1p"), nth)
                act.activation(sp_t[:, 4, 0:n], sp_t[:, 3, 0:n], ACT.Ln).then_inc(sem("softplus_ln"), 1)

            act.wait_ge(sem("c_in"), 16)
            act.activation(fa[:, 11, :], fa[:, 11, :], ACT.Silu).then_inc(sem("cond"), 1)
            for k in range(KT):
                act.wait_ge(sem(f"x_in{k}"), 16)
                if k >= 2:
                    act.wait_ge(sem("sq_used"), k - 1)
                act.activation(fa[:, 8 + 2 * (k % 2), :], fa[:, k, :], ACT.Square).then_inc(sem("sq"), 1)
            act.wait_ge(sem("sq_used"), KT)
            act.wait_ge(sem("zero_set"), 6)
            for hf in range(2):
                act.activation(fa[:, 9, hf * HALF:(hf + 1) * HALF], mb[hf], ACT.Ln, bias=eps[:, 0:1],
                               scale=1.0 / D).then_inc(sem("ln1"), 1)
            act.wait_ge(sem("ln1"), 2)
            act.activation(fa[:, 9, :], fa[:, 9, :], ACT.Exp, scale=-0.5).then_inc(sem("rstd1"), 1)
            for k in range(KT):
                act.wait_ge(sem("h_f32"), k + 1)
                act.activation(h_hi[:, k, :], fa[:, k, :], ACT.Copy).then_inc(sem("h_hi"), 1)
            with act.Fori(0, 5) as i:
                for s in range(2):
                    for hf in range(2):
                        act.wait_ge(sem(f"gb{2 * hf}_full"), i * 2 + (s + 1))
                        act.activation(fa[:, bass.ds(i * 2 + s, 1), hf * HALF:(hf + 1) * HALF], gb[2 * hf], ACT.Copy).then_inc(sem(f"gb{2 * hf}_read"), 1)

            def in_read(j):
                u, hf = 10 + j // 2, j % 2
                slot = u % 2
                act.wait_ge(sem(f"gb{2 * hf}_full"), u + 1)
                if u < 12:
                    act.wait_ge(sem("v_turned"), 4)
                else:
                    act.wait_ge(sem(f"p_out{slot}"), 32 * ((u - 10) // 2))
                act.activation(fa[:, 8 + slot, hf * HALF:(hf + 1) * HALF], gb[2 * hf], ACT.Copy).then_inc(
                    sem(f"gb{2 * hf}_read"), 1)
                if u < 25:
                    act.wait_ge(sem(f"gb{2 * hf}_read"), u + 1)
                    act.dma_start(p_scr[u - 10][:, HALO + hf * HALF:HALO + (hf + 1) * HALF],
                                  fa[:, 8 + slot, hf * HALF:(hf + 1) * HALF]).then_inc(sem(f"p_out{slot}"), 16)

            act.wait_ge(sem("softplus_abs"), 1)
            softplus_act(1, 2)
            for i in range(4):
                act.wait_ge(sem("v_turned"), i + 1)
                act.activation(vtok[:, i * HALF:(i + 1) * HALF], mb[i], ACT.Copy).then_inc(sem("v_copied"), 1)
            for j in LRU_JOBS[0]:
                in_read(j)
            for c in range(2):
                act.wait_ge(sem("lru_ri"), c + 1)
                if c == 1:
                    act.wait_ge(sem("lru_scan"), 1)
                act.activation(fa[:, 13, :], mbank[:, 0:2, :].rearrange("p b s -> p (b s)"), ACT.Sigmoid,
                               bias=pc("lru_br", c)).then_inc(sem("lru_gates"), 1)
                act.activation(fa[:, 14, :], mbank[:, 2:4, :].rearrange("p b s -> p (b s)"), ACT.Sigmoid,
                               bias=pc("lru_bi", c)).then_inc(sem("lru_gates"), 1)
                act.wait_ge(sem("lru_gates"), 2 * c + 1)
                act.wait_ge(sem("sl"), 1)
                act.activation(fa[:, 15, :], fa[:, 13, :], ACT.Exp, scale=sl[:, c:c + 1]).then_inc(sem("lru_a"), 1)
                act.wait_ge(sem("lru_a"), 3 * c + 1)
                act.activation(fa[:, 13, :], fa[:, 13, :], ACT.Tanh, scale=sl[:, 2 + c:3 + c]).then_inc(sem("lru_a"), 1)
                act.activation(fa[:, 2 + c, :], fa[:, 2 + c, :], ACT.Gelu_apprx_tanh).then_inc(sem("lru_gelu"), 1)
                act.wait_ge(sem("lru_b2"), c + 1)
                act.activation(fa[:, 13, :], fa[:, 13, :], ACT.Sqrt).then_inc(sem("lru_a"), 1)
                for j in LRU_JOBS[c + 1]:
                    in_read(j)
                act.wait_ge(sem("lru_o"), c + 1)
                act.activation(ra[:, c, :], fa[:, 12, :], ACT.Copy).then_inc(sem("lru_hi"), 1)

            def sb_sigmoids(n):
                b, hd = SB_STEPS[n]
                keys = (b + 1) * P
                z = mbank[:, 0:2, :].rearrange("p b s -> p (b s)")[:, 0:keys]
                act.wait_ge(sem("sb_z"), n + 1)
                if n == 0:
                    act.wait_ge(sem("lru_lo"), 2)
                if n >= 2:
                    act.wait_ge(sem("sb_turned"), n - 1)
                    act.wait_ge(sem("sb_scan"), n - 1)
                act.activation(fa[:, n % 2, 0:keys], z, ACT.Sigmoid, scale=HEAD ** -0.5).then_inc(sem("sb_sig"), 1)
                act.activation(fa[:, 2 + n % 2, 0:keys], z, ACT.Sigmoid, scale=-HEAD ** -0.5).then_inc(sem("sb_sig"), 1)

            def sb_copy(n):
                b, hd = SB_STEPS[n]
                keys = (b + 1) * P
                act.wait_ge(sem("sb_turned"), n + 1)
                if n >= 2:
                    act.wait_ge(sem("sb_o"), n - 1)
                act.activation(fa[:, 14 + n % 2, 0:keys], mbank[:, 2:4, :].rearrange("p b s -> p (b s)")[:, 0:keys],
                               ACT.Copy).then_inc(sem("sb_turned_read"), 1)

            def sb_hi(n):
                b, hd = SB_STEPS[n]
                bank = 1 + 2 * (n // 4 % 2)
                act.wait_ge(sem("sb_o"), n + 1)
                act.activation(ra[:, 4:6, b * P:(b + 1) * P], gb[bank][:, 0:256].rearrange("p (c s) -> p c s", c=2),
                               ACT.Copy).then_inc(sem("sb_hi"), 1)

            for n in range(len(SB_STEPS) + 1):
                j = n + JOBS_AHEAD
                if n < len(SB_STEPS):
                    sb_sigmoids(n)
                if n >= 1:
                    sb_copy(n - 1)
                if j < 32:
                    in_read(j)
                if n >= 1 and (n - 1) % 4 == 3:
                    sb_hi(n - 1)

            act.wait_ge(sem("ab_read"), 1)
            act.activation(tk[:, 1, :].rearrange("p (b h) -> p b h", h=4), abt[:].rearrange("p (b h) -> p b h", h=8)[:, :, 4:8],
                           ACT.Sigmoid).then_inc(sem("tk_act"), 1)
            act.wait_ge(sem("softplus_abs"), 2)
            softplus_act(2, 32)
            act.activation(ea[:], par[:, PAR["alog"]], ACT.Exp).then_inc(sem("ea"), 1)
            act.wait_ge(sem("tk_sums"), 1)
            act.activation(tk[:, 2, :], mb[1][:, 0:32], ACT.Copy).then_inc(sem("tk_act"), 1)
            act.activation(tk[:, 3, :], mb[1][:, 32:64], ACT.Exp).then_inc(sem("tk_act"), 1)
            act.activation(tk[:, 5, :], mb[1][:, 0:32], ACT.Exp).then_inc(sem("tk_act"), 1)

            with act.Fori(0, NB) as i:
                v = i + 1

                def gate_sig(job):
                    n, hf = divmod(job, 2)
                    if hf == 0:
                        act.wait_ge(sem("gated"), i * 4 + (2 * n if n else 0))
                        act.activation(bgc[:, n:n + 1], par[:, bass.ds(i + (PAR["b_gate"].start + 8 * n), 1)],
                                       ACT.Copy).then_inc(sem("bgc"), 1)
                        act.wait_ge(sem("bgc"), i * 2 + (n + 1))
                    act.wait_ge(sem(f"gb{2 * hf}_full"), i * 2 + (27 + n))
                    act.wait_ge(sem("gated"), i * 4 + job)
                    act.activation(sig, gb[2 * hf], ACT.Sigmoid, bias=bgc[:, n:n + 1]).then_inc(sem(f"gb{2 * hf}_read"), 1)

                act.wait_ge(sem("rw_pm"), at("rw_pm", i))
                act.wait_ge(sem("rw_m2"), at("rw_m2", i, 0))
                act.activation(rw["lt"][0:32, :], rw["pm"][0:32, 6 * P:7 * P], ACT.Tanh).then_inc(done("rw_lt"), 1)
                act.activation(rw["lt"][32:64, :], rw["pm"][32:64, 6 * P:7 * P], ACT.Copy).then_inc(done("rw_lt"), 1)
                act.activation(rw["lt"][64:128, :], rw["pm"][64:128, 6 * P:7 * P], ACT.Sigmoid).then_inc(done("rw_lt"), 1)
                act.wait_ge(sem("rw_kkr"), at("rw_kkr", i))
                act.activation(rw["t1"], rw["kkr"], ACT.Square).then_inc(done("rw_sq"), 1)
                act.wait_ge(sem("rw_p1"), at("rw_p1", i))
                for t in range(2):
                    act.activation(rw["sw"][:, t * P:(t + 1) * P], mb[0][:, t * P:(t + 1) * P], ACT.Sigmoid,
                                   bias=pc("rw_w0", t)).then_inc(done("rw_sw"), 1)
                for t in range(2):
                    act.activation(rw["sa"][:, t * P:(t + 1) * P], mb[0][:, (2 + t) * P:(3 + t) * P], ACT.Sigmoid,
                                   bias=pc("rw_a0", t)).then_inc(done("rw_sa"), 1)
                act.activation(rw["gate"], mb[1][:, 0:256], ACT.Copy).then_inc(done("rw_gate"), 1)
                act.wait_ge(sem("rw_p2"), at("rw_p2", i))
                act.activation(rw["rn"], mb[2][:, 0:256], ACT.Ln, bias=eps[:, 0:1]).then_inc(done("rw_ln"), 1)
                act.wait_ge(sem("rw_ln"), at("rw_ln", i))
                act.activation(rw["rn"], rw["rn"], ACT.Exp, scale=-0.5).then_inc(done("rw_rn"), 1)
                act.wait_ge(sem("rw_gs"), at("rw_gs", i, 2))
                act.activation(rw["ex1"], rw["gs"], ACT.Exp, scale=-E_HALF).then_inc(done("rw_ex"), 1)
                act.activation(rw["exn"], rw["gs"], ACT.Exp, scale=E_HALF).then_inc(done("rw_ex"), 1)
                act.wait_ge(sem("rw_gm"), at("rw_gm", i))
                act.activation(rw["ex0"], rw["gm"], ACT.Exp, scale=-E_HALF).then_inc(done("rw_ex"), 1)
                act.wait_ge(sem("rw_p4"), at("rw_p4", i))
                act.activation(rw["tokVA"], mb[3], ACT.Copy).then_inc(done("rw_tokVA"), 1)
                gate_sig(0)
                act.wait_ge(sem("rw_p5"), at("rw_p5", i))
                act.activation(rw["tokBK"], mb[2], ACT.Copy).then_inc(done("rw_tokBK"), 1)
                act.wait_ge(sem("gd_acc"), at("gd_acc", i))
                act.activation(gd["acc"], gd["acc"], ACT.Silu).then_inc(done("gd_silu"), 1)
                act.activation(t2(gd["z"]), pblk[:, 13:15, HALO:], ACT.Silu).then_inc(done("pblk_read"), 1)
                act.wait_ge(sem("gd_silu"), at("gd_silu", i))
                act.activation(gd["sq"], gd["acc"][:, 0:512], ACT.Square).then_inc(done("gd_sq"), 1)
                act.wait_ge(sem("tkc"), at("tkc", i))
                act.activation(t4(gd["gbc"]), tkc[:, 0:4].rearrange("p (h o) -> p h o", o=1).to_broadcast([P, 4, P]),
                               ACT.Copy).then_inc(done("gd_gbc"), 1)
                act.activation(gd["bb"].rearrange("p (h c) -> p h c", c=64),
                               tkc[:, 0:8].rearrange("p (h o) -> p h o", o=1).to_broadcast([P, 8, 64]),
                               ACT.Copy).then_inc(done("gd_gbc"), 1)
                act.wait_ge(sem("rw_r1"), at("rw_r1", i))
                act.activation(rw["x"], mb[3][:, 0:256], ACT.Copy).then_inc(done("rw_x"), 1)
                act.wait_ge(sem("gd_g1"), at("gd_g1", i))
                act.activation(gd["rn"], mb[1], ACT.Ln, bias=eps[:, 0:1]).then_inc(done("gd_ln"), 1)
                act.wait_ge(sem("gd_ln"), at("gd_ln", i))
                act.activation(gd["rn"], gd["rn"], ACT.Exp, scale=-0.5).then_inc(done("gd_rn"), 1)
                act.wait_ge(sem("gd_dtm"), at("gd_dtm", i))
                act.activation(gd["dt"], gd["dt"], ACT.Exp).then_inc(done("gd_dt"), 1)
                act.wait_ge(sem("gd_g3"), at("gd_g3", i))
                act.activation(gd["eg"], mb[3][:, 0:256], ACT.Exp).then_inc(done("gd_eg"), 1)
                gate_sig(1)
                for nm, bank, b_ in (("rw", 1, rw), ("gd", 3, gd)):
                    act.wait_ge(sem(f"{nm}_r3"), at(f"{nm}_r3", i))
                    act.activation(b_["uw"], mb[bank], ACT.Copy).then_inc(done(f"{nm}_uw"), 1)
                gate_sig(2)
                act.wait_ge(sem("rw_Yd"), at("rw_Yd", i, 2))
                act.activation(rw["y"], mb[2][:, 0:256], ACT.Copy).then_inc(done("rw_y"), 1)
                act.wait_ge(sem("gd_Yd"), at("gd_Yd", i, 2))
                act.activation(gd["y2"], mb[3][:, 0:256], ACT.Square).then_inc(done("gd_y2"), 1)
                act.wait_ge(sem("gd_m"), at("gd_m", i))
                act.activation(gd["rno"], mb[1][:, 0:256], ACT.Ln, bias=eps[:, 0:1], scale=1.0 / HEAD).then_inc(done("gd_lno"), 1)
                act.wait_ge(sem("gd_lno"), at("gd_lno", i))
                act.activation(gd["rno"], gd["rno"], ACT.Exp, scale=-0.5).then_inc(done("gd_rno"), 1)
                act.wait_ge(sem("rw_yc"), at("rw_yc", i))
                act.activation(rw["y2"], rw["yc"], ACT.Square).then_inc(done("rw_y2"), 1)
                gate_sig(3)
                act.wait_ge(sem("rw_m2"), at("rw_m2", i))
                act.activation(rw["u"], mb[0][:, 256:512], ACT.Ln, bias=eps[:, 1:2], scale=1.0 / HEAD).then_inc(done("rw_lno"), 1)
                act.wait_ge(sem("rw_lno"), at("rw_lno", i))
                act.activation(rw["u"], rw["u"], ACT.Exp, scale=-0.5).then_inc(done("rw_rno"), 1)

            act.wait_ge(sem("o_in"), 16)
            for n in range(2):
                act.activation(ra[:, 4 * n:4 * n + 2], fa[:, 8 + 2 * n:10 + 2 * n, :], ACT.Copy).then_inc(sem("o_hi"), 1)
            with act.Fori(0, KT) as i:
                for job in range(4):
                    n, hf = divmod(job, 2)
                    act.wait_ge(sem("gated"), i * 4 + (4 * NB - 3 + job))
                    if hf == 0:
                        act.activation(bgc[:, n:n + 1], par[:, bass.ds(i + (PAR["b_gate"].start + 16 + 8 * n), 1)],
                                       ACT.Copy).then_inc(sem("bgc"), 1)
                        act.wait_ge(sem("bgc"), i * 2 + (2 * NB + n + 1))
                    act.wait_ge(sem(f"gb{2 * hf}_full"), i * 2 + (U_MIX2 + 1 + n))
                    act.activation(sig4[job], gb[2 * hf], ACT.Sigmoid, bias=bgc[:, n:n + 1]).then_inc(sem(f"gb{2 * hf}_read"), 1)
            act.wait_ge(sem("gb0_full"), U_OUT)
            act.wait_ge(sem("gb2_full"), U_OUT)
            act.wait_ge(sem("gated"), 8 * NB)
            for k in range(KT):
                act.activation(h_hi[:, k, :], fa[:, k, :], ACT.Copy).then_inc(sem("mixed_hi"), 1)

            def square(m, par_, nth, ready, count):
                act.wait_ge(sem(ready), count)
                if isinstance(m, int) and m == 0:
                    act.activation(fa[:, ACC, :], fa[:, 0, :], ACT.Square).then_inc(sem("sq"), 1)
                    return
                if not (isinstance(m, int) and m < 3):
                    act.wait_ge(sem("sq_added"), m + (7 * nth - 2))
                src = fa[:, m, :] if isinstance(m, int) else fa[:, bass.ds(m, 1), :]
                act.activation(fa[:, SQ + par_, :], src, ACT.Square).then_inc(sem("sq"), 1)

            def root(n, bank):
                act.wait_ge(sem("sq_summed"), n)
                act.activation(fa[:, RSTD, :], bank, ACT.Ln, bias=eps[:, 0:1], scale=1.0 / D).then_inc(sem("ln2"), 1)
                act.wait_ge(sem("ln2"), n)
                act.activation(fa[:, RSTD, :], fa[:, RSTD, :], ACT.Exp, scale=-0.5).then_inc(sem("rstd"), 1)

            for m in range(KT):
                square(m, m % 2, 0, "x1", 2 * m + 2)
            root(1, mbank[:, 0:2, :].rearrange("p b s -> p (b s)"))
            act.wait_ge(sem("half_done"), 2 * KT)
            for k in range(KT):
                act.wait_ge(sem("h_f32"), KT + k + 1)
                act.activation(h_hi[:, k, :], fa[:, 12 + k % 4, :], ACT.Copy).then_inc(sem("h_hi"), 1)

            def ffn_act(t, s_, half):
                for hf in range(2):
                    act.wait_ge(sem("half_done"), half + hf)
                    if not (isinstance(t, int) and t < 2):
                        act.wait_ge(sem("conv"), t - 1)
                    act.activation(G[s_][:, 2 + hf * HALF:2 + (hf + 1) * HALF], gb[2 * hf], ACT.Copy).then_inc(sem("gate_read"), 1)
                act.wait_ge(sem("conv"), t + 1)
                act.activation(C[s_], C[s_], ACT.Gelu_apprx_tanh).then_inc(sem("gelu"), 1)

            def ffn_hi(t, s_, j):
                act.wait_ge(sem("up_read"), t * 2 + 2)
                act.activation(ra[:, j, :], fa[:, 13 + s_, :], ACT.Copy).then_inc(sem("act_hi"), 1)

            act.wait_ge(sem("g_halo"), 2)
            ffn_act(0, 0, 2 * KT + 1)
            ffn_hi(0, 0, 0)
            with act.Fori(0, NG) as g:
                for q in range(GT):
                    t, u = g * GT + (1 + q), 2 * (2 + 2 * q) + 2 * KT
                    ffn_act(t, (1 + q) % 2, g * (2 * UG) + (u + 1))
                    if q < GT - 1:
                        ffn_hi(t, (1 + q) % 2, 1 + q)
                act.wait_ge(sem("half_done"), g * (2 * UG) + (2 * KT + 4 + 2 * UG))
                ffn_hi(g * GT + GT, 0, 0)
            ffn_act(FT - 1, 1, 2 * (UNITS - U_OUT) - 7)
            ffn_hi(FT - 1, 1, 1)
            for m in range(KT):
                square(m, m % 2, 1, "down_read", KT * NG + m + 1)
            root(2, gbank[:, 0:2, :].rearrange("p b s -> p (b s)"))

        @block.vector
        def _(dve):
            def ada(t, slot, landed, col):
                dve.wait_ge(sem(f"ada_in{slot}"), landed)
                dve.tensor_tensor_reduce(fa[:, 12 + slot, :], fa[:, 12 + slot, :], fa[:, 11, :], 1.0, 0.0, ALU.mult,
                                         ALU.add, col).then_inc(sem("ada_used"), 1)

            dve.wait_ge(sem("cond"), 1)
            for t in range(16):
                ada(t, t % 3, 16 * (t // 3 + 1), mod[:, t:t + 1])
            dve.wait_ge(sem("ada_used"), 16)
            dve.wait_ge(sem("par_in"), 16)
            dve.tensor_tensor(mod[:, 0:16], mod[:, 0:16], par[:, PAR["b_ada"].start:PAR["b_ada"].start + 16],
                              ALU.add).then_inc(sem("mod1"), 1)
            dve.wait_ge(sem("mod1"), 1)
            dve.scalar_tensor_tensor(a1[:, 0:8], mod[:, 8:16], 1.0, par[:, PAR["n1"]], ALU.add, ALU.mult).then_inc(sem("a1"), 1)
            dve.wait_ge(sem("a1"), 1)
            dve.wait_ge(sem("rstd1"), 1)
            for k in range(KT):
                dve.tensor_tensor(fa[:, k, :], fa[:, k, :], fa[:, 9, :], ALU.mult).then_inc(sem("h_norm"), 1)
            for k in range(KT):
                dve.wait_ge(sem("h_norm"), k + 1)
                dve.tensor_scalar(fa[:, k, :], fa[:, k, :], a1[:, k:k + 1], mod[:, k:k + 1], ALU.mult,
                                  ALU.add).then_inc(sem("h_f32"), 1)
                if k >= 1:
                    dve.wait_ge(sem("h_hi"), k)
                    dve.tensor_tensor(h_lo[:, k - 1, :], fa[:, k - 1, :], h_hi[:, k - 1, :].bitcast(F32), ALU.subtract).then_inc(sem("h_done"), 1)
            dve.wait_ge(sem("h_hi"), KT)
            dve.tensor_tensor(h_lo[:, KT - 1, :], fa[:, KT - 1, :], h_hi[:, KT - 1, :].bitcast(F32), ALU.subtract).then_inc(sem("h_done"), 1)
            for t in range(16, 18):
                ada(t, t % 3, 16 * (t // 3 + 1), mod[:, t:t + 1])
            with dve.Fori(0, 5) as i:
                dve.wait_ge(sem("mod_copied"), i)
                for t in range(6):
                    ada(None, t % 3, i * 32 + (96 + 16 * (t // 3 + 1)), mod6[:, t:t + 1])
                dve.wait_ge(sem("ada_used"), i * 6 + 24)
                dve.tensor_copy(mod[:, bass.ds(i * 6 + 18, 6)], mod6[:]).then_inc(sem("mod_copied"), 1)

            def softplus(nth, y, n, out_ap):
                st = sp_t[:, :, 0:n]
                done = sem("softplus_steps")
                dve.scalar_tensor_tensor(st[:, 1, :], y, -1.0, y, ALU.mult, ALU.max).then_inc(sem("softplus_abs"), 1)
                dve.wait_ge(sem("softplus_exp"), nth)
                dve.tensor_scalar(st[:, 3, :], st[:, 2, :], 1.0, None, ALU.add).then_inc(sem("softplus_1p"), 1)
                dve.wait_ge(sem("softplus_1p"), nth)
                dve.tensor_scalar(st[:, 5, :], st[:, 3, :], 1.0, None, ALU.subtract).then_inc(done, 1)
                dve.wait_ge(done, 8 * nth - 7)
                dve.tensor_scalar(st[:, 6, :], st[:, 5, :], 0.0, None, ALU.is_equal).then_inc(done, 1)
                dve.tensor_scalar(st[:, 7, :], st[:, 5, :], 1e-8, None, ALU.max).then_inc(done, 1)
                dve.wait_ge(done, 8 * nth - 5)
                dve.reciprocal(st[:, 5, :], st[:, 7, :]).then_inc(done, 1)
                dve.wait_ge(sem("softplus_ln"), nth)
                dve.wait_ge(done, 8 * nth - 4)
                dve.tensor_tensor(st[:, 5, :], st[:, 5, :], st[:, 4, :], ALU.mult).then_inc(done, 1)
                dve.wait_ge(done, 8 * nth - 3)
                dve.tensor_tensor(st[:, 5, :], st[:, 5, :], st[:, 6, :], ALU.add).then_inc(done, 1)
                dve.wait_ge(done, 8 * nth - 2)
                dve.tensor_tensor(st[:, 5, :], st[:, 5, :], st[:, 2, :], ALU.mult).then_inc(done, 1)
                dve.wait_ge(done, 8 * nth - 1)
                dve.scalar_tensor_tensor(out_ap, y, 0.0, st[:, 5, :], ALU.max, ALU.add).then_inc(done, 1)
                dve.wait_ge(done, 8 * nth)

            dve.tensor_scalar(sp_t[:, 0, 0:2], par[:, PAR["lru_lam"]], -1.0, None, ALU.mult).then_inc(sem("lam_neg"), 1)
            dve.wait_ge(sem("lam_neg"), 1)
            softplus(1, sp_t[:, 0, 0:2], 2, sp_t[:, 6, 0:2])
            dve.tensor_scalar(sl[:, 0:2], sp_t[:, 6, 0:2], -8.0, None, ALU.mult).then_inc(sem("lam_sp"), 1)
            dve.tensor_scalar(sl[:, 2:4], sp_t[:, 6, 0:2], 8.0, None, ALU.mult).then_inc(sem("sl"), 1)

            dve.wait_ge(sem("gb2_read"), 10)
            dve.wait_ge(sem("ada_used"), 48)
            chain = sem("lru_chain")
            n = 0
            for c in range(2):
                x_, u_ = fa[:, c, :], fa[:, 12, :]
                if c == 1:
                    dve.wait_ge(sem("lru_hi"), 1)
                    dve.wait_ge(sem("lru_lo"), 1)
                dve.tensor_scalar(u_, x_, pc("lru_cw", c * 4 + 3), pc("lru_cb", c), ALU.mult, ALU.add).then_inc(chain, 1)
                n += 1
                for t in range(1, 4):
                    dve.wait_ge(chain, n)
                    ins = dve.scalar_tensor_tensor(u_[:, t:], x_[:, 0:S - t], pc("lru_cw", c * 4 + 3 - t), u_[:, t:],
                                                   ALU.mult, ALU.add)
                    if t < 3:
                        ins.then_inc(chain, 1)
                        n += 1
                ins.then_inc(sem("lru_u"), 1)
                dve.wait_ge(sem("lru_gates"), 2 * c + 2)
                dve.wait_ge(sem("lru_u"), c + 1)
                dve.tensor_tensor(fa[:, 14, :], fa[:, 14, :], u_, ALU.mult).then_inc(chain, 1)
                dve.wait_ge(sem("lru_a"), 3 * c + 1)
                dve.tensor_tensor(x_, fa[:, 15, :], fa[:, 15, :], ALU.mult).then_inc(chain, 1)
                n += 2
                dve.wait_ge(sem("lru_a"), 3 * c + 2)
                dve.wait_ge(chain, n)
                dve.scalar_tensor_tensor(fa[:, 13, :], x_, 1.0, fa[:, 13, :], ALU.add, ALU.mult).then_inc(sem("lru_b2"), 1)
                dve.wait_ge(sem("lru_a"), 3 * c + 3)
                dve.tensor_tensor(fa[:, 14, :], fa[:, 14, :], fa[:, 13, :], ALU.mult).then_inc(chain, 1)
                n += 1
                dve.wait_ge(chain, n)
                dve.wait_ge(sem("lru_ri"), c + 1)
                dve.tensor_tensor_scan(u_, fa[:, 15, :], fa[:, 14, :], 0.0, ALU.mult, ALU.add).then_inc(sem("lru_scan"), 1)
                dve.wait_ge(sem("lru_scan"), c + 1)
                dve.wait_ge(sem("lru_gelu"), c + 1)
                dve.tensor_tensor(u_, u_, fa[:, 2 + c, :], ALU.mult).then_inc(sem("lru_o"), 1)
                dve.wait_ge(sem("lru_hi"), c + 1)
                dve.tensor_tensor(ra[:, 2 + c, :], u_, ra[:, c, :].bitcast(F32), ALU.subtract).then_inc(sem("lru_lo"), 1)

            def sb_weights(n):
                b, hd = SB_STEPS[n]
                keys = (b + 1) * P
                beta, keep, prod = fa[:, n % 2, 0:keys], fa[:, 2 + n % 2, 0:keys], fa[:, 12 + n % 2, 0:keys]
                dve.wait_ge(sem("sb_sig"), 2 * n + 2)
                dve.tensor_tensor(beta[:, b * P:], beta[:, b * P:], past, ALU.mult).then_inc(sem("sb_masked"), 1)
                dve.tensor_tensor(keep[:, b * P:], keep[:, b * P:], npast, ALU.max).then_inc(sem("sb_masked"), 1)
                dve.wait_ge(sem("sb_masked"), 2 * n + 2)
                dve.tensor_tensor_scan(prod[:, ::-1], keep[:, ::-1], keep[:, ::-1], 1.0, ALU.mult, ALU.min).then_inc(sem("sb_scan"), 1)
                dve.wait_ge(sem("sb_scan"), n + 1)
                dve.tensor_tensor(beta[:, 0:keys - 1], beta[:, 0:keys - 1], prod[:, 1:keys], ALU.mult).then_inc(sem("sb_wgt"), 1)

            def sb_lo(n):
                b, hd = SB_STEPS[n]
                bank = 1 + 2 * (n // 4 % 2)
                dve.wait_ge(sem("sb_hi"), n // 4 + 1)
                dve.tensor_tensor(ra[:, 6:8, b * P:(b + 1) * P], gb[bank][:, 0:256].rearrange("p (c s) -> p c s", c=2),
                                  ra[:, 4:6, b * P:(b + 1) * P].bitcast(F32), ALU.subtract).then_inc(sem("sb_lo"), 1)

            past, npast = m_("past"), m_("npast")
            for n in range(len(SB_STEPS)):
                sb_weights(n)
                if n % 4 == 1 and n > 4:
                    sb_lo(n - 2)
            sb_lo(len(SB_STEPS) - 1)
            dve.wait_ge(sem("mod_copied"), 5)
            dve.tensor_tensor(mod[:, 16:48], mod[:, 16:48], par[:, PAR["b_ada"].start + 16:PAR["b_ada"].stop],
                              ALU.add).then_inc(sem("mod1"), 1)
            dve.wait_ge(sem("mod1"), 2)
            dve.scalar_tensor_tensor(a1[:, 8:16], mod[:, 32:40], 1.0, par[:, PAR["n2"]], ALU.add, ALU.mult).then_inc(sem("a1"), 1)
            dve.wait_ge(sem("a1"), 2)
            ab = abt[:].rearrange("p (b h) -> p b h", h=8)
            tkb = lambda k: tk[:, k, :].rearrange("p (b h) -> p b h", h=4)
            dve.wait_ge(sem("ab_turned"), 1)
            dve.tensor_copy(abt[:], mb[0][:, 0:64]).then_inc(sem("ab_read"), 1)
            dve.wait_ge(sem("ab_read"), 1)
            dve.tensor_tensor(sp_t[:, 0, :].rearrange("p (b h) -> p b h", h=4), ab[:, :, 0:4],
                              par[:, PAR["dtb"]].rearrange("p (o h) -> p o h", o=1).to_broadcast([P, NB, 4]), ALU.add).then_inc(sem("dt_y"), 1)
            dve.wait_ge(sem("dt_y"), 1)
            softplus(2, sp_t[:, 0, :], 32, sp_t[:, 6, :])
            dve.wait_ge(sem("ea"), 1)
            dve.scalar_tensor_tensor(tkb(0), sp_t[:, 6, :].rearrange("p (b h) -> p b h", h=4), -1.0,
                                     ea[:].rearrange("p (o h) -> p o h", o=1).to_broadcast([P, NB, 4]), ALU.mult,
                                     ALU.mult).then_inc(sem("tk_g"), 1)
            dve.wait_ge(sem("tk_act"), 4)
            dve.scalar_tensor_tensor(tk[:, 4, :], tk[:, 5, :], -1.0, tk[:, 1, :], ALU.mult, ALU.mult).then_inc(sem("tk_ready"), 1)
            dve.wait_ge(sem("tk_ready"), 1)

            with dve.Fori(0, NB) as i:
                v = i + 1
                base = i * ND
                ch = sem("block_steps")
                st = {"n": 0, "seen": 0}

                def did(ins):
                    ins.then_inc(ch, 1)
                    st["n"] += 1
                    return st["n"]

                def after(k):
                    if k > st["seen"]:
                        dve.wait_ge(ch, base + k)
                        st["seen"] = k

                def gated(job):
                    n, hf = divmod(job, 2)
                    dve.wait_ge(sem(f"gb{2 * hf}_read"), i * 2 + (27 + n))
                    dve.wait_ge(sem(f"gb{2 * hf + 1}_full"), i * 2 + (n + 1))
                    m_half = mix[:, hf * HALF:(hf + 1) * HALF]
                    if n == 0:
                        if hf == 0:
                            dve.wait_ge(sem("mix_stored"), i * 16)
                        dve.tensor_tensor(m_half, sig, gb[2 * hf + 1], ALU.mult).then_inc(sem("gated"), 1)
                    else:
                        k = did(dve.tensor_tensor(sig, sig, gb[2 * hf + 1], ALU.mult))
                        after(k)
                        dve.tensor_tensor(m_half, m_half, sig, ALU.add).then_inc(sem("gated"), 1)

                dve.wait_ge(sem("pblk_in"), i * 16 + 16)
                pm3 = t2(rw["pm"])
                cur, prev = pblk[:, 0:7, HALO:], pblk[:, 0:7, HALO - 1:HALO - 1 + P]
                k = did(dve.tensor_tensor(pm3, prev, cur, ALU.subtract))
                after(k)
                k = did(dve.tensor_tensor(pm3, pm3, over_t(PAR["rw_mu"].start, 7), ALU.mult))
                after(k)
                dve.tensor_tensor(pm3, pm3, cur, ALU.add).then_inc(done("rw_pm"), 1)
                dve.wait_ge(sem("rw_pm"), at("rw_pm", i))
                r_, k_, v_ = (rw["pm"][:, a_:a_ + 256] for a_ in (0, 256, 512))
                dve.tensor_tensor(t2(rw["kkr"]), t2(k_), over_t(PAR["rw_kk"].start, 2), ALU.mult).then_inc(done("rw_kkr"), 1)
                dve.wait_ge(sem("rw_sw"), at("rw_sw", i, 2))
                for t in range(2):
                    c = slice(t * P, (t + 1) * P)
                    dve.tensor_tensor_scan(rw["gs"][:, c], m_("reset"), rw["sw"][:, c], 0.0, ALU.mult, ALU.add).then_inc(done("rw_gs"), 1)
                dve.wait_ge(sem("rw_gs"), at("rw_gs", i, 2))
                dve.tensor_tensor(rw["gm"], rw["gs"], rw["sw"], ALU.subtract).then_inc(done("rw_gm"), 1)
                dve.wait_ge(sem("rw_sa"), at("rw_sa", i, 2))
                dve.wait_ge(sem("rw_p2"), at("rw_p2", i))
                k = did(dve.scalar_tensor_tensor(t2(rw["t1"]), t2(rw["sa"]), -1.0, over_t(PAR["rw_ka"].start, 2), ALU.add, ALU.mult))
                after(k)
                k2 = did(dve.scalar_tensor_tensor(rw["t1"], rw["t1"], 1.0, k_, ALU.add, ALU.mult))
                after(k2)
                k = did(dve.tensor_tensor(rw["bon"], r_, rw["t1"], ALU.mult))
                after(k)
                dve.tensor_tensor(t2(rw["bon"]), t2(rw["bon"]), over_t(PAR["rw_rk"].start, 2), ALU.mult).then_inc(done("rw_bonp"), 1)
                dve.wait_ge(sem("rw_rn"), at("rw_rn", i))
                kk = did(dve.tensor_tensor(rw["kkr"], rw["kkr"], rw["rn"], ALU.mult))
                dve.wait_ge(sem("rw_ex"), at("rw_ex", i, 3))
                ar = rw["ar"].rearrange("p (t w c) -> p t w c", t=2, w=2)
                dve.tensor_tensor(ar[:, :, 1, :], t2(r_), t2(rw["ex1"]), ALU.mult).then_inc(done("rw_ar"), 1)
                after(kk)
                dve.scalar_tensor_tensor(ar[:, :, 0, :], t2(rw["kkr"]), -1.0, t2(rw["ex0"]), ALU.mult, ALU.mult).then_inc(done("rw_ar"), 1)
                dve.tensor_tensor(rw["km"], rw["t1"], rw["exn"], ALU.mult).then_inc(done("rw_km"), 1)
                k = did(dve.tensor_tensor(rw["bm"], rw["kkr"], rw["sa"], ALU.mult))
                after(k)
                kb = did(dve.tensor_tensor(rw["bm"], rw["bm"], rw["exn"], ALU.mult))
                ends = rw["ex1"].rearrange("p (c s) -> p c s", s=CHUNK)[:, :, CHUNK - 1:CHUNK].to_broadcast([P, 4, CHUNK])
                c4 = lambda ap: ap.rearrange("p (c s) -> p c s", s=CHUNK)
                dve.wait_ge(sem("rw_km"), at("rw_km", i))
                dve.tensor_tensor(c4(rw["kt"]), c4(rw["km"]), ends, ALU.mult).then_inc(done("rw_tl"), 1)
                after(kb)
                dve.tensor_tensor(c4(rw["bt"]), c4(rw["bm"]), ends, ALU.mult).then_inc(done("rw_tl"), 1)
                dve.wait_ge(sem("rw_p3"), at("rw_p3", i))
                dve.tensor_tensor(rw["bon"], mb[2][:, 256:512], v_, ALU.mult).then_inc(done("rw_bon"), 1)
                both = lambda b0: mbank[:, b0:b0 + 2, :].rearrange("p b (h c) -> p b h c", c=256)
                eo = lambda ap: ap.rearrange("p (t e c) -> p e t c", t=2, e=2)
                eo_mask = lambda name: msk[:, M[name]:M[name] + 1, :].rearrange("p (e t) c -> p e t c", e=1).to_broadcast([P, 2, 2, P])
                dve.wait_ge(sem("rw_p6"), at("rw_p6", i))
                dve.tensor_tensor(eo(rw["akt"]), both(0)[:, :, :, 0:P], eo_mask("strict"), ALU.mult).then_inc(done("rw_akt"), 1)
                dve.tensor_tensor(eo(rw["rkt"]), both(0)[:, :, :, P:256], eo_mask("tri"), ALU.mult).then_inc(done("rw_akt"), 1)
                dve.wait_ge(sem("rw_p7"), at("rw_p7", i))
                dve.tensor_tensor(eo(rw["ltr"]), both(2)[:, :, :, 0:P], eo_mask("nstrict"), ALU.mult).then_inc(done("rw_ltr"), 1)
                dve.tensor_tensor(eo(rw["rbt"]), both(2)[:, :, :, P:256], eo_mask("tri"), ALU.mult).then_inc(done("rw_ltr"), 1)
                gated(0)

                dve.wait_ge(sem("rw_tokVA"), at("rw_tokVA", i))
                acc, tmp = t4(gd["acc"]), t4(gd["tmp"])
                cw = par[:, PAR["gdn_cw"]].rearrange("p (t j o) -> p t j o", j=4, o=1)
                tap = lambda j: (pblk[:, 7:13, j:j + P], cw[:, :, j, :].to_broadcast([P, 6, P]))
                k1 = did(dve.tensor_tensor(acc, *tap(0), ALU.mult))
                for j in range(1, 4):
                    k = did(dve.tensor_tensor(tmp, *tap(j), ALU.mult))
                    after(k)
                    ins = dve.tensor_tensor(acc, acc, tmp, ALU.add)
                    if j < 3:
                        k = did(ins)
                        after(k)
                    else:
                        ins.then_inc(done("gd_acc"), 1)
                dve.tensor_copy(tkc[:].rearrange("p (k h) -> p k h", h=4), tk[:, 0:5, bass.ds(i * 4, 4)]).then_inc(done("tkc"), 1)

                def first_blocks(nm, b_, bank, signal):
                    k0 = did(dve.tensor_tensor(t4(b_["TT"]), t4(b_["ltr"]), over4("lv1T"), ALU.mult))
                    dve.wait_ge(sem(signal), at(signal, i))
                    k1 = did(dve.tensor_tensor(t4(b_["T"]), t4(mb[bank]), over4("lv1"), ALU.mult))
                    after(k1)
                    did(dve.tensor_tensor(t4(b_["TT"]), over4("ident"), t4(b_["TT"]), ALU.subtract))
                    dve.wait_ge(ch, base + st["n"])
                    dve.tensor_tensor(t4(b_["T"]), over4("ident"), t4(b_["T"]), ALU.subtract).then_inc(done(f"{nm}_T"), 1)

                dve.wait_ge(sem("rw_tokBK"), at("rw_tokBK", i))
                dve.wait_ge(sem("rw_ltr"), at("rw_ltr", i, 2))
                first_blocks("rw", rw, 0, "rw_p8")
                dve.wait_ge(sem("gd_rn"), at("gd_rn", i))
                kbq = gd["kbq"].rearrange("p (t w c) -> p t w c", t=2, w=2)
                dve.tensor_tensor(gd["kn"], gd["acc"][:, 256:512], gd["rn"][:, 256:512], ALU.mult).then_inc(done("gd_kn"), 1)
                dve.scalar_tensor_tensor(kbq[:, :, 1, :], t2(gd["acc"][:, 0:256]), HEAD ** -0.5, t2(gd["rn"][:, 0:256]),
                                         ALU.mult, ALU.mult).then_inc(done("gd_kbq"), 1)
                per_head = lambda k, w: tkc[:, 4 * k:4 * k + 4].rearrange("p (h o) -> p h o", o=1).to_broadcast([P, 4, w])
                dve.wait_ge(sem("gd_g2"), at("gd_g2", i))
                k = did(dve.tensor_tensor(t4(gd["dt"]), t4(mb[2]), per_head(2, P), ALU.subtract))
                after(k)
                dve.tensor_tensor(t4(gd["dt"]), t4(gd["dt"]), over4("neg"), ALU.min).then_inc(done("gd_dtm"), 1)
                dve.wait_ge(sem("gd_g3"), at("gd_g3", i))
                dve.wait_ge(sem("gd_kn"), at("gd_kn", i))
                dve.wait_ge(sem("gd_eg"), at("gd_eg", i))
                dve.tensor_tensor(kbq[:, :, 0, :], t2(gd["kn"]), t2(mb[3][:, 256:512]), ALU.mult).then_inc(done("gd_kbq"), 1)
                dve.wait_ge(sem("gd_kbq"), at("gd_kbq", i, 2))
                kqd = did(dve.tensor_tensor(t2(gd["qd"]), kbq[:, :, 1, :], t2(gd["eg"]), ALU.mult))
                dve.wait_ge(sem("gd_g4"), at("gd_g4", i))
                dve.wait_ge(sem("gd_stored"), i * 16)
                h64 = lambda ap: ap.rearrange("p (h c) -> p h c", c=64)
                dve.tensor_tensor(h64(gd["vb"]), h64(mb[1][:, 256:512]), per_head(1, 64), ALU.mult).then_inc(done("gd_tok"), 1)
                dve.tensor_tensor(h64(gd["kbe"]), h64(mb[1][:, 0:256]), per_head(4, 64), ALU.mult).then_inc(done("gd_tok"), 1)
                dve.tensor_tensor(h64(gd["kd"]), h64(mb[1][:, 0:256]), per_head(3, 64), ALU.mult).then_inc(done("gd_tok"), 1)
                gated(1)
                dve.wait_ge(sem("gd_g5"), at("gd_g5", i))
                dve.wait_ge(sem("gd_dt"), at("gd_dt", i))
                k = did(dve.tensor_tensor(eo(gd["ltr"]), both(2)[:, :, :, 0:P], eo(gd["dt"]), ALU.mult))
                after(k)
                dve.tensor_tensor(t4(gd["ltr"]), t4(gd["ltr"]), over4("strict"), ALU.mult).then_inc(done("gd_ltr"), 1)
                dve.tensor_tensor(eo(gd["qkt"]), both(2)[:, :, :, P:256], eo(gd["dt"]), ALU.mult).then_inc(done("gd_qkt"), 1)
                dve.wait_ge(sem("gd_qkt"), at("gd_qkt", i))
                first_blocks("gd", gd, 1, "gd_g6")

                for lv in range(5):
                    for nm, b_, bank in (("rw", rw, 0), ("gd", gd, 3)):
                        dve.wait_ge(sem(f"{nm}_Y"), at(f"{nm}_Y", i, lv + 1))
                        dve.tensor_tensor(t4(b_["Y"]), t4(mb[bank]), over4(f"lv{2 << lv}"), ALU.mult).then_inc(done(f"{nm}_Ym"), 1)
                    for nm, b_, bank in (("rw", rw, 0), ("gd", gd, 3)):
                        if lv < 4:
                            dve.wait_ge(sem(f"{nm}_Z"), at(f"{nm}_Z", i, 2 * lv + 1))
                            dve.tensor_tensor(b_["T"], b_["T"], mb[1], ALU.subtract).then_inc(done(f"{nm}_T"), 1)
                        dve.wait_ge(sem(f"{nm}_Z"), at(f"{nm}_Z", i, (2 * lv + (2 if lv < 4 else 1))))
                        dve.tensor_tensor(b_["TT"], b_["TT"], mb[2], ALU.subtract).then_inc(done(f"{nm}_T"), 1)
                gated(2)

                for par_ in range(2):
                    R = slice(64 * par_, 64 * par_ + 64)
                    for nm, b_, ws in (("rw", rw, 0), ("gd", gd, 256)):
                        if par_ == 0:
                            dve.wait_ge(sem(f"{nm}_uw"), at(f"{nm}_uw", i))
                        dve.wait_ge(sem("gd_ws"), at("gd_ws", i, par_ + 1))
                        dve.tensor_tensor(b_["u"][R, :], b_["uw"][R, 0:256], mb[0][R, ws:ws + 256], ALU.add).then_inc(done(f"{nm}_u"), 1)
                    for nm, b_, st_, sc, dec in (("rw", rw, 0, 1, "ex1"), ("gd", gd, 1, 0, "eg")):
                        dve.wait_ge(sem(f"{nm}_s"), at(f"{nm}_s", i, par_ + 1))
                        for t in range(2):
                            for r in (0, 64):
                                e_ = t * P + 64 * par_ + 63
                                dve.scalar_tensor_tensor(state[r:r + 64, st_, t, r:r + 64], state[r:r + 64, st_, t, r:r + 64],
                                                         b_[dec][r:r + 64, e_:e_ + 1],
                                                         mb[sc][r:r + 64, t * P + r:t * P + r + 64], ALU.mult,
                                                         ALU.add).then_inc(done(f"{nm}_S"), 1)

                dve.wait_ge(sem("rw_m1"), at("rw_m1", i))
                dve.scalar_tensor_tensor(rw["yc"], mb[0][:, 0:256], -1.0 / HEAD, rw["y"], ALU.mult, ALU.add).then_inc(done("rw_yc"), 1)
                dve.wait_ge(sem("gd_rno"), at("gd_rno", i))
                k = did(dve.scalar_tensor_tensor(gd["o"], mb[3][:, 0:256], pc("gdn_ng"), gd["rno"], ALU.mult, ALU.mult))
                after(k)
                dve.tensor_tensor(gd["o"], gd["o"], gd["z"], ALU.mult).then_inc(done("gd_o"), 1)
                gated(3)
                dve.wait_ge(sem("rw_rno"), at("rw_rno", i))
                k = did(dve.tensor_tensor(rw["yc"], rw["yc"], rw["u"], ALU.mult))
                after(k)
                for t in range(2):
                    c = slice(t * P, (t + 1) * P)
                    k = did(dve.tensor_scalar(rw["yc"][:, c], rw["yc"][:, c], pc("rw_lng", t), pc("rw_lnb", t), ALU.mult, ALU.add))
                after(k)
                k = did(dve.tensor_tensor(rw["yc"], rw["yc"], rw["bon"], ALU.add))
                after(k)
                dve.wait_ge(sem("rw_stored"), i * 16)
                dve.tensor_tensor(rw["o"], rw["yc"], rw["gate"], ALU.mult).then_inc(done("rw_o"), 1)
                assert st["n"] == ND, st

            dve.wait_ge(sem("o_in"), 16)
            for n in range(2):
                dve.wait_ge(sem("o_hi"), n + 1)
                dve.tensor_tensor(ra[:, 4 * n + 2:4 * n + 4], fa[:, 8 + 2 * n:10 + 2 * n, :],
                                  ra[:, 4 * n:4 * n + 2].bitcast(F32), ALU.subtract).then_inc(sem("o_lo"), 1)
            dve.wait_ge(sem("mix_in"), 16)
            with dve.Fori(0, KT) as i:
                for job in range(4):
                    n, hf = divmod(job, 2)
                    dve.wait_ge(sem(f"gb{2 * hf}_read"), i * 2 + (U_MIX2 + 1 + n))
                    dve.wait_ge(sem(f"gb{2 * hf + 1}_full"), i * 2 + (2 * NB + 1 + n))
                    dve.tensor_tensor(sig4[job], sig4[job], gb[2 * hf + 1], ALU.mult).then_inc(sem("weighed"), 1)
                    dve.wait_ge(sem("weighed"), i * 4 + (job + 1))
                    dve.wait_ge(sem("gated"), i * 4 + (4 * NB - 1 + job))
                    m_half = fa[:, bass.ds(i, 1), hf * HALF:(hf + 1) * HALF]
                    dve.tensor_tensor(m_half, m_half, sig4[job].rearrange("p (o c) -> p o c", o=1), ALU.add).then_inc(sem("gated"), 1)
            dve.wait_ge(sem("gated"), 8 * NB)
            for k in range(KT):
                dve.wait_ge(sem("mixed_hi"), k + 1)
                dve.tensor_tensor(h_lo[:, k, :], fa[:, k, :], h_hi[:, k, :].bitcast(F32), ALU.subtract).then_inc(sem("mixed_lo"), 1)

            def add_squares(m, par_, nth):
                dve.wait_ge(sem("sq"), (1 + nth) * KT + m + 1)
                if m > 1:
                    dve.wait_ge(sem("sq_added"), m - 1 + 7 * nth)
                dve.tensor_tensor(fa[:, ACC, :], fa[:, ACC, :], fa[:, SQ + par_, :], ALU.add).then_inc(sem("sq_added"), 1)

            for m in range(KT):
                dve.wait_ge(sem(f"x_in{m}"), 32)
                for hf in range(2):
                    dve.wait_ge(sem("half_done"), 2 * m + hf + 1)
                    c = slice(hf * HALF, (hf + 1) * HALF)
                    dve.scalar_tensor_tensor(fa[:, m, c], gb[2 * hf + m % 2], mod[:, 16 + m:17 + m], fa[:, m, c],
                                             ALU.mult, ALU.add).then_inc(sem("x1"), 1)
                if m >= 2:
                    add_squares(m - 1, (m - 1) % 2, 0)
            add_squares(KT - 1, (KT - 1) % 2, 0)
            for s_ in range(2):
                dve.tensor_copy(G[s_][:, 0:2], zero[:, 0:2]).then_inc(sem("g_halo"), 1)
            dve.wait_ge(sem("rstd"), 1)

            def h2_lo(k):
                dve.wait_ge(sem("h_hi"), KT + k + 1)
                dve.tensor_tensor(h_lo[:, k, :], fa[:, 12 + k % 4, :], h_hi[:, k, :].bitcast(F32), ALU.subtract).then_inc(sem("h_done"), 1)

            for k in range(KT):
                dve.tensor_tensor(fa[:, 12 + k % 4, :], fa[:, k, :], fa[:, RSTD, :], ALU.mult).then_inc(sem("h_norm"), 1)
                dve.wait_ge(sem("h_norm"), KT + k + 1)
                dve.tensor_scalar(fa[:, 12 + k % 4, :], fa[:, 12 + k % 4, :], a1[:, 8 + k:9 + k], mod[:, 24 + k:25 + k],
                                  ALU.mult, ALU.add).then_inc(sem("h_f32"), 1)
                if k >= 1:
                    h2_lo(k - 1)
            h2_lo(KT - 1)

            def ffn_dve(t, s_, up_half, cw):
                dve.wait_ge(sem("gate_read"), t * 2 + 2)
                dve.tensor_scalar(C[s_], G[s_][:, 2:2 + S], cw[2], None, ALU.mult).then_inc(sem("conv_steps"), 1)
                dve.wait_ge(sem("conv_steps"), t * 2 + 1)
                dve.scalar_tensor_tensor(C[s_], G[s_][:, 1:1 + S], cw[1], C[s_], ALU.mult, ALU.add).then_inc(sem("conv_steps"), 1)
                dve.wait_ge(sem("conv_steps"), t * 2 + 2)
                dve.scalar_tensor_tensor(C[s_], G[s_][:, 0:S], cw[0], C[s_], ALU.mult, ALU.add).then_inc(sem("conv"), 1)
                dve.wait_ge(sem("gelu"), t + 1)
                for hf in range(2):
                    c = slice(hf * HALF, (hf + 1) * HALF)
                    dve.wait_ge(sem("half_done"), up_half + (hf - 1))
                    dve.tensor_tensor(fa[:, 13 + s_, c], C[s_][:, c], gb[2 * hf + 1], ALU.mult).then_inc(sem("up_read"), 1)

            def ffn_lo(t, s_, j):
                dve.wait_ge(sem("act_hi"), t + 1)
                dve.tensor_tensor(ra[:, GT + j, :], fa[:, 13 + s_, :], ra[:, j, :].bitcast(F32), ALU.subtract).then_inc(sem("act_lo"), 1)

            def down_add(m, bank, count):
                dve.wait_ge(sem("half_done"), count)
                dve.scalar_tensor_tensor(fa[:, m, :], mbank[:, bank:bank + 2, :].rearrange("p b s -> p (b s)"),
                                         mod[:, 40 + m:41 + m], fa[:, m, :], ALU.mult, ALU.add).then_inc(sem("down_read"), 1)

            cw0 = PAR["ffn_cw"].start
            taps = lambda t: [par[:, cw0 + 3 * t + j:cw0 + 3 * t + j + 1] for j in range(3)]
            ffn_dve(0, 0, 2 * KT + 4, taps(0))
            ffn_lo(0, 0, 0)
            with dve.Fori(0, NG) as g:
                dve.tensor_copy(cwc[:], par[:, bass.ds(g * (3 * GT) + (cw0 + 3), 3 * GT)]).then_inc(sem("cwc"), 1)
                dve.wait_ge(sem("cwc"), g + 1)
                for q in range(GT):
                    t, u = g * GT + (1 + q), 2 * (2 + 2 * q) + 2 * KT
                    ffn_dve(t, (1 + q) % 2, g * (2 * UG) + (u + 4), [cwc[:, 3 * q + j:3 * q + j + 1] for j in range(3)])
                    if q < GT - 1:
                        ffn_lo(t, (1 + q) % 2, 1 + q)
                for m in range(KT):
                    down_add(m, 2 * (m % 2), g * (2 * UG) + (2 * KT + 4 + 4 * GT + m + 1))
                ffn_lo(g * GT + GT, 0, 0)
            ffn_dve(FT - 1, 1, 2 * (UNITS - U_OUT) - 4, taps(FT - 1))
            ffn_lo(FT - 1, 1, 1)
            for m in range(KT):
                down_add(m, 2 * (m % 2), 2 * (UNITS - U_OUT) - 3 + m // 2)
                if m >= 2:
                    add_squares(m - 1, (m - 1) % 2, 1)
            add_squares(KT - 1, (KT - 1) % 2, 1)
            dve.wait_ge(sem("rstd"), 2)
            for k in range(KT):
                dve.scalar_tensor_tensor(fa[:, k, :], fa[:, k, :], pc("nf", k), fa[:, RSTD, :], ALU.mult,
                                         ALU.mult).then_inc(sem("out_done"), 1)


def host_layout(x):
    f = lambda v: np.ascontiguousarray(v)
    cols = lambda v: v.reshape(-1, P).T

    def tiles(w):
        k, n = w.shape
        return w.reshape(k // P, P, n // P, P).transpose(2, 1, 0, 3).reshape(n // P, P, k)

    t = {}
    t["xT"] = f(x["x"][0].T).reshape(KT, P, S)
    t["c"] = f(x["c"])
    t["w_ada"] = f(x["w_ada"][0].T).reshape(48, P, D)
    w = x["w_in"][0]
    lru, sbw, gdn, rw = w[:, :512], w[:, 512:1280], w[:, 1280:2312], w[:, 2312:]
    ab = np.zeros((D, P), np.float32)
    ab[:, :8] = gdn[:, 1024:]
    t["w_in"] = f(tiles(np.concatenate([lru, sbw, rw, gdn[:, :1024], ab], axis=1)))
    wg, wb = x["w_gate"][0], x["w_branch"][0]
    pairs = np.concatenate([np.stack([tiles(wg[n]) for n in range(4)]),
                            np.stack([tiles(wb[n]) for n in range(4)])], axis=3)
    t["w_mix"] = f(pairs.reshape(2, 2, KT, P, W_COLS).transpose(0, 2, 1, 3, 4).reshape(4 * KT, P, W_COLS))
    gate, up = tiles(x["ffn_w_gate"][0]), tiles(x["ffn_w_up"][0])
    down = tiles(x["ffn_w_down"][0])

    def downs(g, ks):
        w = down[:, :, g * GT * P:(g * GT + ks) * P]
        return list(w.reshape(ks, KT // ks, P, ks * P).transpose(0, 2, 1, 3).reshape(ks, P, KT * P))

    units = list(tiles(x["w_out"][0])) + [gate[0], up[0]]
    for g in range(NG):
        for q in range(GT):
            units += [gate[g * GT + 1 + q], up[g * GT + 1 + q]]
        units += downs(g, GT)
    units += [gate[FT - 1], up[FT - 1]] + downs(NG, FT - NG * GT)
    t["w_tail"] = f(np.stack(units))
    conv = lambda v, n: v[0].reshape(v.shape[1], n, P).transpose(2, 1, 0).reshape(P, -1)
    bcast = lambda v: np.broadcast_to(v.reshape(1, -1), (P, v.size))
    vals = {"n1": cols(x["norm1_g"]), "n2": cols(x["norm2_g"]), "nf": cols(x["final_g"]), "b_ada": cols(x["b_ada"]),
            "lru_cw": conv(x["lru_conv_w"], 2), "lru_cb": cols(x["lru_conv_b"]), "lru_br": cols(x["lru_b_r"]),
            "lru_bi": cols(x["lru_b_i"]), "lru_lam": cols(x["lru_lambda"]), "gdn_cw": conv(x["gdn_conv_w"], 6),
            "rw_mu": cols(x["rw_mu"]), "rw_w0": cols(x["rw_w0"]), "rw_a0": cols(x["rw_a0"]), "rw_kk": cols(x["rw_k_k"]),
            "rw_ka": cols(x["rw_k_a"]), "rw_rk": cols(x["rw_r_k"]), "rw_lng": cols(x["rw_ln_g"]),
            "rw_lnb": cols(x["rw_ln_b"]), "b_gate": cols(x["b_gate"]), "ffn_cw": conv(x["ffn_conv_w"], FT),
            "gdn_ng": np.concatenate([x["gdn_norm_g"][0]] * 2)[:, None], "alog": bcast(x["gdn_a_log"]),
            "dtb": bcast(x["gdn_dt_bias"])}
    t["par"] = f(np.concatenate([vals[n] for n in PAR], axis=1))
    t["masks"] = mask_table()
    t["lru_w"] = f(np.stack([x["lru_w_r"][0], x["lru_w_i"][0]]))
    t["lora"] = f(np.concatenate([x["rw_w_up"][0], x["rw_a_up"][0], x["rw_g_up"][0]], axis=0))
    return t


def kernel(**inputs):
    import concourse.bacc as bacc
    from concourse.bass_utils import run_bass_kernel_spmd

    arrays = host_layout({name: np.asarray(v) for name, v in inputs.items()})
    nc = bacc.Bacc("TRN2", target_bir_lowering=False, num_devices=1, dynamic_dma_scratch_size=1024)
    aps = {name: nc.dram_tensor("in_" + name, v.shape, mybir.dt.from_np(v.dtype), kind="ExternalInput").ap()
           for name, v in arrays.items()}
    out = nc.dram_tensor("out_0", (KT, P, S), F32, kind="ExternalOutput").ap()
    program(nc, aps, out)
    r = run_bass_kernel_spmd(nc, [{"in_" + name: v for name, v in arrays.items()}], core_ids=[0])
    return np.ascontiguousarray(r.results[0]["out_0"].reshape(D, S).T).reshape(1, S, D)
```

```python
from contextlib import ExitStack

import numpy as np

import concourse.bass as bass
from concourse import mybir

F32 = mybir.dt.float32
F32R = mybir.dt.float32r
ALU = mybir.AluOpType
ACT = mybir.ActivationFunctionType

P = 128
D = 1024
S = 1024
KT = D // P
HALF = 512
NB = S // P
EPS = 1e-6
RW_LN_EPS = 64e-5
HEAD = 64
CHUNK = 64
W_COLS = 10 * P
FFN = 2816
FT = FFN // P
GT = 4
NG = FT // GT
UG = 2 * GT + 4
U_MIX, U_BR, U_OUT, U_FFN = 26, 58, 62, 70
UNITS = U_FFN + 2 * FT + 4 * NG + 2
RW_T, GDN_T = 7, 8
P_TILES = RW_T + GDN_T
HALO = 3
BLK = P + HALO
SB_STEPS = [(b, hd) for b in reversed(range(NB)) for hd in range(4)]
JOBS_AHEAD = 8
LRU_JOBS = [range(0, 2), range(2, 5), range(5, JOBS_AHEAD)]
ND = 30
FILL = [48, 72, 80, 96, 130, 138, 166, 174, 186, 200, 210]
FILL_L, FILL_Y, FILL_Z = 120, 2, 1
E_HALF = float(np.exp(-0.5))

_INV_Z = ["rw_Z", "rw_Z", "gd_Z", "gd_Z"]
EVENTS = {
    "products": (["rw_p1", "rw_p2", "rw_p3", "rw_p4", "rw_p6", "rw_p5", "rw_p7", "rw_p8", "rw_r1"]
                 + ["gd_g1", "gd_g2", "gd_g3", "gd_g4", "gd_g5", "gd_g6"]
                 + (["rw_Y", "gd_Y"] + _INV_Z) * 4 + ["rw_Y", "gd_Y", "rw_Z", "gd_Z", "rw_r3", "gd_r3"]
                 + ["rw_ws", "gd_ws", "rw_s", "rw_Yd", "gd_s", "gd_Yd"] * 2 + ["rw_m1", "gd_m", "rw_m2"]),
    "functions": (["rw_lt"] * 3 + ["rw_sq", "rw_sw", "rw_sw", "rw_sa", "rw_sa", "rw_gate", "rw_ln", "rw_rn"]
                  + ["rw_ex"] * 3 + ["rw_tokVA", "rw_tokBK", "gd_silu", "pblk_read", "gd_sq", "gd_gbc", "gd_gbc"]
                  + ["rw_x", "gd_ln", "gd_rn", "gd_dt", "gd_eg", "rw_uw", "gd_uw", "rw_y", "gd_y2", "gd_lno", "gd_rno"]
                  + ["rw_y2", "rw_lno", "rw_rno"]),
    "values": (["rw_pm", "rw_kkr", "rw_gs", "rw_gs", "rw_gm", "rw_bonp", "rw_ar", "rw_ar", "rw_km", "rw_tl", "rw_tl"]
               + ["rw_bon", "rw_akt", "rw_akt", "rw_ltr", "rw_ltr", "gd_acc", "tkc", "rw_T", "gd_kn", "gd_kbq"]
               + ["gd_dtm", "gd_kbq", "gd_tok", "gd_tok", "gd_tok", "gd_ltr", "gd_qkt", "gd_T"]
               + ["rw_Ym", "gd_Ym", "rw_T", "rw_T", "gd_T", "gd_T"] * 4 + ["rw_Ym", "gd_Ym", "rw_T", "gd_T"]
               + (["rw_u", "gd_u"] + ["rw_S"] * 4 + ["gd_S"] * 4) * 2 + ["rw_yc", "gd_o", "rw_o"]),
}

PAR = {}
_n = 0
for _name, _w in (("n1", 8), ("n2", 8), ("nf", 8), ("b_ada", 48), ("lru_cw", 8), ("lru_cb", 2), ("lru_br", 2),
                  ("lru_bi", 2), ("lru_lam", 2), ("gdn_cw", 24), ("rw_mu", 7), ("rw_w0", 2), ("rw_a0", 2),
                  ("rw_kk", 2), ("rw_ka", 2), ("rw_rk", 2), ("rw_lng", 2), ("rw_lnb", 2), ("b_gate", 32),
                  ("ffn_cw", 66), ("gdn_ng", 1), ("alog", 4), ("dtb", 4)):
    PAR[_name] = slice(_n, _n + _w)
    _n += _w
NPAR = _n

MASKS = ["ident", "tri", "strict", "nstrict", "neg", "suffix", "bd", "lv1", "lv1T", "lv2", "lv4", "lv8", "lv16",
         "lv32", "reset", "ones", "past", "npast"]
M = {n: i for i, n in enumerate(MASKS)}


def mask_table():
    r = np.arange(P)[:, None]
    c = np.arange(P)[None, :]
    same = (r // CHUNK) == (c // CHUNK)
    t = {"ident": r == c, "tri": same & (c >= r), "strict": same & (c > r), "suffix": same & (r > c),
         "bd": (r // HEAD) == (c // HEAD), "ones": (r >= 0) & (c >= 0),
         "past": c < r, "npast": c >= r, "reset": (r >= 0) & (c % CHUNK != 0)}
    for s in (1, 2, 4, 8, 16, 32):
        t[f"lv{s}"] = (r // (2 * s) == c // (2 * s)) & (r % (2 * s) >= s) & (c % (2 * s) < s)
    t["lv1T"] = t["lv1"].T
    out = {k: v.astype(np.float32) for k, v in t.items()}
    out["nstrict"] = -out["strict"]
    out["neg"] = np.where(t["tri"], 0.0, -1e30).astype(np.float32)
    return np.stack([out[n] for n in MASKS], axis=1).reshape(P, len(MASKS) * P)


def program(nc, a, out):
    ctx = ExitStack()
    with ctx:
        def sb(name, shape, dt=F32):
            return ctx.enter_context(nc.sbuf_tensor(name, shape, dt))

        sems = {}
        group_of = {label: group for group, labels in EVENTS.items() for label in labels}
        emitted = {group: [] for group in EVENTS}

        def sem(name):
            name = group_of.get(name, name)
            if name not in sems:
                sems[name] = ctx.enter_context(nc.semaphore(name))
            return sems[name]

        def done(label):
            assert label == EVENTS[group_of[label]][len(emitted[group_of[label]])], label
            emitted[group_of[label]].append(label)
            return sem(label)

        def at(label, i, nth=None):
            events = EVENTS[group_of[label]]
            if isinstance(nth, int) and nth == 0:
                return i * len(events) + 1
            places = [n for n, e in enumerate(events) if e == label]
            return i * len(events) + (places[-1 if nth is None else nth - 1] + 2)

        w_raw = sb("w_raw", [P, 2, W_COLS])
        w_hi = sb("w_hi", [P, 2, W_COLS], F32R)
        w_lo = sb("w_lo", [P, 2, W_COLS], F32R)
        h_hi = sb("h_hi", [P, KT, S], F32R)
        h_lo = sb("h_lo", [P, KT, S], F32R)
        ra = sb("ra", [P, 8, S], F32R)
        fa = sb("fa", [P, 20, S])
        msk = sb("msk", [P, len(MASKS), P])
        par = sb("par", [P, NPAR])
        mod = sb("mod", [P, 48])
        mod6 = sb("mod6", [P, 6])
        a1 = sb("a1", [P, 16])
        sl = sb("sl", [P, 4])
        lora = sb("lora", [P, 6, P])
        state = sb("state", [P, 2, 2, P])
        tk = sb("tk", [P, 6, 32])
        abt = sb("abt", [P, 64])
        ea = sb("ea", [P, 4])
        tkc = sb("tkc", [P, 20])
        bgc = sb("bgc", [P, 2])
        cwc = sb("cwc", [P, 3 * GT])
        zero = sb("zero", [P, 48])
        eps = sb("eps", [P, 2])
        lru_w = fa[:, 16, 0:4 * P].rearrange("p (n c) -> p n c", c=P)
        sp_t = fa[:, 17, 0:256].rearrange("p (k c) -> p k c", c=32)
        gbank = ctx.enter_context(nc.psum_tensor("gbank", [P, 4, HALF], F32))
        mbank = ctx.enter_context(nc.psum_tensor("mbank", [P, 4, HALF], F32))
        gb = [gbank[:, i, :] for i in range(4)]
        mb = [mbank[:, i, :] for i in range(4)]

        p_scr = nc.dram_tensor("p_scr", (P_TILES, P, HALO + S), F32, kind="Internal").ap()

        def m_(name):
            return msk[:, M[name], :]

        def pc(name, j=0):
            b = PAR[name].start + j
            return par[:, b:b + 1]

        mix_scr = nc.dram_tensor("mix_scr", (KT, P, S), F32, kind="Internal").ap()
        sig_scr = nc.dram_tensor("sig_scr", (KT, 2, P, S), F32, kind="Internal").ap()
        o_scr = nc.dram_tensor("o_scr", (4, P, S), F32, kind="Internal").ap()

        flat = fa[:].rearrange("p t s -> p (t s)")
        used = [0]
        names = {}

        def room(name, cols, like=None):
            if like is None:
                names[name] = flat[:, used[0]:used[0] + cols]
                used[0] += cols
                assert used[0] <= 20 * S, used
            else:
                names[name] = like[:, 0:cols]
            return names[name]

        pblk = room("pblk", P_TILES * BLK).rearrange("p (t c) -> p t c", c=BLK)
        sig, sig_out, mix = room("sig", HALF), room("sig_out", HALF), room("mix", S)
        X = room("X", 3328)
        xo = [0]

        def xroom(cols):
            xo[0] += cols
            assert xo[0] <= 3328, xo
            return X[:, xo[0] - cols:xo[0]]

        rw = {}
        for n_, c_ in (("pm", 7 * P), ("sw", 256), ("gs", 256), ("gm", 256), ("ex0", 256), ("exn", 256), ("sa", 256),
                       ("kkr", 256), ("t1", 256), ("rn", 256), ("lt", P)):
            rw[n_] = xroom(c_)
        for n_, c_ in (("ex1", 256), ("gate", 256), ("ar", 512), ("bm", 256), ("km", 256), ("tokVA", 512),
                       ("tokBK", 512), ("ltr", 512), ("akt", 512), ("rbt", 512), ("rkt", 512), ("T", 512), ("TT", 512),
                       ("Y", 512), ("uw", 512), ("u", 256), ("x", 256), ("bon", 256)):
            rw[n_] = room("rw_" + n_, c_)
        rw["bt"], rw["kt"] = rw["T"][:, 0:256], rw["T"][:, 256:512]
        rw["y"], rw["yc"], rw["y2"] = rw["x"], rw["uw"][:, 0:256], rw["uw"][:, 256:512]
        rw["o"] = rw["yc"]
        xo[0] = 0
        gd = {}
        for n_, c_ in (("acc", 768), ("tmp", 768), ("sq", 512), ("rn", 512), ("kbc", 0)):
            gd[n_] = xroom(c_)
        for n_, c_ in (("z", 256), ("kn", 256), ("kbq", 512), ("qd", 256), ("eg", 256), ("vb", 256), ("kbe", 256),
                       ("kd", 256), ("ltr", 512), ("qkt", 512), ("T", 512), ("TT", 512), ("Y", 512), ("uw", 512),
                       ("u", 256)):
            gd[n_] = room("gd_" + n_, c_)
        gd["gbc"], gd["dt"], gd["bb"] = gd["Y"], gd["T"], gd["uw"]
        gd["o"], gd["y2"], gd["rno"] = gd["vb"], gd["kbe"], gd["kd"]

        def t2(ap):
            return ap.rearrange("p (t c) -> p t c", c=P)

        def t4(ap):
            return ap.rearrange("p (t c) -> p t c", c=P)

        def over4(name):
            return msk[:, M[name]:M[name] + 1, :].to_broadcast([P, 4, P])

        def over_t(col, n, w=P):
            return par[:, col:col + n].rearrange("p (t o) -> p t o", o=1).to_broadcast([P, n, w])

        vtok = fa[:, 10:12, :].rearrange("p t s -> p (t s)")

        SQ, ACC, RSTD = 16, 18, 19
        G = [flat[:, 8 * S + s_ * (S + 2):8 * S + (s_ + 1) * (S + 2)] for s_ in range(2)]
        C = [fa[:, 11, :], fa[:, 15, :]]

        block = ctx.enter_context(nc.Block())

        @block.sync
        def _(sp):
            def unit(name, row, slot, u, cols=KT * P):
                if not (isinstance(u, int) and u < 2):
                    sp.wait_ge(sem("w_split"), u - 1)
                sp.dma_start(w_raw[:, slot, 0:cols], a[name][row]).then_inc(sem(f"w_in{slot}"), 16)

            sp.dma_start(fa[:, 11, :], a["c"].to_broadcast([P, D])).then_inc(sem("c_in"), 16)
            for k in range(KT):
                sp.dma_start(fa[:, k, :], a["xT"][k]).then_inc(sem(f"x_in{k}"), 16)
                if k == 2:
                    sp.dma_start(msk[:].rearrange("p m c -> p (m c)"), a["masks"]).then_inc(sem("msk_in"), 16)
            unit("w_in", 0, 0, 0)
            for t in range(18):
                if t >= 3:
                    sp.wait_ge(sem("ada_used"), t - 2)
                sp.dma_start(fa[:, 12 + t % 3, :], a["w_ada"][t]).then_inc(sem(f"ada_in{t % 3}"), 16)
                if t == 10:
                    sp.dma_start(par[:], a["par"]).then_inc(sem("par_in"), 16)
                    unit("w_in", 1, 1, 1)
            sp.wait_ge(sem("zero_set"), 6)
            for g in range(2):
                for r in range(2):
                    sp.dma_start(lru_w[64 * r:64 * r + 64, 2 * g:2 * g + 2, 64 * r:64 * r + 64],
                                 a["lru_w"][g, r::2].rearrange("n e f -> e n f")).then_inc(sem("lru_w_in"), 16)
            for t in range(2):
                cols = slice(t * P, (t + 1) * P)
                sp.dma_start(lora[0:32, t, :], a["lora"][0:32, cols]).then_inc(sem("lora_in"), 16)
                sp.dma_start(lora[32:64, 2 + t, :], a["lora"][32:64, cols]).then_inc(sem("lora_in"), 16)
                sp.dma_start(lora[64:128, 4 + t, :], a["lora"][64:128, cols]).then_inc(sem("lora_in"), 16)
            for nm, t0, t1 in (("block", 0, RW_T), ("sig", RW_T, P_TILES)):
                sp.dma_start(p_scr[t0:t1, :, 0:HALO].rearrange("t p c -> p t c"),
                             zero[:, 0:(t1 - t0) * HALO].rearrange("p (t c) -> p t c", c=HALO)).then_inc(sem(f"{nm}_stored"), 16)
            with sp.Fori(0, 4) as i:
                for s in range(2):
                    unit("w_in", i * 2 + (2 + s), s, i * 2 + (2 + s))
                for t in range(6):
                    sp.wait_ge(sem("ada_used"), i * 6 + (t + 16))
                    sp.dma_start(fa[:, 12 + t % 3, :], a["w_ada"][i * 6 + (18 + t)]).then_inc(sem(f"ada_in{t % 3}"), 16)
            for t in range(42, 48):
                sp.wait_ge(sem("ada_used"), t - 2)
                sp.dma_start(fa[:, 12 + t % 3, :], a["w_ada"][t]).then_inc(sem(f"ada_in{t % 3}"), 16)
            for u in range(10, 26):
                unit("w_in", u, u % 2, u)
            for n in range(2):
                unit("w_mix", n, n, U_MIX + n, W_COLS)
            sp.wait_ge(sem("p_out0"), 16 * 16)
            sp.wait_ge(sem("p_out1"), 14 * 16)
            sp.wait_ge(sem("sig_stored"), 16)
            sp.wait_ge(sem("sb_lo"), 8)
            sp.wait_ge(sem("ab_read"), 1)

            def block_in(i):
                sp.wait_ge(sem("block_stored"), 16)
                sp.dma_start(pblk, p_scr[:, :, bass.ds(i * P, BLK)].rearrange("t p c -> p t c")).then_inc(sem("pblk_in"), 16)

            def block_out(i):
                sp.wait_ge(sem("gated"), i * 4 + 4)
                sp.wait_ge(sem("rw_o"), at("rw_o", i))
                sp.dma_start(mix_scr[bass.ds(i, 1)].rearrange("t p c -> p (t c)"), mix).then_inc(sem("block_stored"), 16)
                for o_, t in ((rw["o"], 2), (gd["o"], 0)):
                    sp.dma_start(o_scr[t:t + 2, :, bass.ds(i * P, P)].rearrange("t p c -> p t c"), t2(o_)).then_inc(sem("block_stored"), 16)

            block_in(0)
            with sp.Fori(0, NB - 1) as i:
                for n in range(2):
                    unit("w_gate", i * 2 + n, n, i * 4 + (U_MIX + 2 + n))
                sp.wait_ge(sem("pblk_read"), at("pblk_read", i))
                block_in(i + 1)
                for n in range(2):
                    unit("w_mix", i * 2 + (2 + n), n, i * 4 + (U_MIX + 4 + n), W_COLS)
                block_out(i)
            for n in range(2):
                unit("w_gate", 2 * NB - 2 + n, n, U_BR - 2 + n)
            for n in range(2):
                unit("w_branch", n, n, U_BR + n)
            block_out(NB - 1)

            sp.wait_ge(sem("gated"), 4 * NB)
            sp.wait_ge(sem("block_stored"), 16 + 48 * NB)
            sp.wait_ge(sem("sig_stored"), 16 + 64 * NB)
            sp.wait_ge(sem("rw_o"), at("rw_o", NB - 1))
            for n in range(2):
                sp.dma_start(fa[:, 8 + 2 * n:10 + 2 * n, :], o_scr[2 * n:2 * n + 2].rearrange("t p c -> p t c")).then_inc(sem(f"o_in{n}"), 16)

            def gate_in(pair, s_, t):
                sp.dma_start(fa[:, 12 + s_, :], sig_scr[pair, s_ % 2]).then_inc(sem(f"sig_in{s_}"), 16)

            for s_ in range(4):
                gate_in(s_ // 2, s_, s_)
            for n in range(2):
                sp.dma_start(fa[:, 4 * n:4 * n + 4, :], mix_scr[4 * n:4 * n + 4].rearrange("t p c -> p t c")).then_inc(sem(f"mix_in{n}"), 16)
            for un in range(1, 4):
                if un >= 2:
                    unit("w_branch", un, un % 2, U_BR + un)
                for s_ in range(4):
                    sp.wait_ge(sem("mixed"), 4 * un + s_ - 3)
                    gate_in(2 * un + s_ // 2, s_, s_)
            for n in range(2):
                unit("w_tail", n, n, U_OUT + n)
            for k in range(KT):
                sp.wait_ge(sem("mixed_lo"), k + 1)
                sp.dma_start(fa[:, k, :], a["xT"][k]).then_inc(sem(f"x_in{k}"), 16)
            with sp.Fori(0, (UNITS - U_OUT) // 2 - 1) as i:
                for n in range(2):
                    unit("w_tail", i * 2 + (2 + n), n, i * 2 + (U_OUT + 2 + n))
            for k in range(KT):
                sp.wait_ge(sem("out_done"), k + 1)
                sp.dma_start(out[k], fa[:, k, :]).then_inc(sem("stored"), 16)
            sp.wait_ge(sem("stored"), 16 * KT)

        @block.gpsimd
        def _(pool):
            pool.memset(zero[:], 0.0).then_inc(sem("zero_set"), 1)
            pool.memset(eps[:, 0:1], EPS).then_inc(sem("zero_set"), 1)
            pool.memset(eps[:, 1:2], RW_LN_EPS).then_inc(sem("zero_set"), 1)
            pool.memset(lru_w, 0.0).then_inc(sem("zero_set"), 1)
            pool.memset(lora[:], 0.0).then_inc(sem("zero_set"), 1)
            pool.memset(state[:], 0.0).then_inc(sem("zero_set"), 1)
            pool.wait_ge(sem("zero_set"), 6)

            def split(u, slot, landed, cols=KT * P, used=None):
                raw, hi, lo = w_raw[:, slot, 0:cols], w_hi[:, slot, 0:cols], w_lo[:, slot, 0:cols]
                pool.wait_ge(sem(f"w_in{slot}"), landed)
                if used:
                    pool.wait_ge(*used)
                elif not (isinstance(u, int) and u < 2):
                    pool.wait_ge(sem("gb2_full"), u - 1)
                pool.tensor_tensor(hi, raw, zero[:, 0:1].to_broadcast([P, cols]), ALU.add).then_inc(sem("w_hi_set"), 1)
                pool.wait_ge(sem("w_hi_set"), u + 1)
                pool.tensor_tensor(lo, raw, hi.bitcast(F32), ALU.subtract).then_inc(sem("w_split"), 1)

            split(0, 0, 16)
            pool.wait_ge(sem("rstd1"), 1)
            for k in range(KT):
                pool.tensor_tensor(fa[:, k, :], fa[:, k, :], fa[:, 9, :], ALU.mult).then_inc(sem("h_norm"), 1)
            split(1, 1, 16)
            with pool.Fori(0, 4) as i:
                split(i * 2 + 2, 0, i * 16 + 32)
                split(i * 2 + 3, 1, i * 16 + 32)
            for u in range(10, 26):
                split(u, u % 2, 16 * (u // 2 + 1))
            def split_mix(i):
                for n in range(2):
                    split(i * 4 + (U_MIX + n), n, i * 32 + 16 * (U_MIX // 2 + 1), W_COLS)
                for n in range(2):
                    pool.wait_ge(sem("gb3_full"), i * 2 + (1 + n))
                    split(i * 4 + (U_MIX + 2 + n), n, i * 32 + 16 * (U_MIX // 2 + 2))

            with pool.Fori(0, NB) as i:
                split_mix(i)
            for un in range(4):
                used = (sem("gb2_full"), U_BR - 1 + un) if un < 2 else (sem("br_full"), 4 * un - 4)
                split(U_BR + un, un % 2, 16 * ((U_BR + un) // 2 + 1), used=used)
            for n in range(2):
                split(U_OUT + n, n, 16 * (U_OUT // 2 + 1), used=(sem("br_full"), 12 + 4 * n))
            with pool.Fori(0, (UNITS - U_OUT) // 2 - 1) as i:
                for n in range(2):
                    split(i * 2 + (U_OUT + 2 + n), n, i * 16 + 16 * (U_OUT // 2 + 2),
                          used=(sem("half_done"), i * 4 + (2 + 2 * n)))

        @block.tensor
        def _(pe):
            pe.wait_ge(sem("msk_in"), 16)
            for k in range(KT):
                pe.wait_ge(sem("sq"), k + 1)
                for hf in range(2):
                    last = pe.matmul(mb[hf], m_("ones"), fa[:, 8 + 2 * (k % 2), hf * HALF:(hf + 1) * HALF],
                                     start=(k == 0), stop=(k == KT - 1))
                last.then_inc(sem("sq_used"), 1)

            def gemm(bank, slot, hf, rhs_hi, rhs_lo, ks, first=0, last=None, off=0):
                last = 3 * ks if last is None else last
                for q in range(first, last):
                    k, which = divmod(q, 3)
                    w = (w_lo if which == 2 else w_hi)[:, slot, off + k * P:off + (k + 1) * P]
                    r = (rhs_lo if which == 1 else rhs_hi)[:, k, hf * HALF:(hf + 1) * HALF]
                    mm = pe.matmul(gb[bank], w, r, start=(q == 0), stop=(q == 3 * ks - 1))
                return mm

            def in_pair(i, first):
                for s in range(2):
                    pe.wait_ge(sem("w_split"), i * 2 + (s + 1))
                    for hf in range(2):
                        if first and s == 0 and hf == 0:
                            for k in range(KT):
                                pe.wait_ge(sem("h_done"), k + 1)
                                mm = gemm(0, 0, 0, h_hi, h_lo, KT, 3 * k, 3 * k + 3)
                        else:
                            if not (first and s == 0):
                                pe.wait_ge(sem(f"gb{2 * hf}_read"), i * 2 + s)
                            mm = gemm(2 * hf, s, hf, h_hi, h_lo, KT)
                        mm.then_inc(sem(f"gb{2 * hf}_full"), 1)

            in_pair(0, True)
            with pe.Fori(0, 4) as i:
                in_pair(i + 1, False)

            pe.wait_ge(sem("gb2_read"), 10)
            pe.wait_ge(sem("rstd1"), 1)
            for blk in range(NB):
                for c in range(2):
                    o = (blk % 2) * 256 + c * P
                    last = pe.transpose(mb[blk // 2][:, o:o + P], fa[:, 8 + c, blk * P:(blk + 1) * P], m_("ident"))
                if blk % 2:
                    last.then_inc(sem("v_turned"), 1)

            def in_job(j, first=0, last=None):
                u, hf = 10 + j // 2, j % 2
                if first == 0:
                    pe.wait_ge(sem("w_split"), u + 1)
                    pe.wait_ge(sem(f"gb{2 * hf}_read"), u)
                mm = gemm(2 * hf, u % 2, hf, h_hi, h_lo, KT, first, last)
                if last is None or last == 3 * KT:
                    mm.then_inc(sem(f"gb{2 * hf}_full"), 1)

            pe.wait_ge(sem("lru_w_in"), 64)
            for c in range(2):
                for j in LRU_JOBS[c]:
                    in_job(j)
                pe.wait_ge(sem("lru_u"), c + 1)
                pe.wait_ge(sem("v_copied"), 4)
                if c == 1:
                    pe.wait_ge(sem("lru_gates"), 2)
                for g in range(2):
                    for hf in range(2):
                        last = pe.matmul(mb[2 * g + hf], lru_w[:, 2 * g + c, :], fa[:, 12, hf * HALF:(hf + 1) * HALF],
                                         start=True, stop=True)
                last.then_inc(sem("lru_ri"), 1)
            for j in LRU_JOBS[2]:
                in_job(j)

            def sb_scores(n):
                b, hd = SB_STEPS[n]
                r, c, keys = 64 * (hd % 2), hd // 2, (b + 1) * P
                pe.wait_ge(sem("sb_sig"), 2 * n)
                if n == 0:
                    pe.wait_ge(sem("lru_gates"), 4)
                for k0 in range(0, keys, HALF):
                    w = min(HALF, keys - k0)
                    last = pe.matmul(mb[k0 // HALF][:, 0:w], fa[r:r + 64, 4 + c, b * P:(b + 1) * P],
                                     fa[r:r + 64, 6 + c, k0:k0 + w], start=True, stop=True)
                last.then_inc(sem("sb_z"), 1)

            def sb_turn(n):
                b, hd = SB_STEPS[n]
                pe.wait_ge(sem("sb_wgt"), n + 1)
                pe.wait_ge(sem("sb_turned_read"), n)
                for k in range(b + 1):
                    last = pe.transpose(mb[2 + k // 4][:, (k % 4) * P:(k % 4 + 1) * P],
                                        fa[:, n % 2, k * P:(k + 1) * P], m_("ident"))
                last.then_inc(sem("sb_turned"), 1)

            def sb_values(n):
                b, hd = SB_STEPS[n]
                r, c, bank = 64 * (hd % 2), hd // 2, 1 + 2 * (n // 4 % 2)
                pe.wait_ge(sem("sb_turned_read"), n + 1)
                if n % 4 == 0 and n >= 8:
                    pe.wait_ge(sem("sb_lo"), n // 4 - 1)
                for k in range(b + 1):
                    last = pe.matmul(gb[bank][r:r + 64, c * P:(c + 1) * P],
                                     vtok[:, k * 256 + hd * 64:k * 256 + hd * 64 + 64],
                                     fa[:, 14 + n % 2, k * P:(k + 1) * P], start=(k == 0), stop=(k == b))
                last.then_inc(sem("sb_o"), 1)

            for n in range(len(SB_STEPS) + 1):
                j = n + JOBS_AHEAD
                if n < len(SB_STEPS):
                    sb_scores(n)
                if j < 32:
                    in_job(j, 0, 12)
                if n >= 1:
                    sb_turn(n - 1)
                if j < 32:
                    in_job(j, 12, 24)
                if n >= 1:
                    sb_values(n - 1)

            pe.wait_ge(sem("sb_turned_read"), 32)
            pe.wait_ge(sem("gb0_read"), 26)
            pe.wait_ge(sem("gb2_read"), 26)
            for blk in range(NB):
                last = pe.transpose(mb[0][:, blk * 8:blk * 8 + 8], fa[0:8, 9, blk * P:(blk + 1) * P],
                                    m_("ident")[0:8, 0:8])
            last.then_inc(sem("ab_turned"), 1)
            pe.wait_ge(sem("tk_g"), 1)
            pe.matmul(mb[1][:, 0:32], m_("tri"), tk[:, 0, :], start=True, stop=True)
            pe.matmul(mb[1][:, 32:64], m_("suffix"), tk[:, 0, :], start=True, stop=True).then_inc(sem("products"), 1)
            pe.wait_ge(sem("lora_in"), 96)
            for nm, n in (("lru_hi", 2), ("lru_lo", 2), ("sb_hi", 8), ("sb_lo", 8)):
                pe.wait_ge(sem(nm), n)

            with pe.Fori(0, NB) as i:
                v = i + 1
                at_mm = [0]

                def gates(upto):
                    while at_mm[0] < upto:
                        if at_mm[0] < 120:
                            n, q = divmod(at_mm[0], 60)
                        else:
                            n, q = 2 + (at_mm[0] - 120) // 48, (at_mm[0] - 120) % 48
                        if q == 0:
                            pe.wait_ge(sem("w_split"), i * 4 + (U_MIX + 1 + n))
                        if q < 48:
                            hf, q0 = divmod(q, 24)
                            if q0 == 0:
                                pe.wait_ge(sem(f"gb{2 * hf}_read"), i * 4 + (U_MIX + n))
                            step = min(upto - at_mm[0], 24 - q0)
                            mm = gemm(2 * hf, n % 2, hf, h_hi, h_lo, KT, q0, q0 + step)
                            if q0 + step == 24:
                                mm.then_inc(sem(f"gb{2 * hf}_full"), 1)
                        else:
                            hf, q0 = divmod(q - 48, 6)
                            if q0 == 0 and n == 0:
                                pe.wait_ge(sem("rw_o"), at("rw_o", i, 0))
                            elif q0 == 0:
                                pe.wait_ge(sem("gated"), i * 4 + (1 + hf))
                            step = min(upto - at_mm[0], 6 - q0)
                            mm = gemm(2 * hf + 1, n, hf, ra[:, 4 * n:4 * n + 2], ra[:, 4 * n + 2:4 * n + 4], 2, q0,
                                      q0 + step, KT * P)
                            if q0 + step == 6:
                                mm.then_inc(sem(f"gb{2 * hf + 1}_full"), 1)
                        at_mm[0] += step

                def heads(bank, lhs, rhs, signal, turn=False):
                    for h in range(4):
                        c = slice(h * P, (h + 1) * P)
                        if turn:
                            mm = pe.transpose(mb[bank][:, c], lhs[:, c], m_("ident"))
                        else:
                            mm = pe.matmul(mb[bank][:, c], lhs[:, c], rhs[:, c], start=True, stop=True)
                    mm.then_inc(done(signal), 1)

                gates(FILL[0])
                pe.wait_ge(sem("rw_lt"), at("rw_lt", i, 3))
                pe.wait_ge(sem("rw_o"), at("rw_o", i, 0))
                for t in range(6):
                    last = pe.matmul(mb[t // 4][:, (t % 4) * P:(t % 4 + 1) * P], lora[:, t, :], rw["lt"], start=True,
                                     stop=True)
                last.then_inc(done("rw_p1"), 1)
                pe.wait_ge(sem("rw_sq"), at("rw_sq", i))
                pe.matmul(mb[2][:, 0:256], m_("bd"), rw["t1"], start=True, stop=True).then_inc(done("rw_p2"), 1)
                gates(FILL[1])
                pe.wait_ge(sem("rw_bonp"), at("rw_bonp", i))
                pe.wait_ge(sem("rw_ln"), at("rw_ln", i))
                pe.matmul(mb[2][:, 256:512], m_("bd"), rw["bon"], start=True, stop=True).then_inc(done("rw_p3"), 1)
                pe.wait_ge(sem("rw_ar"), at("rw_ar", i, 2))
                for t in range(2):
                    pe.transpose(mb[3][:, t * P:(t + 1) * P], rw["pm"][:, (4 + t) * P:(5 + t) * P], m_("ident"))
                for t in range(2):
                    last = pe.transpose(mb[3][:, (2 + t) * P:(3 + t) * P], rw["ar"][:, t * 256:t * 256 + P], m_("ident"))
                last.then_inc(done("rw_p4"), 1)
                gates(FILL[2])
                pe.wait_ge(sem("rw_km"), at("rw_km", i))
                pe.wait_ge(sem("rw_gate"), at("rw_gate", i))

                def scores(b0, key, both, signal):
                    for h in range(4):
                        r, t = 64 * (h % 2), h // 2
                        last = pe.matmul(mb[b0 + h % 2][:, t * 256:t * 256 + 256],
                                         key[r:r + 64, t * P:(t + 1) * P], both[r:r + 64, t * 256:(t + 1) * 256],
                                         start=True, stop=True)
                    last.then_inc(done(signal), 1)

                scores(0, rw["km"], rw["ar"], "rw_p6")
                pe.wait_ge(sem("rw_bon"), at("rw_bon", i))
                for t in range(4):
                    last = pe.transpose(mb[2][:, t * P:(t + 1) * P], (rw["bt"] if t < 2 else rw["kt"])[:, (t % 2) * P:(t % 2 + 1) * P], m_("ident"))
                last.then_inc(done("rw_p5"), 1)
                pe.wait_ge(sem("rw_tokBK"), at("rw_tokBK", i))
                scores(2, rw["bm"], rw["ar"], "rw_p7")
                gates(FILL[3])
                pe.wait_ge(sem("rw_ltr"), at("rw_ltr", i, 2))
                heads(0, rw["ltr"], None, "rw_p8", turn=True)
                for h in range(4):
                    last = pe.matmul(mb[3][:, h * 64:h * 64 + 64], rw["akt"][:, h * P:(h + 1) * P],
                                     rw["tokVA"][:, h * 64:h * 64 + 64], start=True, stop=True)
                last.then_inc(done("rw_r1"), 1)

                gates(FILL_L)
                pe.wait_ge(sem("gd_sq"), at("gd_sq", i))
                pe.matmul(mb[1][:], m_("bd"), gd["sq"], start=True, stop=True).then_inc(done("gd_g1"), 1)
                pe.wait_ge(sem("gd_gbc"), at("gd_gbc", i, 2))
                for h in range(4):
                    last = pe.matmul(mb[2][:, h * P:(h + 1) * P], gd["gbc"][:, h * P:(h + 1) * P], m_("tri"), start=True,
                                     stop=True)
                last.then_inc(done("gd_g2"), 1)
                gates(FILL[4])
                pe.wait_ge(sem("rw_x"), at("rw_x", i))
                for t in range(4):
                    last = pe.matmul(mb[3][:, t * P:(t + 1) * P], gd["bb"][:, t * P:(t + 1) * P],
                                     m_("tri" if t < 2 else "ident"), start=True, stop=True)
                last.then_inc(done("gd_g3"), 1)
                pe.wait_ge(sem("gd_rn"), at("gd_rn", i))
                pe.wait_ge(sem("gd_kn"), at("gd_kn", i))
                for t in range(2):
                    pe.transpose(mb[1][:, t * P:(t + 1) * P], gd["kn"][:, t * P:(t + 1) * P], m_("ident"))
                for t in range(2):
                    last = pe.transpose(mb[1][:, (2 + t) * P:(3 + t) * P], gd["acc"][:, (4 + t) * P:(5 + t) * P], m_("ident"))
                last.then_inc(done("gd_g4"), 1)
                pe.wait_ge(sem("gd_kbq"), at("gd_kbq", i, 2))
                pe.wait_ge(sem("gd_eg"), at("gd_eg", i))
                scores(2, gd["kn"], gd["kbq"], "gd_g5")
                gates(FILL[5])
                pe.wait_ge(sem("gd_ltr"), at("gd_ltr", i))
                heads(1, gd["ltr"], None, "gd_g6", turn=True)

                fill = FILL[5]
                for lv in range(5):
                    last_lv = lv == 4
                    for nm, b_, st in (("rw", rw, 0), ("gd", gd, 1)):
                        pe.wait_ge(sem(f"{nm}_T"), at(f"{nm}_T", i, 2 * lv + 1))
                        heads(0 if nm == "rw" else 3, b_["ltr"], b_["T"], f"{nm}_Y")
                    fill += FILL_Y
                    gates(fill)
                    for nm, b_ in (("rw", rw), ("gd", gd)):
                        if nm == "rw":
                            pe.wait_ge(sem("rw_Ym"), at("rw_Ym", i, lv + 1))
                        else:
                            pe.wait_ge(sem("rw_T"), at("rw_T", i, min(2 * lv + 3, 10)))
                        if not last_lv:
                            heads(1, b_["TT"], b_["Y"], f"{nm}_Z")
                        heads(2, b_["Y"], b_["TT"], f"{nm}_Z")
                        fill += FILL_Z
                        gates(fill)

                def intra(nm, bank, b_, rhs, key):
                    pe.wait_ge(sem(f"{nm}_T"), at(f"{nm}_T", i, 10))
                    for h in range(4):
                        pe.matmul(mb[bank][:, h * 64:h * 64 + 64], b_["TT"][:, h * P:(h + 1) * P],
                                  rhs[:, h * 64:h * 64 + 64], start=True, stop=True)
                    for h in range(4):
                        r, c = 64 * (h % 2), 256 + (h // 2) * P
                        last = pe.matmul(mb[bank][r:r + 64, c:c + P], key[:, h * 64:h * 64 + 64],
                                         b_["TT"][:, h * P:(h + 1) * P], start=True, stop=True)
                    last.then_inc(done(f"{nm}_r3"), 1)

                intra("rw", 1, rw, rw["x"], rw["tokVA"][:, 256:512])
                intra("gd", 3, gd, gd["vb"], gd["kbe"])
                gates(FILL[6])
                for par_ in range(2):
                    R = slice(64 * par_, 64 * par_ + 64)
                    for nm, b_, st, ws in (("rw", rw, 0, 0), ("gd", gd, 1, 256)):
                        if par_ == 0:
                            pe.wait_ge(sem(f"{nm}_uw"), at(f"{nm}_uw", i))
                        if nm == "rw":
                            pe.wait_ge(sem("gd_S"), at("gd_S", i, 4 * par_))
                        for t in range(2):
                            last = pe.matmul(mb[0][R, ws + t * P:ws + (t + 1) * P],
                                             b_["uw"][:, 256 + t * P + 64 * par_:256 + t * P + 64 * par_ + 64],
                                             state[:, st, t, :], start=True, stop=True)
                        last.then_inc(done(f"{nm}_ws"), 1)
                    gates(FILL[7 + par_])
                    for nm, b_, st, yb, sc in (("rw", rw, 0, 2, 1), ("gd", gd, 1, 3, 0)):
                        for t in range(2):
                            q_ = (rw["ar"][:, t * 256 + P + 64 * par_:t * 256 + P + 64 * par_ + 64] if nm == "rw"
                                  else gd["qd"][:, t * P + 64 * par_:t * P + 64 * par_ + 64])
                            if nm == "rw" and par_ == 0 and t == 0:
                                pe.wait_ge(sem("gd_T"), at("gd_T", i, 10))
                            pe.matmul(mb[yb][:, t * P + 64 * par_:t * P + 64 * par_ + 64], state[:, st, t, :], q_,
                                      start=(par_ == 0 and t == 0), stop=True, skip_group_check=True)
                        pe.wait_ge(sem(f"{nm}_u"), at(f"{nm}_u", i, par_ + 1))
                        for t in range(2):
                            c = slice(t * P, (t + 1) * P)
                            if nm == "rw":
                                pe.matmul(mb[sc][:, c], rw["tokBK"][R, c], rw["u"][R, c],
                                          start=True, stop=False)
                                last = pe.matmul(mb[sc][:, c], rw["tokBK"][R, 256 + t * P:256 + (t + 1) * P], rw["tokVA"][R, c],
                                                 start=False, stop=True)
                            else:
                                last = pe.matmul(mb[sc][:, c], gd["kd"][R, c], gd["u"][R, c], start=True, stop=True)
                        last.then_inc(done(f"{nm}_s"), 1)
                        terms = [(b_["u"], rw["rbt"] if nm == "rw" else gd["qkt"])]
                        if nm == "rw":
                            terms.append((rw["tokVA"], rw["rkt"]))
                        for h in range(4):
                            r, c = 64 * (h % 2), (h // 2) * P + 64 * par_
                            for lhs, rhs in terms:
                                last = pe.matmul(mb[yb][r:r + 64, c:c + 64], lhs[R, h * 64:h * 64 + 64],
                                                 rhs[R, h * P + 64 * par_:h * P + 64 * par_ + 64], start=False, stop=True,
                                                 skip_group_check=True)
                        last.then_inc(done(f"{nm}_Yd"), 1)
                gates(FILL[9])
                pe.wait_ge(sem("rw_y"), at("rw_y", i))
                pe.wait_ge(sem("gd_S"), at("gd_S", i, 8))
                pe.matmul(mb[0][:, 0:256], m_("bd"), rw["y"], start=True, stop=True).then_inc(done("rw_m1"), 1)
                
                pe.wait_ge(sem("gd_y2"), at("gd_y2", i))
                pe.matmul(mb[1][:, 0:256], m_("bd"), gd["y2"], start=True, stop=True).then_inc(done("gd_m"), 1)
                gates(FILL[10])
                pe.wait_ge(sem("rw_y2"), at("rw_y2", i))
                pe.matmul(mb[0][:, 256:512], m_("bd"), rw["y2"], start=True, stop=True).then_inc(done("rw_m2"), 1)
                gates(216)

            for hf in range(2):
                pe.wait_ge(sem(f"gb{2 * hf}_read"), U_BR)
            with pe.Fori(0, 2) as i:
                for n in range(2):
                    pe.wait_ge(sem("w_split"), i * 2 + (U_BR + 1 + n))
                    for q in range(4):
                        br, bank = q % 2, 2 * (q % 2)
                        pe.wait_ge(sem("gated"), i * 8 + (4 * NB - 1 + 4 * n + q))
                        pe.wait_ge(sem("o_lo"), 1 + br)
                        for hf in range(2):
                            mm = gemm(bank + hf, n, hf, ra[:, 4 * br:4 * br + 2], ra[:, 4 * br + 2:4 * br + 4], 2, off=q * 256)
                        mm.then_inc(sem("br_full"), 1)

            def out_unit(m, slot, first):
                pe.wait_ge(sem("w_split"), m + (U_OUT + 1))
                for hf in range(2):
                    if first:
                        pe.wait_ge(sem("gated"), 6 * NB)
                    else:
                        pe.wait_ge(sem("x1"), m * 2 + (hf - 3))
                    if first and slot == 0:
                        for k in range(KT):
                            pe.wait_ge(sem("mixed_lo"), k + 1)
                            mm = gemm(2 * hf + slot, slot, hf, h_hi, h_lo, KT, 3 * k, 3 * k + 3)
                    else:
                        mm = gemm(2 * hf + slot, slot, hf, h_hi, h_lo, KT)
                    mm.then_inc(sem("half_done"), 1)

            for m in range(2):
                out_unit(m, m, True)
            with pe.Fori(0, KT // 2 - 1) as i:
                for n in range(2):
                    out_unit(i * 2 + (2 + n), n, False)

            def sum_over_channels(n, bank):
                pe.wait_ge(sem("sq_added"), n * (KT - 1))
                for hf in range(2):
                    mm = pe.matmul(bank[hf], m_("ones"), fa[:, ACC, hf * HALF:(hf + 1) * HALF], start=True, stop=True)
                mm.then_inc(sem("sq_summed"), 1)

            pe.wait_ge(sem("rw_rno"), at("rw_rno", NB - 1))
            pe.wait_ge(sem("rw_o"), at("rw_o", NB - 1))
            sum_over_channels(1, mb)

            def ffn_tile(t, u):
                first = isinstance(t, int) and t == 0
                for up in range(2):
                    pe.wait_ge(sem("w_split"), u + (1 + up))
                    for hf in range(2):
                        if first:
                            pe.wait_ge(sem("x1"), 2 * KT)
                        else:
                            pe.wait_ge(sem("up_read" if up else "gate_read"), t * 2 + (hf - 1))
                        if first and not up and hf == 0:
                            for k in range(KT):
                                pe.wait_ge(sem("h_done"), KT + k + 1)
                                mm = gemm(2 * hf + up, up, hf, h_hi, h_lo, KT, 3 * k, 3 * k + 3)
                        else:
                            mm = gemm(2 * hf + up, up, hf, h_hi, h_lo, KT)
                        mm.then_inc(sem("half_done"), 1)

            def ffn_down(g, u, d, ks):
                pe.wait_ge(sem("w_split"), u + (1 + d))
                n = KT // ks
                for ml in range(n):
                    m = d * n + ml
                    if m >= 2:
                        pe.wait_ge(sem("down_read"), g * KT + (m - 1))
                    for hf in range(2):
                        for q in range(3 * ks):
                            k, which = divmod(q, 3)
                            w = (w_lo if which == 2 else w_hi)[:, d % 2, (ml * ks + k) * P:(ml * ks + k + 1) * P]
                            x_ = ra[:, (GT if which == 1 else 0) + k, hf * HALF:(hf + 1) * HALF]
                            mm = pe.matmul(mb[2 * (ml % 2) + hf], w, x_, start=(q == 0), stop=(q == 3 * ks - 1))
                    if ml % (n // 2) == n // 2 - 1:
                        mm.then_inc(sem("half_done"), 1)

            ffn_tile(0, U_FFN)
            pe.wait_ge(sem("rstd"), 1)
            with pe.Fori(0, NG) as g:
                for q in range(GT):
                    ffn_tile(g * GT + (1 + q), g * UG + (U_FFN + 2 + 2 * q))
                pe.wait_ge(sem("act_lo"), g * GT + GT)
                for d in range(4):
                    ffn_down(g, g * UG + (U_FFN + 2 + 2 * GT), d, GT)
            ffn_tile(FT - 1, UNITS - 4)
            pe.wait_ge(sem("act_lo"), FT)
            for d in range(2):
                ffn_down(NG, UNITS - 2, d, FT - NG * GT)

            pe.wait_ge(sem("up_read"), 2 * FT)
            pe.wait_ge(sem("gate_read"), 2 * FT)
            sum_over_channels(2, gb)

        @block.scalar
        def _(act):
            def softplus_act(nth, n):
                act.activation(sp_t[:, 2, 0:n], sp_t[:, 1, 0:n], ACT.Exp, scale=-1.0).then_inc(sem("softplus_exp"), 1)
                act.wait_ge(sem("softplus_1p"), nth)
                act.activation(sp_t[:, 4, 0:n], sp_t[:, 3, 0:n], ACT.Ln).then_inc(sem("softplus_ln"), 1)

            act.wait_ge(sem("c_in"), 16)
            act.activation(fa[:, 11, :], fa[:, 11, :], ACT.Silu).then_inc(sem("cond"), 1)
            for k in range(KT):
                act.wait_ge(sem(f"x_in{k}"), 16)
                if k >= 2:
                    act.wait_ge(sem("sq_used"), k - 1)
                act.activation(fa[:, 8 + 2 * (k % 2), :], fa[:, k, :], ACT.Square).then_inc(sem("sq"), 1)
            act.wait_ge(sem("sq_used"), KT)
            act.wait_ge(sem("zero_set"), 6)
            for hf in range(2):
                act.activation(fa[:, 9, hf * HALF:(hf + 1) * HALF], mb[hf], ACT.Ln, bias=eps[:, 0:1],
                               scale=1.0 / D).then_inc(sem("ln1"), 1)
            act.wait_ge(sem("ln1"), 2)
            act.activation(fa[:, 9, :], fa[:, 9, :], ACT.Exp, scale=-0.5).then_inc(sem("rstd1"), 1)
            for k in range(KT):
                act.wait_ge(sem("h_f32"), k + 1)
                act.activation(h_hi[:, k, :], fa[:, k, :], ACT.Copy).then_inc(sem("h_hi"), 1)
            with act.Fori(0, 5) as i:
                for s in range(2):
                    for hf in range(2):
                        act.wait_ge(sem(f"gb{2 * hf}_full"), i * 2 + (s + 1))
                        act.activation(fa[:, bass.ds(i * 2 + s, 1), hf * HALF:(hf + 1) * HALF], gb[2 * hf], ACT.Copy).then_inc(sem(f"gb{2 * hf}_read"), 1)

            def in_read(j):
                u, hf = 10 + j // 2, j % 2
                slot = u % 2
                act.wait_ge(sem(f"gb{2 * hf}_full"), u + 1)
                if u < 12:
                    act.wait_ge(sem("v_turned"), 4)
                else:
                    act.wait_ge(sem(f"p_out{slot}"), 32 * ((u - 10) // 2))
                act.activation(fa[:, 8 + slot, hf * HALF:(hf + 1) * HALF], gb[2 * hf], ACT.Copy).then_inc(
                    sem(f"gb{2 * hf}_read"), 1)
                if u < 25:
                    act.wait_ge(sem(f"gb{2 * hf}_read"), u + 1)
                    act.dma_start(p_scr[u - 10][:, HALO + hf * HALF:HALO + (hf + 1) * HALF],
                                  fa[:, 8 + slot, hf * HALF:(hf + 1) * HALF]).then_inc(sem(f"p_out{slot}"), 16)

            act.wait_ge(sem("softplus_abs"), 1)
            softplus_act(1, 2)
            for i in range(4):
                act.wait_ge(sem("v_turned"), i + 1)
                act.activation(vtok[:, i * HALF:(i + 1) * HALF], mb[i], ACT.Copy).then_inc(sem("v_copied"), 1)
            for j in LRU_JOBS[0]:
                in_read(j)
            for c in range(2):
                act.wait_ge(sem("lru_ri"), c + 1)
                if c == 1:
                    act.wait_ge(sem("lru_scan"), 1)
                act.activation(fa[:, 13, :], mbank[:, 0:2, :].rearrange("p b s -> p (b s)"), ACT.Sigmoid,
                               bias=pc("lru_br", c)).then_inc(sem("lru_gates"), 1)
                act.activation(fa[:, 14, :], mbank[:, 2:4, :].rearrange("p b s -> p (b s)"), ACT.Sigmoid,
                               bias=pc("lru_bi", c)).then_inc(sem("lru_gates"), 1)
                act.wait_ge(sem("lru_gates"), 2 * c + 1)
                act.wait_ge(sem("sl"), 1)
                act.activation(fa[:, 15, :], fa[:, 13, :], ACT.Exp, scale=sl[:, c:c + 1]).then_inc(sem("lru_a"), 1)
                act.wait_ge(sem("lru_a"), 3 * c + 1)
                act.activation(fa[:, 13, :], fa[:, 13, :], ACT.Tanh, scale=sl[:, 2 + c:3 + c]).then_inc(sem("lru_a"), 1)
                act.activation(fa[:, 2 + c, :], fa[:, 2 + c, :], ACT.Gelu_apprx_tanh).then_inc(sem("lru_gelu"), 1)
                act.wait_ge(sem("lru_b2"), c + 1)
                act.activation(fa[:, 13, :], fa[:, 13, :], ACT.Sqrt).then_inc(sem("lru_a"), 1)
                for j in LRU_JOBS[c + 1]:
                    in_read(j)
                act.wait_ge(sem("lru_o"), c + 1)
                act.activation(ra[:, c, :], fa[:, 12, :], ACT.Copy).then_inc(sem("lru_hi"), 1)

            def sb_sigmoids(n):
                b, hd = SB_STEPS[n]
                keys = (b + 1) * P
                z = mbank[:, 0:2, :].rearrange("p b s -> p (b s)")[:, 0:keys]
                act.wait_ge(sem("sb_z"), n + 1)
                if n == 0:
                    act.wait_ge(sem("lru_lo"), 2)
                if n >= 2:
                    act.wait_ge(sem("sb_turned"), n - 1)
                    act.wait_ge(sem("sb_scan"), n - 1)
                act.activation(fa[:, n % 2, 0:keys], z, ACT.Sigmoid, scale=HEAD ** -0.5).then_inc(sem("sb_sig"), 1)
                act.activation(fa[:, 2 + n % 2, 0:keys], z, ACT.Sigmoid, scale=-HEAD ** -0.5).then_inc(sem("sb_sig"), 1)

            def sb_copy(n):
                b, hd = SB_STEPS[n]
                keys = (b + 1) * P
                act.wait_ge(sem("sb_turned"), n + 1)
                if n >= 2:
                    act.wait_ge(sem("sb_o"), n - 1)
                act.activation(fa[:, 14 + n % 2, 0:keys], mbank[:, 2:4, :].rearrange("p b s -> p (b s)")[:, 0:keys],
                               ACT.Copy).then_inc(sem("sb_turned_read"), 1)

            def sb_hi(n):
                b, hd = SB_STEPS[n]
                bank = 1 + 2 * (n // 4 % 2)
                act.wait_ge(sem("sb_o"), n + 1)
                act.activation(ra[:, 4:6, b * P:(b + 1) * P], gb[bank][:, 0:256].rearrange("p (c s) -> p c s", c=2),
                               ACT.Copy).then_inc(sem("sb_hi"), 1)

            for n in range(len(SB_STEPS) + 1):
                j = n + JOBS_AHEAD
                if n < len(SB_STEPS):
                    sb_sigmoids(n)
                if n >= 1:
                    sb_copy(n - 1)
                if j < 32:
                    in_read(j)
                if n >= 1 and (n - 1) % 4 == 3:
                    sb_hi(n - 1)

            act.wait_ge(sem("ab_read"), 1)
            act.activation(tk[:, 1, :].rearrange("p (b h) -> p b h", h=4), abt[:].rearrange("p (b h) -> p b h", h=8)[:, :, 4:8],
                           ACT.Sigmoid).then_inc(sem("tk_act"), 1)
            act.wait_ge(sem("softplus_abs"), 2)
            softplus_act(2, 32)
            act.activation(ea[:], par[:, PAR["alog"]], ACT.Exp).then_inc(sem("ea"), 1)
            act.wait_ge(sem("products"), 1)
            act.activation(tk[:, 2, :], mb[1][:, 0:32], ACT.Copy).then_inc(sem("tk_act"), 1)
            act.activation(tk[:, 3, :], mb[1][:, 32:64], ACT.Exp).then_inc(sem("tk_act"), 1)
            act.activation(tk[:, 5, :], mb[1][:, 0:32], ACT.Exp).then_inc(sem("functions"), 1)

            with act.Fori(0, NB) as i:
                v = i + 1

                def gate_sig(job):
                    n, hf = divmod(job, 2)
                    if hf == 0:
                        act.activation(bgc[:, n % 2:n % 2 + 1], par[:, bass.ds(i + (PAR["b_gate"].start + 8 * n), 1)],
                                       ACT.Copy).then_inc(sem("bgc"), 1)
                        act.wait_ge(sem("bgc"), i * 4 + (n + 1))
                    act.wait_ge(sem(f"gb{2 * hf}_full"), i * 4 + (U_MIX + 1 + n))
                    if 0 < job < 4:
                        act.wait_ge(sem("gated"), i * 4 + job)
                    if job >= 4:
                        act.wait_ge(sem("sig_stored"), i * 64 + (16 * (job - 4) + 16))
                    act.activation(sig if job < 4 else sig_out, gb[2 * hf], ACT.Sigmoid,
                                   bias=bgc[:, n % 2:n % 2 + 1]).then_inc(sem(f"gb{2 * hf}_read"), 1)
                    if job >= 4:
                        act.wait_ge(sem(f"gb{2 * hf}_read"), i * 4 + (U_MIX + 1 + n))
                        act.dma_start(sig_scr[bass.ds(i, 1), n - 2, :, hf * HALF:(hf + 1) * HALF].rearrange("t p c -> p (t c)"),
                                      sig_out).then_inc(sem("sig_stored"), 16)

                act.wait_ge(sem("rw_pm"), at("rw_pm", i))
                act.wait_ge(sem("rw_m2"), at("rw_m2", i, 0))
                act.activation(rw["lt"][0:32, :], rw["pm"][0:32, 6 * P:7 * P], ACT.Tanh).then_inc(done("rw_lt"), 1)
                act.activation(rw["lt"][32:64, :], rw["pm"][32:64, 6 * P:7 * P], ACT.Copy).then_inc(done("rw_lt"), 1)
                act.activation(rw["lt"][64:128, :], rw["pm"][64:128, 6 * P:7 * P], ACT.Sigmoid).then_inc(done("rw_lt"), 1)
                act.wait_ge(sem("rw_kkr"), at("rw_kkr", i))
                act.activation(rw["t1"], rw["kkr"], ACT.Square).then_inc(done("rw_sq"), 1)
                gate_sig(0)
                act.wait_ge(sem("rw_p1"), at("rw_p1", i))
                for t in range(2):
                    act.activation(rw["sw"][:, t * P:(t + 1) * P], mb[0][:, t * P:(t + 1) * P], ACT.Sigmoid,
                                   bias=pc("rw_w0", t)).then_inc(done("rw_sw"), 1)
                for t in range(2):
                    act.activation(rw["sa"][:, t * P:(t + 1) * P], mb[0][:, (2 + t) * P:(3 + t) * P], ACT.Sigmoid,
                                   bias=pc("rw_a0", t)).then_inc(done("rw_sa"), 1)
                act.activation(rw["gate"], mb[1][:, 0:256], ACT.Copy).then_inc(done("rw_gate"), 1)
                act.wait_ge(sem("rw_p2"), at("rw_p2", i))
                act.activation(rw["rn"], mb[2][:, 0:256], ACT.Ln, bias=eps[:, 0:1]).then_inc(done("rw_ln"), 1)
                act.wait_ge(sem("rw_ln"), at("rw_ln", i))
                act.activation(rw["rn"], rw["rn"], ACT.Exp, scale=-0.5).then_inc(done("rw_rn"), 1)
                act.wait_ge(sem("rw_gs"), at("rw_gs", i, 2))
                act.activation(rw["ex1"], rw["gs"], ACT.Exp, scale=-E_HALF).then_inc(done("rw_ex"), 1)
                act.activation(rw["exn"], rw["gs"], ACT.Exp, scale=E_HALF).then_inc(done("rw_ex"), 1)
                act.wait_ge(sem("rw_gm"), at("rw_gm", i))
                act.activation(rw["ex0"], rw["gm"], ACT.Exp, scale=-E_HALF).then_inc(done("rw_ex"), 1)
                act.wait_ge(sem("rw_p4"), at("rw_p4", i))
                act.activation(rw["tokVA"], mb[3], ACT.Copy).then_inc(done("rw_tokVA"), 1)
                gate_sig(1)
                act.wait_ge(sem("rw_p5"), at("rw_p5", i))
                act.activation(rw["tokBK"], mb[2], ACT.Copy).then_inc(done("rw_tokBK"), 1)
                act.wait_ge(sem("gd_acc"), at("gd_acc", i))
                act.activation(gd["acc"], gd["acc"], ACT.Silu).then_inc(done("gd_silu"), 1)
                act.activation(t2(gd["z"]), pblk[:, 13:15, HALO:], ACT.Silu).then_inc(done("pblk_read"), 1)
                act.wait_ge(sem("gd_silu"), at("gd_silu", i))
                act.activation(gd["sq"], gd["acc"][:, 0:512], ACT.Square).then_inc(done("gd_sq"), 1)
                act.wait_ge(sem("tkc"), at("tkc", i))
                act.activation(t4(gd["gbc"]), tkc[:, 0:4].rearrange("p (h o) -> p h o", o=1).to_broadcast([P, 4, P]),
                               ACT.Copy).then_inc(done("gd_gbc"), 1)
                act.activation(gd["bb"].rearrange("p (h c) -> p h c", c=64),
                               tkc[:, 0:8].rearrange("p (h o) -> p h o", o=1).to_broadcast([P, 8, 64]),
                               ACT.Copy).then_inc(done("gd_gbc"), 1)
                gate_sig(2)
                act.wait_ge(sem("rw_r1"), at("rw_r1", i))
                act.activation(rw["x"], mb[3][:, 0:256], ACT.Copy).then_inc(done("rw_x"), 1)
                act.wait_ge(sem("gd_g1"), at("gd_g1", i))
                act.activation(gd["rn"], mb[1], ACT.Ln, bias=eps[:, 0:1]).then_inc(done("gd_ln"), 1)
                act.wait_ge(sem("gd_ln"), at("gd_ln", i))
                act.activation(gd["rn"], gd["rn"], ACT.Exp, scale=-0.5).then_inc(done("gd_rn"), 1)
                act.wait_ge(sem("gd_dtm"), at("gd_dtm", i))
                act.activation(gd["dt"], gd["dt"], ACT.Exp).then_inc(done("gd_dt"), 1)
                act.wait_ge(sem("gd_g3"), at("gd_g3", i))
                act.activation(gd["eg"], mb[3][:, 0:256], ACT.Exp).then_inc(done("gd_eg"), 1)
                for job in (3, 4):
                    gate_sig(job)
                for nm, bank, b_ in (("rw", 1, rw), ("gd", 3, gd)):
                    act.wait_ge(sem(f"{nm}_r3"), at(f"{nm}_r3", i))
                    act.activation(b_["uw"], mb[bank], ACT.Copy).then_inc(done(f"{nm}_uw"), 1)
                gate_sig(5)
                act.wait_ge(sem("rw_Yd"), at("rw_Yd", i, 2))
                act.activation(rw["y"], mb[2][:, 0:256], ACT.Copy).then_inc(done("rw_y"), 1)
                act.wait_ge(sem("gd_Yd"), at("gd_Yd", i, 2))
                act.activation(gd["y2"], mb[3][:, 0:256], ACT.Square).then_inc(done("gd_y2"), 1)
                act.wait_ge(sem("gd_m"), at("gd_m", i))
                act.activation(gd["rno"], mb[1][:, 0:256], ACT.Ln, bias=eps[:, 0:1], scale=1.0 / HEAD).then_inc(done("gd_lno"), 1)
                act.wait_ge(sem("gd_lno"), at("gd_lno", i))
                act.activation(gd["rno"], gd["rno"], ACT.Exp, scale=-0.5).then_inc(done("gd_rno"), 1)
                act.wait_ge(sem("rw_yc"), at("rw_yc", i))
                act.activation(rw["y2"], rw["yc"], ACT.Square).then_inc(done("rw_y2"), 1)
                gate_sig(6)
                act.wait_ge(sem("rw_m2"), at("rw_m2", i))
                act.activation(rw["u"], mb[0][:, 256:512], ACT.Ln, bias=eps[:, 1:2], scale=1.0 / HEAD).then_inc(done("rw_lno"), 1)
                act.wait_ge(sem("rw_lno"), at("rw_lno", i))
                act.activation(rw["u"], rw["u"], ACT.Exp, scale=-0.5).then_inc(done("rw_rno"), 1)
                gate_sig(7)

            for n in range(2):
                act.wait_ge(sem(f"o_in{n}"), 16)
                act.activation(ra[:, 4 * n:4 * n + 2], fa[:, 8 + 2 * n:10 + 2 * n, :], ACT.Copy).then_inc(sem("o_hi"), 1)
            for k in range(KT):
                act.wait_ge(sem("mixed"), 2 * k + 2)
                act.activation(h_hi[:, k, :], fa[:, k, :], ACT.Copy).then_inc(sem("mixed_hi"), 1)

            def square(m, par_, nth, ready, count):
                act.wait_ge(sem(ready), count)
                if isinstance(m, int) and m == 0:
                    act.activation(fa[:, ACC, :], fa[:, 0, :], ACT.Square).then_inc(sem("sq"), 1)
                    return
                if not (isinstance(m, int) and m < 3):
                    act.wait_ge(sem("sq_added"), m + (7 * nth - 2))
                src = fa[:, m, :] if isinstance(m, int) else fa[:, bass.ds(m, 1), :]
                act.activation(fa[:, SQ + par_, :], src, ACT.Square).then_inc(sem("sq"), 1)

            def root(n, bank):
                act.wait_ge(sem("sq_summed"), n)
                act.activation(fa[:, RSTD, :], bank, ACT.Ln, bias=eps[:, 0:1], scale=1.0 / D).then_inc(sem("ln2"), 1)
                act.wait_ge(sem("ln2"), n)
                act.activation(fa[:, RSTD, :], fa[:, RSTD, :], ACT.Exp, scale=-0.5).then_inc(sem("rstd"), 1)

            for m in range(KT):
                square(m, m % 2, 0, "x1", 2 * m + 2)
            root(1, mbank[:, 0:2, :].rearrange("p b s -> p (b s)"))
            act.wait_ge(sem("half_done"), 2 * KT)
            for k in range(KT):
                act.wait_ge(sem("h_norm"), KT + k + 1)
                act.activation(fa[:, 12 + k % 4, :], fa[:, 12 + k % 4, :], ACT.Identity, bias=mod[:, 24 + k:25 + k],
                               scale=a1[:, 8 + k:9 + k]).then_inc(sem("h_f32"), 1)
                act.wait_ge(sem("h_f32"), KT + k + 1)
                act.activation(h_hi[:, k, :], fa[:, 12 + k % 4, :], ACT.Copy).then_inc(sem("h_hi"), 1)

            def ffn_act(t, s_, half):
                for hf in range(2):
                    act.wait_ge(sem("half_done"), half + hf)
                    act.activation(G[s_][:, 2 + hf * HALF:2 + (hf + 1) * HALF], gb[2 * hf], ACT.Copy).then_inc(sem("gate_read"), 1)
                act.wait_ge(sem("conv"), t + 1)
                act.activation(C[s_], C[s_], ACT.Gelu_apprx_tanh).then_inc(sem("gelu"), 1)

            def ffn_hi(t, s_, j):
                act.wait_ge(sem("up_read"), t * 2 + 2)
                act.activation(ra[:, j, :], fa[:, 13 + s_, :], ACT.Copy).then_inc(sem("act_hi"), 1)

            act.wait_ge(sem("g_halo"), 2)
            ffn_act(0, 0, 2 * KT + 1)
            ffn_hi(0, 0, 0)
            with act.Fori(0, NG) as g:
                for q in range(GT):
                    t, u = g * GT + (1 + q), 2 * (2 + 2 * q) + 2 * KT
                    ffn_act(t, (1 + q) % 2, g * (2 * UG) + (u + 1))
                    if q < GT - 1:
                        ffn_hi(t, (1 + q) % 2, 1 + q)
                act.wait_ge(sem("half_done"), g * (2 * UG) + (2 * KT + 4 + 2 * UG))
                ffn_hi(g * GT + GT, 0, 0)
            ffn_act(FT - 1, 1, 2 * (UNITS - U_OUT) - 7)
            ffn_hi(FT - 1, 1, 1)
            for m in range(KT):
                square(m, m % 2, 1, "down_read", KT * NG + m + 1)
            root(2, gbank[:, 0:2, :].rearrange("p b s -> p (b s)"))

        @block.vector
        def _(dve):
            def ada(t, slot, landed, col):
                dve.wait_ge(sem(f"ada_in{slot}"), landed)
                dve.tensor_tensor_reduce(fa[:, 12 + slot, :], fa[:, 12 + slot, :], fa[:, 11, :], 1.0, 0.0, ALU.mult,
                                         ALU.add, col).then_inc(sem("ada_used"), 1)

            dve.wait_ge(sem("cond"), 1)
            for t in range(16):
                ada(t, t % 3, 16 * (t // 3 + 1), mod[:, t:t + 1])
            dve.wait_ge(sem("ada_used"), 16)
            dve.wait_ge(sem("par_in"), 16)
            dve.tensor_tensor(mod[:, 0:16], mod[:, 0:16], par[:, PAR["b_ada"].start:PAR["b_ada"].start + 16],
                              ALU.add).then_inc(sem("mod1"), 1)
            dve.wait_ge(sem("mod1"), 1)
            dve.scalar_tensor_tensor(a1[:, 0:8], mod[:, 8:16], 1.0, par[:, PAR["n1"]], ALU.add, ALU.mult).then_inc(sem("a1"), 1)
            dve.wait_ge(sem("a1"), 1)
            for k in range(KT):
                dve.wait_ge(sem("h_norm"), k + 1)
                dve.tensor_scalar(fa[:, k, :], fa[:, k, :], a1[:, k:k + 1], mod[:, k:k + 1], ALU.mult,
                                  ALU.add).then_inc(sem("h_f32"), 1)
                if k >= 1:
                    dve.wait_ge(sem("h_hi"), k)
                    dve.tensor_tensor(h_lo[:, k - 1, :], fa[:, k - 1, :], h_hi[:, k - 1, :].bitcast(F32), ALU.subtract).then_inc(sem("h_done"), 1)
            dve.wait_ge(sem("h_hi"), KT)
            dve.tensor_tensor(h_lo[:, KT - 1, :], fa[:, KT - 1, :], h_hi[:, KT - 1, :].bitcast(F32), ALU.subtract).then_inc(sem("h_done"), 1)
            for t in range(16, 18):
                ada(t, t % 3, 16 * (t // 3 + 1), mod[:, t:t + 1])
            with dve.Fori(0, 5) as i:
                for t in range(6):
                    ada(None, t % 3, i * 32 + (96 + 16 * (t // 3 + 1)), mod6[:, t:t + 1])
                dve.wait_ge(sem("ada_used"), i * 6 + 24)
                dve.tensor_copy(mod[:, bass.ds(i * 6 + 18, 6)], mod6[:]).then_inc(sem("mod_copied"), 1)
                dve.wait_ge(sem("mod_copied"), i + 1)

            def softplus(nth, y, n, out_ap):
                st = sp_t[:, :, 0:n]
                done = sem("softplus_steps")
                dve.scalar_tensor_tensor(st[:, 1, :], y, -1.0, y, ALU.mult, ALU.max).then_inc(sem("softplus_abs"), 1)
                dve.wait_ge(sem("softplus_exp"), nth)
                dve.tensor_scalar(st[:, 3, :], st[:, 2, :], 1.0, None, ALU.add).then_inc(sem("softplus_1p"), 1)
                dve.wait_ge(sem("softplus_1p"), nth)
                dve.tensor_scalar(st[:, 5, :], st[:, 3, :], 1.0, None, ALU.subtract).then_inc(done, 1)
                dve.wait_ge(done, 8 * nth - 7)
                dve.tensor_scalar(st[:, 6, :], st[:, 5, :], 0.0, None, ALU.is_equal).then_inc(done, 1)
                dve.tensor_scalar(st[:, 7, :], st[:, 5, :], 1e-8, None, ALU.max).then_inc(done, 1)
                dve.wait_ge(done, 8 * nth - 5)
                dve.reciprocal(st[:, 5, :], st[:, 7, :]).then_inc(done, 1)
                dve.wait_ge(sem("softplus_ln"), nth)
                dve.wait_ge(done, 8 * nth - 4)
                dve.tensor_tensor(st[:, 5, :], st[:, 5, :], st[:, 4, :], ALU.mult).then_inc(done, 1)
                dve.wait_ge(done, 8 * nth - 3)
                dve.tensor_tensor(st[:, 5, :], st[:, 5, :], st[:, 6, :], ALU.add).then_inc(done, 1)
                dve.wait_ge(done, 8 * nth - 2)
                dve.tensor_tensor(st[:, 5, :], st[:, 5, :], st[:, 2, :], ALU.mult).then_inc(done, 1)
                dve.wait_ge(done, 8 * nth - 1)
                dve.scalar_tensor_tensor(out_ap, y, 0.0, st[:, 5, :], ALU.max, ALU.add).then_inc(done, 1)
                dve.wait_ge(done, 8 * nth)

            dve.tensor_scalar(sp_t[:, 0, 0:2], par[:, PAR["lru_lam"]], -1.0, None, ALU.mult).then_inc(sem("lam_neg"), 1)
            dve.wait_ge(sem("lam_neg"), 1)
            softplus(1, sp_t[:, 0, 0:2], 2, sp_t[:, 6, 0:2])
            dve.tensor_scalar(sl[:, 0:2], sp_t[:, 6, 0:2], -8.0, None, ALU.mult).then_inc(sem("lam_sp"), 1)
            dve.tensor_scalar(sl[:, 2:4], sp_t[:, 6, 0:2], 8.0, None, ALU.mult).then_inc(sem("sl"), 1)

            dve.wait_ge(sem("gb2_read"), 10)
            dve.wait_ge(sem("ada_used"), 48)
            chain = sem("lru_chain")
            n = 0
            for c in range(2):
                x_, u_ = fa[:, c, :], fa[:, 12, :]
                if c == 1:
                    dve.wait_ge(sem("lru_hi"), 1)
                    dve.wait_ge(sem("lru_lo"), 1)
                dve.tensor_scalar(u_, x_, pc("lru_cw", c * 4 + 3), pc("lru_cb", c), ALU.mult, ALU.add).then_inc(chain, 1)
                n += 1
                for t in range(1, 4):
                    dve.wait_ge(chain, n)
                    ins = dve.scalar_tensor_tensor(u_[:, t:], x_[:, 0:S - t], pc("lru_cw", c * 4 + 3 - t), u_[:, t:],
                                                   ALU.mult, ALU.add)
                    if t < 3:
                        ins.then_inc(chain, 1)
                        n += 1
                ins.then_inc(sem("lru_u"), 1)
                dve.wait_ge(sem("lru_gates"), 2 * c + 2)
                dve.wait_ge(sem("lru_u"), c + 1)
                dve.tensor_tensor(fa[:, 14, :], fa[:, 14, :], u_, ALU.mult).then_inc(chain, 1)
                dve.wait_ge(sem("lru_a"), 3 * c + 1)
                dve.tensor_tensor(x_, fa[:, 15, :], fa[:, 15, :], ALU.mult).then_inc(chain, 1)
                n += 2
                dve.wait_ge(sem("lru_a"), 3 * c + 2)
                dve.wait_ge(chain, n)
                dve.scalar_tensor_tensor(fa[:, 13, :], x_, 1.0, fa[:, 13, :], ALU.add, ALU.mult).then_inc(sem("lru_b2"), 1)
                dve.wait_ge(sem("lru_a"), 3 * c + 3)
                dve.tensor_tensor(fa[:, 14, :], fa[:, 14, :], fa[:, 13, :], ALU.mult).then_inc(chain, 1)
                n += 1
                dve.wait_ge(chain, n)
                dve.wait_ge(sem("lru_ri"), c + 1)
                dve.tensor_tensor_scan(u_, fa[:, 15, :], fa[:, 14, :], 0.0, ALU.mult, ALU.add).then_inc(sem("lru_scan"), 1)
                dve.wait_ge(sem("lru_scan"), c + 1)
                dve.wait_ge(sem("lru_gelu"), c + 1)
                dve.tensor_tensor(u_, u_, fa[:, 2 + c, :], ALU.mult).then_inc(sem("lru_o"), 1)
                dve.wait_ge(sem("lru_hi"), c + 1)
                dve.tensor_tensor(ra[:, 2 + c, :], u_, ra[:, c, :].bitcast(F32), ALU.subtract).then_inc(sem("lru_lo"), 1)

            def sb_weights(n):
                b, hd = SB_STEPS[n]
                keys = (b + 1) * P
                beta, keep, prod = fa[:, n % 2, 0:keys], fa[:, 2 + n % 2, 0:keys], fa[:, 12 + n % 2, 0:keys]
                dve.wait_ge(sem("sb_sig"), 2 * n + 2)
                dve.tensor_tensor(beta[:, b * P:], beta[:, b * P:], past, ALU.mult).then_inc(sem("sb_masked"), 1)
                dve.tensor_tensor(keep[:, b * P:], keep[:, b * P:], npast, ALU.max).then_inc(sem("sb_masked"), 1)
                dve.wait_ge(sem("sb_masked"), 2 * n + 2)
                dve.tensor_tensor_scan(prod[:, ::-1], keep[:, ::-1], keep[:, ::-1], 1.0, ALU.mult, ALU.min).then_inc(sem("sb_scan"), 1)
                dve.wait_ge(sem("sb_scan"), n + 1)
                dve.tensor_tensor(beta[:, 0:keys - 1], beta[:, 0:keys - 1], prod[:, 1:keys], ALU.mult).then_inc(sem("sb_wgt"), 1)

            def sb_lo(n):
                b, hd = SB_STEPS[n]
                bank = 1 + 2 * (n // 4 % 2)
                dve.wait_ge(sem("sb_hi"), n // 4 + 1)
                dve.tensor_tensor(ra[:, 6:8, b * P:(b + 1) * P], gb[bank][:, 0:256].rearrange("p (c s) -> p c s", c=2),
                                  ra[:, 4:6, b * P:(b + 1) * P].bitcast(F32), ALU.subtract).then_inc(sem("sb_lo"), 1)

            past, npast = m_("past"), m_("npast")
            for n in range(len(SB_STEPS)):
                sb_weights(n)
                if n % 4 == 1 and n > 4:
                    sb_lo(n - 2)
            sb_lo(len(SB_STEPS) - 1)
            dve.wait_ge(sem("mod_copied"), 5)
            dve.tensor_tensor(mod[:, 16:48], mod[:, 16:48], par[:, PAR["b_ada"].start + 16:PAR["b_ada"].stop],
                              ALU.add).then_inc(sem("mod1"), 1)
            dve.wait_ge(sem("mod1"), 2)
            dve.scalar_tensor_tensor(a1[:, 8:16], mod[:, 32:40], 1.0, par[:, PAR["n2"]], ALU.add, ALU.mult).then_inc(sem("a1"), 1)
            dve.wait_ge(sem("a1"), 2)
            ab = abt[:].rearrange("p (b h) -> p b h", h=8)
            tkb = lambda k: tk[:, k, :].rearrange("p (b h) -> p b h", h=4)
            dve.wait_ge(sem("ab_turned"), 1)
            dve.tensor_copy(abt[:], mb[0][:, 0:64]).then_inc(sem("ab_read"), 1)
            dve.wait_ge(sem("ab_read"), 1)
            dve.tensor_tensor(sp_t[:, 0, :].rearrange("p (b h) -> p b h", h=4), ab[:, :, 0:4],
                              par[:, PAR["dtb"]].rearrange("p (o h) -> p o h", o=1).to_broadcast([P, NB, 4]), ALU.add).then_inc(sem("dt_y"), 1)
            dve.wait_ge(sem("dt_y"), 1)
            softplus(2, sp_t[:, 0, :], 32, sp_t[:, 6, :])
            dve.wait_ge(sem("ea"), 1)
            dve.scalar_tensor_tensor(tkb(0), sp_t[:, 6, :].rearrange("p (b h) -> p b h", h=4), -1.0,
                                     ea[:].rearrange("p (o h) -> p o h", o=1).to_broadcast([P, NB, 4]), ALU.mult,
                                     ALU.mult).then_inc(sem("tk_g"), 1)
            dve.wait_ge(sem("tk_act"), 3)
            dve.wait_ge(sem("functions"), 1)
            dve.scalar_tensor_tensor(tk[:, 4, :], tk[:, 5, :], -1.0, tk[:, 1, :], ALU.mult, ALU.mult).then_inc(sem("values"), 1)
            dve.wait_ge(sem("values"), 1)

            with dve.Fori(0, NB) as i:
                v = i + 1
                base = i * ND
                ch = sem("block_steps")
                st = {"n": 0, "seen": 0}

                def did(ins):
                    ins.then_inc(ch, 1)
                    st["n"] += 1
                    return st["n"]

                def after(k):
                    if k > st["seen"]:
                        dve.wait_ge(ch, base + k)
                        st["seen"] = k

                def gated(job):
                    n, hf = divmod(job, 2)
                    dve.wait_ge(sem(f"gb{2 * hf}_read"), i * 4 + (U_MIX + 1 + n))
                    dve.wait_ge(sem(f"gb{2 * hf + 1}_full"), i * 2 + (n + 1))
                    m_half = mix[:, hf * HALF:(hf + 1) * HALF]
                    if n == 0:
                        if hf == 0:
                            dve.wait_ge(sem("block_stored"), i * 48 + 16)
                        dve.tensor_tensor(m_half, sig, gb[2 * hf + 1], ALU.mult).then_inc(sem("gated"), 1)
                    else:
                        k = did(dve.tensor_tensor(sig, sig, gb[2 * hf + 1], ALU.mult))
                        after(k)
                        dve.tensor_tensor(m_half, m_half, sig, ALU.add).then_inc(sem("gated"), 1)

                dve.wait_ge(sem("pblk_in"), i * 16 + 16)
                pm3 = t2(rw["pm"])
                cur, prev = pblk[:, 0:7, HALO:], pblk[:, 0:7, HALO - 1:HALO - 1 + P]
                k = did(dve.tensor_tensor(pm3, prev, cur, ALU.subtract))
                after(k)
                k = did(dve.tensor_tensor(pm3, pm3, over_t(PAR["rw_mu"].start, 7), ALU.mult))
                after(k)
                dve.tensor_tensor(pm3, pm3, cur, ALU.add).then_inc(done("rw_pm"), 1)
                dve.wait_ge(sem("rw_pm"), at("rw_pm", i))
                r_, k_, v_ = (rw["pm"][:, a_:a_ + 256] for a_ in (0, 256, 512))
                dve.tensor_tensor(t2(rw["kkr"]), t2(k_), over_t(PAR["rw_kk"].start, 2), ALU.mult).then_inc(done("rw_kkr"), 1)
                dve.wait_ge(sem("rw_sw"), at("rw_sw", i, 2))
                for t in range(2):
                    c = slice(t * P, (t + 1) * P)
                    dve.tensor_tensor_scan(rw["gs"][:, c], m_("reset"), rw["sw"][:, c], 0.0, ALU.mult, ALU.add).then_inc(done("rw_gs"), 1)
                dve.wait_ge(sem("rw_gs"), at("rw_gs", i, 2))
                dve.tensor_tensor(rw["gm"], rw["gs"], rw["sw"], ALU.subtract).then_inc(done("rw_gm"), 1)
                dve.wait_ge(sem("rw_sa"), at("rw_sa", i, 2))
                dve.wait_ge(sem("rw_p2"), at("rw_p2", i))
                k = did(dve.scalar_tensor_tensor(t2(rw["t1"]), t2(rw["sa"]), -1.0, over_t(PAR["rw_ka"].start, 2), ALU.add, ALU.mult))
                after(k)
                k2 = did(dve.scalar_tensor_tensor(rw["t1"], rw["t1"], 1.0, k_, ALU.add, ALU.mult))
                after(k2)
                k = did(dve.tensor_tensor(rw["bon"], r_, rw["t1"], ALU.mult))
                after(k)
                dve.tensor_tensor(t2(rw["bon"]), t2(rw["bon"]), over_t(PAR["rw_rk"].start, 2), ALU.mult).then_inc(done("rw_bonp"), 1)
                dve.wait_ge(sem("rw_rn"), at("rw_rn", i))
                kk = did(dve.tensor_tensor(rw["kkr"], rw["kkr"], rw["rn"], ALU.mult))
                dve.wait_ge(sem("rw_ex"), at("rw_ex", i, 3))
                ar = rw["ar"].rearrange("p (t w c) -> p t w c", t=2, w=2)
                dve.tensor_tensor(ar[:, :, 1, :], t2(r_), t2(rw["ex1"]), ALU.mult).then_inc(done("rw_ar"), 1)
                after(kk)
                dve.scalar_tensor_tensor(ar[:, :, 0, :], t2(rw["kkr"]), -1.0, t2(rw["ex0"]), ALU.mult, ALU.mult).then_inc(done("rw_ar"), 1)
                dve.tensor_tensor(rw["km"], rw["t1"], rw["exn"], ALU.mult).then_inc(done("rw_km"), 1)
                k = did(dve.tensor_tensor(rw["bm"], rw["kkr"], rw["sa"], ALU.mult))
                after(k)
                kb = did(dve.tensor_tensor(rw["bm"], rw["bm"], rw["exn"], ALU.mult))
                ends = rw["ex1"].rearrange("p (c s) -> p c s", s=CHUNK)[:, :, CHUNK - 1:CHUNK].to_broadcast([P, 4, CHUNK])
                c4 = lambda ap: ap.rearrange("p (c s) -> p c s", s=CHUNK)
                dve.wait_ge(sem("rw_km"), at("rw_km", i))
                dve.tensor_tensor(c4(rw["kt"]), c4(rw["km"]), ends, ALU.mult).then_inc(done("rw_tl"), 1)
                after(kb)
                dve.tensor_tensor(c4(rw["bt"]), c4(rw["bm"]), ends, ALU.mult).then_inc(done("rw_tl"), 1)
                gated(0)
                dve.wait_ge(sem("rw_p3"), at("rw_p3", i))
                dve.tensor_tensor(rw["bon"], mb[2][:, 256:512], v_, ALU.mult).then_inc(done("rw_bon"), 1)
                both = lambda b0: mbank[:, b0:b0 + 2, :].rearrange("p b (h c) -> p b h c", c=256)
                eo = lambda ap: ap.rearrange("p (t e c) -> p e t c", t=2, e=2)
                eo_mask = lambda name: msk[:, M[name]:M[name] + 1, :].rearrange("p (e t) c -> p e t c", e=1).to_broadcast([P, 2, 2, P])
                dve.wait_ge(sem("rw_p6"), at("rw_p6", i))
                dve.tensor_tensor(eo(rw["akt"]), both(0)[:, :, :, 0:P], eo_mask("strict"), ALU.mult).then_inc(done("rw_akt"), 1)
                dve.tensor_tensor(eo(rw["rkt"]), both(0)[:, :, :, P:256], eo_mask("tri"), ALU.mult).then_inc(done("rw_akt"), 1)
                dve.wait_ge(sem("rw_p7"), at("rw_p7", i))
                dve.tensor_tensor(eo(rw["ltr"]), both(2)[:, :, :, 0:P], eo_mask("nstrict"), ALU.mult).then_inc(done("rw_ltr"), 1)
                dve.tensor_tensor(eo(rw["rbt"]), both(2)[:, :, :, P:256], eo_mask("tri"), ALU.mult).then_inc(done("rw_ltr"), 1)

                dve.wait_ge(sem("rw_tokVA"), at("rw_tokVA", i))
                acc, tmp = t4(gd["acc"]), t4(gd["tmp"])
                cw = par[:, PAR["gdn_cw"]].rearrange("p (t j o) -> p t j o", j=4, o=1)
                tap = lambda j: (pblk[:, 7:13, j:j + P], cw[:, :, j, :].to_broadcast([P, 6, P]))
                k1 = did(dve.tensor_tensor(acc, *tap(0), ALU.mult))
                for j in range(1, 4):
                    k = did(dve.tensor_tensor(tmp, *tap(j), ALU.mult))
                    after(k)
                    ins = dve.tensor_tensor(acc, acc, tmp, ALU.add)
                    if j < 3:
                        k = did(ins)
                        after(k)
                    else:
                        ins.then_inc(done("gd_acc"), 1)
                dve.tensor_copy(tkc[:].rearrange("p (k h) -> p k h", h=4), tk[:, 0:5, bass.ds(i * 4, 4)]).then_inc(done("tkc"), 1)

                def first_blocks(nm, b_, bank, signal):
                    k0 = did(dve.tensor_tensor(t4(b_["TT"]), t4(b_["ltr"]), over4("lv1T"), ALU.mult))
                    dve.wait_ge(sem(signal), at(signal, i))
                    k1 = did(dve.tensor_tensor(t4(b_["T"]), t4(mb[bank]), over4("lv1"), ALU.mult))
                    after(k1)
                    did(dve.tensor_tensor(t4(b_["TT"]), over4("ident"), t4(b_["TT"]), ALU.subtract))
                    dve.wait_ge(ch, base + st["n"])
                    dve.tensor_tensor(t4(b_["T"]), over4("ident"), t4(b_["T"]), ALU.subtract).then_inc(done(f"{nm}_T"), 1)

                gated(1)
                dve.wait_ge(sem("rw_tokBK"), at("rw_tokBK", i))
                dve.wait_ge(sem("rw_ltr"), at("rw_ltr", i, 2))
                first_blocks("rw", rw, 0, "rw_p8")
                dve.wait_ge(sem("gd_rn"), at("gd_rn", i))
                kbq = gd["kbq"].rearrange("p (t w c) -> p t w c", t=2, w=2)
                dve.tensor_tensor(gd["kn"], gd["acc"][:, 256:512], gd["rn"][:, 256:512], ALU.mult).then_inc(done("gd_kn"), 1)
                dve.scalar_tensor_tensor(kbq[:, :, 1, :], t2(gd["acc"][:, 0:256]), HEAD ** -0.5, t2(gd["rn"][:, 0:256]),
                                         ALU.mult, ALU.mult).then_inc(done("gd_kbq"), 1)
                per_head = lambda k, w: tkc[:, 4 * k:4 * k + 4].rearrange("p (h o) -> p h o", o=1).to_broadcast([P, 4, w])
                dve.wait_ge(sem("gd_g2"), at("gd_g2", i))
                k = did(dve.tensor_tensor(t4(gd["dt"]), t4(mb[2]), per_head(2, P), ALU.subtract))
                after(k)
                dve.tensor_tensor(t4(gd["dt"]), t4(gd["dt"]), over4("neg"), ALU.min).then_inc(done("gd_dtm"), 1)
                dve.wait_ge(sem("gd_g3"), at("gd_g3", i))
                dve.wait_ge(sem("gd_kn"), at("gd_kn", i))
                dve.wait_ge(sem("gd_eg"), at("gd_eg", i))
                dve.tensor_tensor(kbq[:, :, 0, :], t2(gd["kn"]), t2(mb[3][:, 256:512]), ALU.mult).then_inc(done("gd_kbq"), 1)
                dve.wait_ge(sem("gd_kbq"), at("gd_kbq", i, 2))
                kqd = did(dve.tensor_tensor(t2(gd["qd"]), kbq[:, :, 1, :], t2(gd["eg"]), ALU.mult))
                dve.wait_ge(sem("gd_g4"), at("gd_g4", i))
                h64 = lambda ap: ap.rearrange("p (h c) -> p h c", c=64)
                dve.tensor_tensor(h64(gd["vb"]), h64(mb[1][:, 256:512]), per_head(1, 64), ALU.mult).then_inc(done("gd_tok"), 1)
                dve.tensor_tensor(h64(gd["kbe"]), h64(mb[1][:, 0:256]), per_head(4, 64), ALU.mult).then_inc(done("gd_tok"), 1)
                dve.tensor_tensor(h64(gd["kd"]), h64(mb[1][:, 0:256]), per_head(3, 64), ALU.mult).then_inc(done("gd_tok"), 1)
                gated(2)
                dve.wait_ge(sem("gd_g5"), at("gd_g5", i))
                dve.wait_ge(sem("gd_dt"), at("gd_dt", i))
                k = did(dve.tensor_tensor(eo(gd["ltr"]), both(2)[:, :, :, 0:P], eo(gd["dt"]), ALU.mult))
                after(k)
                dve.tensor_tensor(t4(gd["ltr"]), t4(gd["ltr"]), over4("strict"), ALU.mult).then_inc(done("gd_ltr"), 1)
                dve.tensor_tensor(eo(gd["qkt"]), both(2)[:, :, :, P:256], eo(gd["dt"]), ALU.mult).then_inc(done("gd_qkt"), 1)
                dve.wait_ge(sem("gd_qkt"), at("gd_qkt", i))
                first_blocks("gd", gd, 1, "gd_g6")

                for lv in range(5):
                    for nm, b_, bank in (("rw", rw, 0), ("gd", gd, 3)):
                        dve.wait_ge(sem(f"{nm}_Y"), at(f"{nm}_Y", i, lv + 1))
                        dve.tensor_tensor(t4(b_["Y"]), t4(mb[bank]), over4(f"lv{2 << lv}"), ALU.mult).then_inc(done(f"{nm}_Ym"), 1)
                    for nm, b_, bank in (("rw", rw, 0), ("gd", gd, 3)):
                        if lv < 4:
                            dve.wait_ge(sem(f"{nm}_Z"), at(f"{nm}_Z", i, 2 * lv + 1))
                            dve.tensor_tensor(b_["T"], b_["T"], mb[1], ALU.subtract).then_inc(done(f"{nm}_T"), 1)
                        dve.wait_ge(sem(f"{nm}_Z"), at(f"{nm}_Z", i, (2 * lv + (2 if lv < 4 else 1))))
                        dve.tensor_tensor(b_["TT"], b_["TT"], mb[2], ALU.subtract).then_inc(done(f"{nm}_T"), 1)
                    if lv == 1:
                        gated(3)
                for par_ in range(2):
                    R = slice(64 * par_, 64 * par_ + 64)
                    for nm, b_, ws in (("rw", rw, 0), ("gd", gd, 256)):
                        if par_ == 0:
                            dve.wait_ge(sem(f"{nm}_uw"), at(f"{nm}_uw", i))
                        dve.wait_ge(sem("gd_ws"), at("gd_ws", i, par_ + 1))
                        dve.tensor_tensor(b_["u"][R, :], b_["uw"][R, 0:256], mb[0][R, ws:ws + 256], ALU.add).then_inc(done(f"{nm}_u"), 1)
                    for nm, b_, st_, sc, dec in (("rw", rw, 0, 1, "ex1"), ("gd", gd, 1, 0, "eg")):
                        dve.wait_ge(sem(f"{nm}_s"), at(f"{nm}_s", i, par_ + 1))
                        for t in range(2):
                            for r in (0, 64):
                                e_ = t * P + 64 * par_ + 63
                                dve.scalar_tensor_tensor(state[r:r + 64, st_, t, r:r + 64], state[r:r + 64, st_, t, r:r + 64],
                                                         b_[dec][r:r + 64, e_:e_ + 1],
                                                         mb[sc][r:r + 64, t * P + r:t * P + r + 64], ALU.mult,
                                                         ALU.add).then_inc(done(f"{nm}_S"), 1)

                dve.wait_ge(sem("rw_m1"), at("rw_m1", i))
                dve.scalar_tensor_tensor(rw["yc"], mb[0][:, 0:256], -1.0 / HEAD, rw["y"], ALU.mult, ALU.add).then_inc(done("rw_yc"), 1)
                dve.wait_ge(sem("gd_rno"), at("gd_rno", i))
                k = did(dve.scalar_tensor_tensor(gd["o"], mb[3][:, 0:256], pc("gdn_ng"), gd["rno"], ALU.mult, ALU.mult))
                after(k)
                dve.tensor_tensor(gd["o"], gd["o"], gd["z"], ALU.mult).then_inc(done("gd_o"), 1)
                dve.wait_ge(sem("rw_rno"), at("rw_rno", i))
                k = did(dve.tensor_tensor(rw["yc"], rw["yc"], rw["u"], ALU.mult))
                after(k)
                for t in range(2):
                    c = slice(t * P, (t + 1) * P)
                    k = did(dve.tensor_scalar(rw["yc"][:, c], rw["yc"][:, c], pc("rw_lng", t), pc("rw_lnb", t), ALU.mult, ALU.add))
                after(k)
                k = did(dve.tensor_tensor(rw["yc"], rw["yc"], rw["bon"], ALU.add))
                after(k)
                dve.tensor_tensor(rw["o"], rw["yc"], rw["gate"], ALU.mult).then_inc(done("rw_o"), 1)
                assert st["n"] == ND, st

            for n in range(2):
                dve.wait_ge(sem(f"o_in{n}"), 16)
                dve.wait_ge(sem("o_hi"), n + 1)
                dve.tensor_tensor(ra[:, 4 * n + 2:4 * n + 4], fa[:, 8 + 2 * n:10 + 2 * n, :],
                                  ra[:, 4 * n:4 * n + 2].bitcast(F32), ALU.subtract).then_inc(sem("o_lo"), 1)
            def mixed_lo(k):
                dve.wait_ge(sem("mixed_hi"), k + 1)
                dve.tensor_tensor(h_lo[:, k, :], fa[:, k, :], h_hi[:, k, :].bitcast(F32), ALU.subtract).then_inc(sem("mixed_lo"), 1)

            for m in range(KT):
                for n in range(2):
                    t, s_ = 2 * m + n, (2 * m + n) % 4
                    dve.wait_ge(sem(f"sig_in{s_}"), 16 * (t // 4 + 1))
                    dve.wait_ge(sem("br_full"), t + 1)
                    dve.tensor_tensor(fa[:, 12 + s_, :], fa[:, 12 + s_, :],
                                      gbank[:, 2 * n:2 * n + 2, :].rearrange("p b s -> p (b s)"), ALU.mult).then_inc(sem("gated"), 1)
                    dve.wait_ge(sem(f"mix_in{m // 4}"), 16)
                    dve.wait_ge(sem("gated"), 4 * NB + t + 1)
                    if n:
                        dve.wait_ge(sem("mixed"), t)
                    dve.tensor_tensor(fa[:, m, :], fa[:, m, :], fa[:, 12 + s_, :], ALU.add).then_inc(sem("mixed"), 1)
                if m:
                    mixed_lo(m - 1)
            mixed_lo(KT - 1)

            def add_squares(m, par_, nth):
                dve.wait_ge(sem("sq"), (1 + nth) * KT + m + 1)
                if m > 1:
                    dve.wait_ge(sem("sq_added"), m - 1 + 7 * nth)
                dve.tensor_tensor(fa[:, ACC, :], fa[:, ACC, :], fa[:, SQ + par_, :], ALU.add).then_inc(sem("sq_added"), 1)

            for m in range(KT):
                dve.wait_ge(sem(f"x_in{m}"), 32)
                for hf in range(2):
                    dve.wait_ge(sem("half_done"), 2 * m + hf + 1)
                    c = slice(hf * HALF, (hf + 1) * HALF)
                    dve.scalar_tensor_tensor(fa[:, m, c], gb[2 * hf + m % 2], mod[:, 16 + m:17 + m], fa[:, m, c],
                                             ALU.mult, ALU.add).then_inc(sem("x1"), 1)
                if m >= 2:
                    add_squares(m - 1, (m - 1) % 2, 0)
            add_squares(KT - 1, (KT - 1) % 2, 0)
            for s_ in range(2):
                dve.tensor_copy(G[s_][:, 0:2], zero[:, 0:2]).then_inc(sem("g_halo"), 1)
            dve.wait_ge(sem("rstd"), 1)

            def h2_lo(k):
                dve.wait_ge(sem("h_hi"), KT + k + 1)
                dve.tensor_tensor(h_lo[:, k, :], fa[:, 12 + k % 4, :], h_hi[:, k, :].bitcast(F32), ALU.subtract).then_inc(sem("h_done"), 1)

            for k in range(KT):
                if k >= 4:
                    dve.wait_ge(sem("h_done"), KT + k - 3)
                dve.tensor_tensor(fa[:, 12 + k % 4, :], fa[:, k, :], fa[:, RSTD, :], ALU.mult).then_inc(sem("h_norm"), 1)
                if k >= 2:
                    h2_lo(k - 2)
            for k in range(KT - 2, KT):
                h2_lo(k)

            def ffn_dve(t, s_, up_half, cw):
                dve.wait_ge(sem("gate_read"), t * 2 + 2)
                dve.tensor_scalar(C[s_], G[s_][:, 2:2 + S], cw[2], None, ALU.mult).then_inc(sem("conv_steps"), 1)
                dve.wait_ge(sem("conv_steps"), t * 2 + 1)
                dve.scalar_tensor_tensor(C[s_], G[s_][:, 1:1 + S], cw[1], C[s_], ALU.mult, ALU.add).then_inc(sem("conv_steps"), 1)
                dve.wait_ge(sem("conv_steps"), t * 2 + 2)
                dve.scalar_tensor_tensor(C[s_], G[s_][:, 0:S], cw[0], C[s_], ALU.mult, ALU.add).then_inc(sem("conv"), 1)
                dve.wait_ge(sem("gelu"), t + 1)
                for hf in range(2):
                    c = slice(hf * HALF, (hf + 1) * HALF)
                    dve.wait_ge(sem("half_done"), up_half + (hf - 1))
                    dve.tensor_tensor(fa[:, 13 + s_, c], C[s_][:, c], gb[2 * hf + 1], ALU.mult).then_inc(sem("up_read"), 1)

            def ffn_lo(t, s_, j):
                dve.wait_ge(sem("act_hi"), t + 1)
                dve.tensor_tensor(ra[:, GT + j, :], fa[:, 13 + s_, :], ra[:, j, :].bitcast(F32), ALU.subtract).then_inc(sem("act_lo"), 1)

            def down_add(m, bank, count):
                dve.wait_ge(sem("half_done"), count)
                dve.scalar_tensor_tensor(fa[:, m, :], mbank[:, bank:bank + 2, :].rearrange("p b s -> p (b s)"),
                                         mod[:, 40 + m:41 + m], fa[:, m, :], ALU.mult, ALU.add).then_inc(sem("down_read"), 1)

            cw0 = PAR["ffn_cw"].start
            taps = lambda t: [par[:, cw0 + 3 * t + j:cw0 + 3 * t + j + 1] for j in range(3)]
            ffn_dve(0, 0, 2 * KT + 4, taps(0))
            ffn_lo(0, 0, 0)
            with dve.Fori(0, NG) as g:
                dve.tensor_copy(cwc[:], par[:, bass.ds(g * (3 * GT) + (cw0 + 3), 3 * GT)]).then_inc(sem("cwc"), 1)
                dve.wait_ge(sem("cwc"), g + 1)
                for q in range(GT):
                    t, u = g * GT + (1 + q), 2 * (2 + 2 * q) + 2 * KT
                    ffn_dve(t, (1 + q) % 2, g * (2 * UG) + (u + 4), [cwc[:, 3 * q + j:3 * q + j + 1] for j in range(3)])
                    if q < GT - 1:
                        ffn_lo(t, (1 + q) % 2, 1 + q)
                for m in range(KT):
                    down_add(m, 2 * (m % 2), g * (2 * UG) + (2 * KT + 4 + 4 * GT + m + 1))
                ffn_lo(g * GT + GT, 0, 0)
            ffn_dve(FT - 1, 1, 2 * (UNITS - U_OUT) - 4, taps(FT - 1))
            ffn_lo(FT - 1, 1, 1)
            for m in range(KT):
                down_add(m, 2 * (m % 2), 2 * (UNITS - U_OUT) - 3 + m // 2)
                if m >= 2:
                    add_squares(m - 1, (m - 1) % 2, 1)
            add_squares(KT - 1, (KT - 1) % 2, 1)
            dve.wait_ge(sem("rstd"), 2)
            for k in range(KT):
                dve.scalar_tensor_tensor(fa[:, k, :], fa[:, k, :], pc("nf", k), fa[:, RSTD, :], ALU.mult,
                                         ALU.mult).then_inc(sem("out_done"), 1)


def host_layout(x):
    f = lambda v: np.ascontiguousarray(v)
    cols = lambda v: v.reshape(-1, P).T

    def tiles(w):
        k, n = w.shape
        return w.reshape(k // P, P, n // P, P).transpose(2, 1, 0, 3).reshape(n // P, P, k)

    t = {}
    t["xT"] = f(x["x"][0].T).reshape(KT, P, S)
    t["c"] = f(x["c"])
    t["w_ada"] = f(x["w_ada"][0].T).reshape(48, P, D)
    w = x["w_in"][0]
    lru, sbw, gdn, rw = w[:, :512], w[:, 512:1280], w[:, 1280:2312], w[:, 2312:]
    ab = np.zeros((D, P), np.float32)
    ab[:, :8] = gdn[:, 1024:]
    t["w_in"] = f(tiles(np.concatenate([lru, sbw, rw, gdn[:, :1024], ab], axis=1)))
    wg, wb = x["w_gate"][0], x["w_branch"][0]
    t["w_mix"] = f(np.concatenate([np.stack([tiles(wg[n]) for n in range(2)]), np.stack([tiles(wb[n]) for n in range(2)])],
                                  axis=3).transpose(1, 0, 2, 3).reshape(2 * KT, P, W_COLS))
    t["w_gate"] = f(np.stack([tiles(wg[n]) for n in (2, 3)], axis=1).reshape(2 * KT, P, KT * P))
    t["w_branch"] = f(np.stack([tiles(wb[n]) for n in (2, 3)], axis=1).reshape(4, 4, P, 2 * P).transpose(0, 2, 1, 3)
                      .reshape(4, P, KT * P))
    gate, up = tiles(x["ffn_w_gate"][0]), tiles(x["ffn_w_up"][0])
    down = tiles(x["ffn_w_down"][0])

    def downs(g, ks):
        w = down[:, :, g * GT * P:(g * GT + ks) * P]
        return list(w.reshape(ks, KT // ks, P, ks * P).transpose(0, 2, 1, 3).reshape(ks, P, KT * P))

    units = list(tiles(x["w_out"][0])) + [gate[0], up[0]]
    for g in range(NG):
        for q in range(GT):
            units += [gate[g * GT + 1 + q], up[g * GT + 1 + q]]
        units += downs(g, GT)
    units += [gate[FT - 1], up[FT - 1]] + downs(NG, FT - NG * GT)
    t["w_tail"] = f(np.stack(units))
    conv = lambda v, n: v[0].reshape(v.shape[1], n, P).transpose(2, 1, 0).reshape(P, -1)
    bcast = lambda v: np.broadcast_to(v.reshape(1, -1), (P, v.size))
    vals = {"n1": cols(x["norm1_g"]), "n2": cols(x["norm2_g"]), "nf": cols(x["final_g"]), "b_ada": cols(x["b_ada"]),
            "lru_cw": conv(x["lru_conv_w"], 2), "lru_cb": cols(x["lru_conv_b"]), "lru_br": cols(x["lru_b_r"]),
            "lru_bi": cols(x["lru_b_i"]), "lru_lam": cols(x["lru_lambda"]), "gdn_cw": conv(x["gdn_conv_w"], 6),
            "rw_mu": cols(x["rw_mu"]), "rw_w0": cols(x["rw_w0"]), "rw_a0": cols(x["rw_a0"]), "rw_kk": cols(x["rw_k_k"]),
            "rw_ka": cols(x["rw_k_a"]), "rw_rk": cols(x["rw_r_k"]), "rw_lng": cols(x["rw_ln_g"]),
            "rw_lnb": cols(x["rw_ln_b"]), "b_gate": cols(x["b_gate"]), "ffn_cw": conv(x["ffn_conv_w"], FT),
            "gdn_ng": np.concatenate([x["gdn_norm_g"][0]] * 2)[:, None], "alog": bcast(x["gdn_a_log"]),
            "dtb": bcast(x["gdn_dt_bias"])}
    t["par"] = f(np.concatenate([vals[n] for n in PAR], axis=1))
    t["masks"] = mask_table()
    t["lru_w"] = f(np.stack([x["lru_w_r"][0], x["lru_w_i"][0]]))
    t["lora"] = f(np.concatenate([x["rw_w_up"][0], x["rw_a_up"][0], x["rw_g_up"][0]], axis=0))
    return t


def kernel(**inputs):
    import concourse.bacc as bacc
    from concourse.bass_utils import run_bass_kernel_spmd

    arrays = host_layout({name: np.asarray(v) for name, v in inputs.items()})
    nc = bacc.Bacc("TRN2", target_bir_lowering=False, num_devices=1, dynamic_dma_scratch_size=1024)
    aps = {name: nc.dram_tensor("in_" + name, v.shape, mybir.dt.from_np(v.dtype), kind="ExternalInput").ap()
           for name, v in arrays.items()}
    out = nc.dram_tensor("out_0", (KT, P, S), F32, kind="ExternalOutput").ap()
    program(nc, aps, out)
    r = run_bass_kernel_spmd(nc, [{"in_" + name: v for name, v in arrays.items()}], core_ids=[0])
    return np.ascontiguousarray(r.results[0]["out_0"].reshape(D, S).T).reshape(1, S, D)
```
